# Optimizing a Trainium2 kernel written in Bass

```python
import jax, jax.numpy as jnp
from jax import lax
import numpy as np

D_MODEL = 1024
BATCH = 1
SEQ = 1024
DEPTH = 1
DEC_BATCH = 8
DEC_SEQ = 1
PAST_LEN = 8192
PAGE_SIZE = 128

CHUNK = 128
GM_HEADS = 8
GM_DIM = D_MODEL // 2 // GM_HEADS
GM_WIDTH = GM_HEADS * GM_DIM
N_HEADS = 8
KV_HEADS = 2
HEAD_DIM = 64
GROUP = N_HEADS // KV_HEADS
WINDOW = 128
ATT_BLOCK = 128
ROPE_THETA = 10000.0
Q_WIDTH = N_HEADS * HEAD_DIM
KV_WIDTH = KV_HEADS * HEAD_DIM
D_FF = 3 * D_MODEL
CONV_W = 3
EPS = 1e-6
IN_WIDTH = 2 * GM_WIDTH + Q_WIDTH + 2 * KV_WIDTH + 2 * D_MODEL

kernel_name = 'hybrid_gmlp_swa_sink_convffn_step'

def rms_norm(x, g):
    xf = x.astype(jnp.float32)
    y = xf * lax.rsqrt(jnp.mean(xf * xf, axis=-1, keepdims=True) + EPS)
    return (y * g.astype(jnp.float32)).astype(x.dtype)

def layer_norm(x, g, b):
    xf = x.astype(jnp.float32)
    mu = jnp.mean(xf, axis=-1, keepdims=True)
    var = jnp.mean(jnp.square(xf - mu), axis=-1, keepdims=True)
    y = (xf - mu) * lax.rsqrt(var + EPS)
    return (y * g.astype(jnp.float32) + b.astype(jnp.float32)).astype(x.dtype)

def rotary(x, pos):
    half = HEAD_DIM // 2
    inv = ROPE_THETA ** (-jnp.arange(half, dtype=jnp.float32) / half)
    ang = pos.astype(jnp.float32)[:, None] * inv[None, :]
    cos = jnp.cos(ang)[None, :, None, :]
    sin = jnp.sin(ang)[None, :, None, :]
    xf = x.astype(jnp.float32)
    x1, x2 = xf[..., :half], xf[..., half:]
    return jnp.concatenate([x1 * cos - x2 * sin, x2 * cos + x1 * sin], axis=-1).astype(x.dtype)

def sink_softmax(s, mask, sink):
    s = jnp.where(mask, s, -jnp.inf)
    sink = sink.astype(jnp.float32)
    m = jnp.maximum(jnp.max(s, axis=-1, keepdims=True), sink)
    p = jnp.exp(s - m)
    return p / (jnp.sum(p, axis=-1, keepdims=True) + jnp.exp(sink - m))

def in_projection(h, w_in, ln_v_g, ln_v_b):
    B, S = h.shape[0], h.shape[1]
    z = h @ w_in
    a = jax.nn.gelu(z[..., :2 * GM_WIDTH])
    u = a[..., :GM_WIDTH]
    vg = layer_norm(a[..., GM_WIDTH:], ln_v_g, ln_v_b).reshape(B, S, GM_HEADS, GM_DIM)
    o = 2 * GM_WIDTH
    q = z[..., o:o + Q_WIDTH].reshape(B, S, N_HEADS, HEAD_DIM)
    o += Q_WIDTH
    k = z[..., o:o + KV_WIDTH].reshape(B, S, KV_HEADS, HEAD_DIM)
    o += KV_WIDTH
    v = z[..., o:o + KV_WIDTH].reshape(B, S, KV_HEADS, HEAD_DIM)
    o += KV_WIDTH
    ga = z[..., o:o + D_MODEL]
    gb = z[..., o + D_MODEL:]
    return u, vg, q, k, v, ga, gb

def spatial_gate(u, vg, w_s, b_s):
    B, S = u.shape[0], u.shape[1]
    T = min(S, CHUNK)
    nc = S // T
    causal = jnp.tril(jnp.ones((T, T), dtype=bool))
    ws = jnp.where(causal[None], w_s[:, :T, :T], 0.0).astype(vg.dtype)
    vc = vg.reshape(B, nc, T, GM_HEADS, GM_DIM)
    mix = jnp.einsum('hts,bcshd->bcthd', ws, vc) + b_s[:, :T].T[:, :, None].astype(vg.dtype)
    return u * mix.reshape(B, S, GM_WIDTH)

def swa_prompt(q, k, v, sinks):
    B, S = q.shape[0], q.shape[1]
    T = ATT_BLOCK
    nb = S // T
    qb = q.reshape(B, nb, T, KV_HEADS, GROUP, HEAD_DIM)
    kb = k.reshape(B, nb, T, KV_HEADS, HEAD_DIM)
    vb = v.reshape(B, nb, T, KV_HEADS, HEAD_DIM)
    kprev = jnp.concatenate([jnp.zeros_like(kb[:, :1]), kb[:, :-1]], axis=1)
    vprev = jnp.concatenate([jnp.zeros_like(vb[:, :1]), vb[:, :-1]], axis=1)
    kk = jnp.concatenate([kprev, kb], axis=2)
    vv = jnp.concatenate([vprev, vb], axis=2)
    s = jnp.einsum('bcqhgd,bckhd->bchgqk', qb, kk).astype(jnp.float32) * (HEAD_DIM ** -0.5)
    i = jnp.arange(T)[:, None]
    j = jnp.arange(2 * T)[None, :]
    diff = i + T - j
    band = (diff >= 0) & (diff <= WINDOW)
    blk = jnp.arange(nb)[:, None, None]
    mask = band[None] & ((blk > 0) | (j >= T)[None])
    sink = sinks.reshape(KV_HEADS, GROUP)[None, None, :, :, None, None]
    p = sink_softmax(s, mask[None, :, None, None], sink)
    o = jnp.einsum('bchgqk,bckhd->bcqhgd', p.astype(vv.dtype), vv)
    return o.reshape(B, S, Q_WIDTH)

def swa_sample(q, k_new, v_new, cache_k, cache_v, sinks):
    Bd, n = q.shape[0], q.shape[1]
    W = cache_k.shape[1]
    kk = jnp.concatenate([cache_k.astype(k_new.dtype), k_new], axis=1)
    vv = jnp.concatenate([cache_v.astype(v_new.dtype), v_new], axis=1)
    qpos = PAST_LEN + jnp.arange(n)
    kpos = jnp.concatenate([PAST_LEN - W + jnp.arange(W), qpos])
    diff = qpos[:, None] - kpos[None, :]
    mask = (diff >= 0) & (diff <= WINDOW)
    qg = q.reshape(Bd, n, KV_HEADS, GROUP, HEAD_DIM)
    s = jnp.einsum('bqhgd,bkhd->bhgqk', qg, kk).astype(jnp.float32) * (HEAD_DIM ** -0.5)
    sink = sinks.reshape(KV_HEADS, GROUP)[None, :, :, None, None]
    p = sink_softmax(s, mask, sink)
    o = jnp.einsum('bhgqk,bkhd->bqhgd', p.astype(vv.dtype), vv).reshape(Bd, n, Q_WIDTH)
    return o, kk[:, -W:], vv[:, -W:]

def conv_ffn(h, prefix, w_up, conv_w, conv_b, w_down):
    S = h.shape[1]
    z = h @ w_up
    zc = jnp.concatenate([prefix.astype(z.dtype), z], axis=1)
    c = conv_b
    for t in range(CONV_W):
        c = c + conv_w[t] * zc[:, t:t + S]
    y = (jax.nn.gelu(c[..., :D_FF]) * c[..., D_FF:]) @ w_down
    return y, zc[:, -(CONV_W - 1):]

def decoder_layer(x, pos, wl, cache_k, cache_v, conv_state):
    (g_mix, w_in, ln_v_g, ln_v_b, w_s, b_s, sinks, w_pa, w_pb, w_o,
     g_ffn, w_up, conv_w, conv_b, w_down) = wl
    B, S = x.shape[0], x.shape[1]
    h = rms_norm(x, g_mix)
    u, vg, q, k, v, ga, gb = in_projection(h, w_in, ln_v_g, ln_v_b)
    q = rotary(q, pos)
    k = rotary(k, pos)
    y_a = spatial_gate(u, vg, w_s, b_s)
    last = S - ((S - 1) // CHUNK) * CHUNK
    gm_rows = vg[:, S - last:]
    if cache_k is None:
        y_b = swa_prompt(q, k, v, sinks)
        keep = min(WINDOW, S)
        new_k, new_v = k[:, S - keep:], v[:, S - keep:]
        prefix = jnp.zeros((B, CONV_W - 1, 2 * D_FF), dtype=x.dtype)
    else:
        y_b, new_k, new_v = swa_sample(q, k, v, cache_k, cache_v, sinks)
        prefix = conv_state
    merged = jax.nn.sigmoid(ga) * (y_a @ w_pa) + jax.nn.sigmoid(gb) * (y_b @ w_pb)
    x = x + merged @ w_o
    y_f, new_conv = conv_ffn(rms_norm(x, g_ffn), prefix, w_up, conv_w, conv_b, w_down)
    x = x + y_f
    return x, new_k, new_v, gm_rows, new_conv

def setup_inputs(seed: int = 0) -> dict:
    key = jax.random.key(seed)
    ks = jax.random.split(key, 24)
    f32 = jnp.float32
    w_buf = min(WINDOW, PAST_LEN)
    nrm = lambda k, shape, s: jax.random.normal(k, shape, f32) * s
    return {
        'x_prompt': nrm(ks[0], (BATCH, SEQ, D_MODEL), 1.0),
        'x_sample': nrm(ks[1], (DEC_BATCH, DEC_SEQ, D_MODEL), 1.0),
        'cache_swa_k': nrm(ks[2], (DEPTH, DEC_BATCH, w_buf, KV_HEADS, HEAD_DIM), 1.0),
        'cache_swa_v': nrm(ks[3], (DEPTH, DEC_BATCH, w_buf, KV_HEADS, HEAD_DIM), 1.0),
        'state_ffn_conv': nrm(ks[4], (DEPTH, DEC_BATCH, CONV_W - 1, 2 * D_FF), 1.0),
        'g_mix': 1.0 + nrm(ks[5], (DEPTH, D_MODEL), 0.05),
        'w_in': nrm(ks[6], (DEPTH, D_MODEL, IN_WIDTH), D_MODEL ** -0.5),
        'ln_v_g': 1.0 + nrm(ks[7], (DEPTH, GM_WIDTH), 0.05),
        'ln_v_b': nrm(ks[8], (DEPTH, GM_WIDTH), 0.02),
        'w_s': nrm(ks[9], (DEPTH, GM_HEADS, CHUNK, CHUNK), CHUNK ** -0.5),
        'b_s': 1.0 + nrm(ks[10], (DEPTH, GM_HEADS, CHUNK), 0.1),
        'sinks': nrm(ks[11], (DEPTH, N_HEADS), 0.5),
        'w_pa': nrm(ks[12], (DEPTH, GM_WIDTH, D_MODEL), GM_WIDTH ** -0.5),
        'w_pb': nrm(ks[13], (DEPTH, Q_WIDTH, D_MODEL), Q_WIDTH ** -0.5),
        'w_o': nrm(ks[14], (DEPTH, D_MODEL, D_MODEL), D_MODEL ** -0.5),
        'g_ffn': 1.0 + nrm(ks[15], (DEPTH, D_MODEL), 0.05),
        'w_up': nrm(ks[16], (DEPTH, D_MODEL, 2 * D_FF), D_MODEL ** -0.5),
        'conv_w': nrm(ks[17], (DEPTH, CONV_W, 2 * D_FF), CONV_W ** -0.5),
        'conv_b': nrm(ks[18], (DEPTH, 2 * D_FF), 0.02),
        'w_down': nrm(ks[19], (DEPTH, D_FF, D_MODEL), D_FF ** -0.5),
        'g_final': 1.0 + nrm(ks[20], (D_MODEL,), 0.05),
    }

def reference(x_prompt, x_sample, cache_swa_k, cache_swa_v, state_ffn_conv,
              g_mix, w_in, ln_v_g, ln_v_b, w_s, b_s, sinks, w_pa, w_pb, w_o,
              g_ffn, w_up, conv_w, conv_b, w_down, g_final):
    xp, xs = x_prompt, x_sample
    pos_p = jnp.arange(xp.shape[1], dtype=jnp.int32)
    pos_s = PAST_LEN + jnp.arange(xs.shape[1], dtype=jnp.int32)
    kp_l, vp_l, ap_l, cp_l = [], [], [], []
    ks_l, vs_l, as_l, cs_l = [], [], [], []
    for l in range(DEPTH):
        wl = (g_mix[l], w_in[l], ln_v_g[l], ln_v_b[l], w_s[l], b_s[l], sinks[l],
              w_pa[l], w_pb[l], w_o[l], g_ffn[l], w_up[l], conv_w[l], conv_b[l], w_down[l])
        xp, kp, vp, ap, cp = decoder_layer(xp, pos_p, wl, None, None, None)
        xs, ksn, vsn, asn, csn = decoder_layer(xs, pos_s, wl, cache_swa_k[l], cache_swa_v[l], state_ffn_conv[l])
        kp_l.append(kp); vp_l.append(vp); ap_l.append(ap); cp_l.append(cp)
        ks_l.append(ksn); vs_l.append(vsn); as_l.append(asn); cs_l.append(csn)
    y_prompt = rms_norm(xp, g_final)
    y_sample = rms_norm(xs, g_final)
    new_swa_k_prompt = jnp.stack(kp_l, axis=0)
    new_swa_v_prompt = jnp.stack(vp_l, axis=0)
    new_gm_v_prompt = jnp.stack(ap_l, axis=0)
    new_conv_prompt = jnp.stack(cp_l, axis=0)
    new_swa_k_sample = jnp.stack(ks_l, axis=0)
    new_swa_v_sample = jnp.stack(vs_l, axis=0)
    new_gm_v_sample = jnp.stack(as_l, axis=0)
    new_conv_sample = jnp.stack(cs_l, axis=0)
    return (y_prompt, y_sample, new_swa_k_prompt, new_swa_v_prompt, new_gm_v_prompt, new_conv_prompt,
            new_swa_k_sample, new_swa_v_sample, new_gm_v_sample, new_conv_sample)


_drawn_inputs = setup_inputs


def setup_inputs(seed=0):
    import zlib

    import numpy as np

    out = dict(_drawn_inputs(seed))
    spreads = {}
    factors = {'ln_v_b': 2.959, 'sinks': 8.0, 'conv_b': 3.944}
    for name, (base, spread) in spreads.items():
        noise = np.random.default_rng([zlib.crc32(name.encode()), seed]).standard_normal(out[name].shape)
        drawn = base * np.exp(spread * noise) if base else spread * noise
        out[name] = __import__('jax').numpy.asarray(drawn.astype(out[name].dtype))
    for name, factor in factors.items():
        out[name] = (out[name] * factor).astype(out[name].dtype)
    return out
```

```python
import math
import numpy as np
import concourse.bass as bass
from concourse import mybir

F32 = mybir.dt.float32
F32R = mybir.dt.float32r
ALU = mybir.AluOpType
ACT = mybir.ActivationFunctionType
AX = mybir.AxisListType

P = 128
D = 1024
SEQ = 1024
NS = 8
T = SEQ + NS
NPC = 3
PC = T // NPC
KT = D // P
GMW = 512
NB = SEQ // P
HEADS, KVH, HD = 8, 2, 64
GRP = HEADS // KVH
SCALE = HD ** -0.5
DFF = 3 * D
EPS = 1e-6
NPAIR = DFF // P
GP = 4
NG = NPAIR // GP
ZW = 2 + SEQ + 3 * NS
CW = ZW - 2
CH = 8 * P
MASKED = -1.0e30

C_GMV = 0
C_K, C_V, C_Q, C_U = 4, 5, 6, 10
C_A = 14
C_B = 30
C_WO = 46
C_UP0 = 54
C_LOOP = 62
C_LAST = 62 + 12 * (NG - 1)


def build(nc, x_t, w_main, w_half, w_ffn, cols, rope, eye, lnv, ws_t, bs_t, ws_first, mask, sink_rows, sink_cols,
          same_sample, k_cache, v_cache, conv_par, conv_state,
          y, kv_prompt, gm_prompt, gm_sample, k_sample, v_sample, v_new, conv_new):
    base = (nc.sbuf_base + 31) // 32 * 32
    arena_bytes = 212800
    nc.alloc_sbuf_tensor("arena", [P, arena_bytes // 4], F32)
    row = T * 4
    R_H = base
    R_QY = R_H + 16 * row
    R_KV = R_QY + 8 * row
    R_M = R_KV + 4 * row
    R_YA = R_M + 8 * row
    R_RSTD = R_YA + 8 * row
    R_RAW = R_RSTD + row
    R_HL = R_RAW + 2 * CH * 4
    R_SMALL = R_HL + 4 * CH * 4
    small_at = [R_SMALL]

    def at(name, shape, dt, offset):
        return nc.alloc_sbuf_tensor_at(name, shape, dt, offset=offset)

    def small(name, shape, dt=F32):
        words = 1
        for s in shape[1:]:
            words *= s
        t = at(name, shape, dt, small_at[0])
        small_at[0] += (words * 4 + 31) // 32 * 32
        assert small_at[0] <= base + arena_bytes, small_at[0] - base - arena_bytes
        return t

    Hh = at("Hh", [P, KT, T], F32R, R_H)
    Hl = at("Hl", [P, KT, T], F32R, R_H + 8 * row)
    WOh = at("WOh", [P, KT, CH], F32R, R_H)
    WOl = at("WOl", [P, KT, CH], F32R, R_H + 8 * CH * 4)
    QYh = at("QYh", [P, GRP, T], F32R, R_QY)
    QYl = at("QYl", [P, GRP, T], F32R, R_QY + 4 * row)
    gv = at("gv", [P, NB + 1, GMW], F32, R_QY)
    lnvb = at("lnvb", [P, 2, GMW], F32, R_QY + 18432)
    bst = at("bst", [P, NB + 1, 6], F32, R_QY + 30784)
    wdiag = at("wdiag", [NS, HEADS, NS], F32, R_QY + 31008)
    sqx = at("sqx", [P, 2, T], F32, R_QY + 22528)
    kh = at("kh", [P, T], F32R, R_KV)
    kl = at("kl", [P, T], F32R, R_KV + row)
    Vh = at("Vh", [P, NB, P], F32R, R_KV + 2 * row)
    Vl = at("Vl", [P, NB, P], F32R, R_KV + 2 * row + NB * P * 4)
    ssq = at("ssq", [P, T], F32, R_KV)
    nv = at("nv", [P, PC], F32, R_KV + row)
    nsq = at("nsq", [P, PC], F32, R_KV + row + PC * 4)
    nt = at("nt", [P, PC], F32, R_KV + row + 2 * PC * 4)
    bsb = at("bsb", [P, 4, P], F32, R_KV)
    wsh = at("wsh", [P, HEADS, P], F32R, R_KV + row)
    wsl = at("wsl", [P, HEADS, P], F32R, R_KV + row + 4096)
    sig = at("sig", [P, T], F32, R_KV + row + 8192)
    x_raw = at("x_raw", [P, KT, T], F32, R_M)
    vnf = at("vnf", [P, NB, GMW], F32, R_M)
    vnl = at("vnl", [P, NB, GMW], F32R, R_M)
    vnh = at("vnh", [P, NB, GMW], F32R, R_M + NB * GMW * 4)
    band = at("band", [P, 2 * P], F32, R_M + NB * GMW * 4)
    Qz = at("Qz", [P, NS, 64], F32, R_M + NB * GMW * 4 + 1024)
    MG = at("MG", [P, KT, T], F32, R_M)
    Wgh = at("Wgh", [P, KT, GMW], F32R, R_YA)
    Wgl = at("Wgl", [P, KT, GMW], F32R, R_YA + KT * GMW * 4)
    YAh = at("YAh", [P, 4, T], F32R, R_YA)
    YAl = at("YAl", [P, 4, T], F32R, R_YA + 4 * row)
    YAt = at("YAt", [P, 4, T], F32, R_YA)
    U = at("U", [P, 4, T], F32, R_YA + 4 * row)
    rope_sb = at("rope_sb", [P, 2, T], F32, R_YA)
    zt = at("zt", [P, 2, T], F32, R_YA + 2 * row)
    sw = at("sw", [P, 2, T], F32, R_YA + 6 * row)
    Pb = at("Pb", [P, 2, GRP, 2 * P], F32, R_YA)
    PTh = at("PTh", [P, 2, GRP * P], F32R, R_YA + 8192)
    PTl = at("PTl", [P, 2, GRP * P], F32R, R_YA + 12288)
    Kc = at("Kc", [P, NS, P + 1], F32, R_YA)
    Vc = at("Vc", [P, NS, P], F32, R_YA + row)
    Ps = at("Ps", [64, P + 1], F32, R_YA + 2 * row)
    Dm = at("Dm", [64, NS], F32, R_YA + 2 * row + 544)
    PTs = at("PTs", [P, 64], F32, R_YA + 2 * row + 576)
    Dt = at("Dt", [NS, 64], F32, R_YA + 2 * row + 832)
    ws_raw = at("ws_raw", [P, HEADS, P], F32, R_YA + 12288)
    X1 = at("X1", [P, KT, T], F32, R_YA)
    rstd = at("rstd", [P, T], F32, R_RSTD)
    raw = at("raw", [P, 2, CH], F32, R_RAW)
    Wh = at("Wh", [P, 2, CH], F32R, R_HL)
    Wl = at("Wl", [P, 2, CH], F32R, R_HL + 2 * CH * 4)
    MSh = [at(f"MSh{i}", [P, KT, PC], F32R, R_QY + i * 16 * PC * 4) for i in range(2)]
    MSl = [at(f"MSl{i}", [P, KT, PC], F32R, R_QY + (i * 16 + 8) * PC * 4) for i in range(2)]
    xr = at("xr", [P, 3, PC], F32, R_KV + row + 8192)
    Gh = at("Gh", [P, GP, T], F32R, R_QY)
    Gl = at("Gl", [P, GP, T], F32R, R_QY + 4 * row)
    R_Z = R_QY + 8 * row
    zb = [at(f"zb{i}", [P, ZW], F32, R_Z + i * 4224) for i in range(2)]
    ca = at("ca", [P, CW], F32, R_Z + 2 * 4224)
    cb = at("cb", [P, CW], F32, R_Z + 3 * 4224)
    R_WD = R_Z + 4 * 4224
    WDh = at("WDh", [P, 2, CH], F32R, R_WD)
    WDl = at("WDl", [P, 2, CH], F32R, R_WD + 2 * CH * 4)
    R_PAR = R_WD + 4 * CH * 4
    cpar = at("cpar", [P, 2 * NPAIR, 4], F32, R_PAR)
    cst = at("cst", [P, 2 * NPAIR, NS, 2], F32, R_PAR + 768)
    cnew = at("cnew", [P, 2 * NPAIR, 2 + 2 * NS], F32, R_PAR + 768 + 3072)
    sqe = at("sqe", [P, 2, PC], F32, R_PAR + 768 + 3072 + 3456)
    assert R_PAR + 768 + 3072 + 3456 + 2 * PC * 4 <= R_YA
    R_N2 = R_Z
    nv2 = at("nv2", [P, PC], F32, R_N2)
    nsq2 = at("nsq2", [P, PC], F32, R_N2 + PC * 4)
    nt2 = at("nt2", [P, PC], F32, R_N2 + 2 * PC * 4)
    nvm = at("nvm", [P, PC], F32, R_QY + 16 * PC * 4)
    nsm = at("nsm", [P, PC], F32, R_QY + 17 * PC * 4)
    ntm = at("ntm", [P, PC], F32, R_QY + 18 * PC * 4)
    colsb = small("colsb", [P, 3, KT])
    ident = small("ident", [P, P])
    ones = small("ones", [P, P])
    vS = small("vS", [NS, P])
    mixS = small("mixS", [P, 4, NS])
    rtok = small("rtok", [P, NB + 1])
    mv = small("mv", [P, NB + 1, 2])
    lnr = small("lnr", [P, 3, NB + 1])
    kS = small("kS", [P, NS])
    snk = small("snk", [P, 2, HEADS])
    snS = small("snS", [64, 2])
    mx = small("mx", [P, 2, GRP])
    nm = small("nm", [P, 2, GRP])
    sm = small("sm", [P, 2, GRP])
    es = small("es", [P, 2, GRP])
    ri = small("ri", [P, 2, GRP])
    st = small("st", [64, 6])
    bmask = small("bmask", [64, NS])

    PS = nc.alloc_psum_tensor("PS", [P, 8, 512], F32)
    MGv = MG[:, :, :].rearrange("p k (c t) -> p (k c) t", c=NPC)
    X1v = X1[:, :, :].rearrange("p k (c t) -> p (k c) t", c=NPC)
    rstd3 = rstd[:, :].rearrange("p (c t) -> p c t", c=NPC)

    def thirds(ap):
        return ap.rearrange("p (c t) -> p c t", c=NPC)

    def pcs(p):
        return slice(p * PC, (p + 1) * PC)

    def blk(b):
        return slice(b * P, (b + 1) * P)

    def sem(name):
        return nc.alloc_semaphore(name)

    raw_full = [sem("raw_full0"), sem("raw_full1")]
    w_hi, w_lo, w_used = sem("w_hi"), sem("w_lo"), sem("w_used")
    x_in = [sem(f"x_in{k}") for k in range(KT)]
    cols_in, small_in, rope_in, band_in = sem("cols_in"), sem("small_in"), sem("rope_in"), sem("band_in")
    kc_in, vc_in, ws_in, bs_in, par_in = sem("kc_in"), sem("vc_in"), sem("ws_in"), sem("bs_in"), sem("par_in")
    xr_in = [sem(f"xr_in{k}") for k in range(3)]
    k_out, v_out, gm_out, s_out, y_out = sem("k_out"), sem("v_out"), sem("gm_out"), sem("s_out"), sem("y_out")
    ones_set, h_hi, h_lo, sq_done, ss_done = sem("ones_set"), sem("h_hi"), sem("h_lo"), sem("sq_done"), sem("ss_done")
    stat_done, v_done, root_done, rstd_done = sem("stat_done"), sem("v_done"), sem("root_done"), sem("rstd_done")
    tok_done, rt_done, rtok_done, gv_done = sem("tok_done"), sem("rt_done"), sem("rtok_done"), sem("gv_done")
    lnv_done, lns_done, ln_done, mixp_done, mix_done = (sem("lnv_done"), sem("lns_done"), sem("ln_done"),
                                                        sem("mixp_done"), sem("mix_done"))
    z_ev, swapped, sw_sin, rot_done, rot_hi, rot_lo = (sem("z_ev"), sem("swapped"), sem("sw_sin"), sem("rot_done"),
                                                       sem("rot_hi"), sem("rot_lo"))
    vt_done, vt_hi, vt_lo, vs_done, qz_zero = sem("vt_done"), sem("vt_hi"), sem("vt_lo"), sem("vs_done"), sem("qz_zero")
    s_done, masked, nm_done, esin_done, exp_done, es_done, ri_done, pn_done = (
        sem("s_done"), sem("masked"), sem("nm_done"), sem("esin_done"), sem("exp_done"), sem("es_done"),
        sem("ri_done"), sem("pn_done"))
    pt_done, pt_hi, pt_lo, pv_done, o_hi, o_ev, u_done, u_ev = (
        sem("pt_done"), sem("pt_hi"), sem("pt_lo"), sem("pv_done"), sem("o_hi"), sem("o_ev"), sem("u_done"), sem("u_ev"))
    kn_done, ss_sc, sn_done, sx_done, sp_done, spt_done, sptc_done, spv_done, so_hi, so_lo = (
        sem("kn_done"), sem("ss_sc"), sem("sn_done"), sem("sx_done"), sem("sp_done"), sem("spt_done"),
        sem("sptc_done"), sem("spv_done"), sem("so_hi"), sem("so_lo"))
    tri_done, ws_hi, ws_lo, vn_hi, vn_lo, ug_done = (sem("tri_done"), sem("ws_hi"), sem("ws_lo"), sem("vn_hi"),
                                                     sem("vn_lo"), sem("ug_done"))
    sp_mm, sp_ev, ya_done, ya_hi, ya_lo = sem("sp_mm"), sem("sp_ev"), sem("ya_done"), sem("ya_hi"), sem("ya_lo")
    g_ev, th_done, p_ev, mg_hi, mg_lo, wo_done, x1_ev = (sem("g_ev"), sem("th_done"), sem("p_ev"), sem("mg_hi"),
                                                         sem("mg_lo"), sem("wo_done"), sem("x1_ev"))
    f_ev, z_rdy, c0_done, conv_done, cnew_done, gelu_done, g_done, g_hi, g_lo, dn_half = (
        sem("f_ev"), sem("z_rdy"), sem("c0_done"), sem("conv_done"), sem("cnew_done"), sem("gelu_done"),
        sem("g_done"), sem("g_hi"), sem("g_lo"), sem("dn_half"))
    last_mm, y_ev, y_done = sem("last_mm"), sem("y_ev"), sem("y_done")
    dve_step, pool_step = sem("dve_step"), sem("pool_step")

    class Link:

        def __init__(self, eng, s):
            self.eng, self.s, self.n, self.off = eng, s, 0, 0

        def __call__(self, ins):
            self.n += 1
            ins.then_inc(self.s, 1)
            self.eng.wait_ge(self.s, self.off + self.n)

    def mm3(out, ah, al, bh, bl, first, last):
        nc.tensor.matmul(out, ah, bh, start=first, stop=False)
        nc.tensor.matmul(out, ah, bl, start=False, stop=False)
        return nc.tensor.matmul(out, al, bh, start=False, stop=last)

    F = lambda ap: ap.bitcast(F32)

    def load(sp, half, j, src, n=CH, wait=True):
        if wait:
            sp.wait_ge(w_lo, 2 * half + j - 1)
        sp.dma_start(raw[:, j, 0:n], src).then_inc(raw_full[j], 16)

    def split_hi(act, half, j, dst=None, n=CH, used=None):
        act.wait_ge(raw_full[j], 16 * half + 16)
        if used is None:
            used = 2 * half + j - 1
        if used is not False:
            act.wait_ge(w_used, used)
        nc.scalar.activation(Wh[:, j, 0:n] if dst is None else dst, raw[:, j, 0:n], ACT.Copy).then_inc(w_hi, 1)

    def split_lo(pool, half, j, dst=None, n=CH):
        h, l = (Wh[:, j, 0:n], Wl[:, j, 0:n]) if dst is None else dst
        pool.wait_ge(w_hi, 2 * half + j + 1)
        nc.gpsimd.tensor_tensor(l, raw[:, j, 0:n], F(h), ALU.subtract).then_inc(w_lo, 1)

    def gmv_dst(c):
        return (Wgh[:, 2 * c:2 * c + 2, :].rearrange("p k n -> p (k n)"),
                Wgl[:, 2 * c:2 * c + 2, :].rearrange("p k n -> p (k n)"))

    def rotating(n):
        return n != 1

    UNITS = 2 * NB
    FILL = {f + f // 3: f for f in range(12)}

    LAST_ORDER = [list(range(KT)), list(range(KT)), [1, 2, 3, 4, 5, 6, 7, 0]]
    LAST_ROOT = {(2, 0): 0, (2, 4): 1, (2, 7): 2}

    block_cm = nc.Block()
    block = block_cm.__enter__()

    @block.sync
    def _(sp):
        def x_load(k):
            sp.dma_start(x_raw[:, k, :], x_t[:, k, :]).then_inc(x_in[k], 16)

        x_load(0)
        load(sp, 0, 0, w_main[0], wait=False)
        x_load(1)
        load(sp, 0, 1, w_main[1], wait=False)
        for k in range(2, KT):
            x_load(k)
        for c in (2, 3, 4, 5):
            load(sp, c // 2, c % 2, w_main[c])
        sp.wait_ge(w_used, 4)
        sp.dma_start(rope_sb[:, :, :], rope).then_inc(rope_in, 16)
        load(sp, 3, 0, w_main[6])
        sp.wait_ge(gv_done, NB + 1)
        sp.dma_start(band[:, :], mask).then_inc(band_in, 16)
        load(sp, 3, 1, w_main[7])
        sp.wait_ge(ln_done, NB + 1)
        sp.dma_start(gm_prompt, vnf[:, NB - 1, :]).then_inc(gm_out, 16)
        sp.dma_start(gm_sample, gv[0:NS, NB, :]).then_inc(gm_out, 16)
        sp.wait_ge(rot_done, 1)
        sp.dma_start(kv_prompt[0], zt[:, 0, SEQ - P:SEQ]).then_inc(k_out, 16)
        sp.wait_ge(z_ev, 2)
        sp.dma_start(kv_prompt[1], zt[:, 1, SEQ - P:SEQ]).then_inc(v_out, 16)
        for c in range(8, 15):
            load(sp, c // 2, c % 2, w_main[c])
        sp.wait_ge(vs_done, 1)
        sp.dma_start(v_new, vS[:, :]).then_inc(s_out, 16)
        load(sp, 7, 1, w_half[0], n=CH // 2)
        sp.wait_ge(pv_done, UNITS)
        sp.dma_start(Kc[:, :, 0:P], k_cache).then_inc(kc_in, 16)
        sp.dma_start(Vc[:, :, :], v_cache).then_inc(vc_in, 16)
        sp.dma_start(ws_raw[:, :, :], ws_t).then_inc(ws_in, 16)
        sp.dma_start(bsb[:, :, :], bs_t).then_inc(bs_in, 16)
        load(sp, 8, 0, w_main[15])
        sp.wait_ge(kn_done, 1)
        sp.dma_start(k_sample, Kc[:, :, 1:P + 1]).then_inc(s_out, 16)
        sp.wait_ge(vc_in, 16)
        sp.dma_start(v_sample, Vc[1:P, :, :]).then_inc(s_out, 16)
        load(sp, 8, 1, w_half[1], n=CH // 2)
        with sp.Fori(2, 16) as q:
            load(sp, q + 7, 0, w_main[q + 14])
            load(sp, q + 7, 1, w_half[q], n=CH // 2)
        for m in range(2):
            load(sp, 23 + m // 2, m % 2, w_main[30 + m])
        sp.wait_ge(p_ev, 16)
        for w in range(NPC * KT):
            if w >= 3:
                sp.wait_ge(x1_ev, w - 2)
            sp.dma_start(xr[:, w % 3, :], x_t[:, w % KT, pcs(w // KT)]).then_inc(xr_in[w % 3], 16)
            if 2 <= w + 2 < KT:
                load(sp, 23 + (w + 2) // 2, w % 2, w_main[32 + w])
            if w == KT - 2:
                load(sp, 27, 0, w_ffn[0])
            if w == KT - 1:
                load(sp, 27, 1, w_ffn[1])
        sp.wait_ge(ss_done, 7 * (NPC + 1))
        for dst, src in ((cpar, conv_par), (cst, conv_state)):
            sp.dma_start(dst.ap(), src).then_inc(par_in, 16)
        for c in range(2, 8):
            load(sp, 27 + c // 2, c % 2, w_ffn[c])
        with sp.Fori(0, NG - 1) as g:
            for c in range(12):
                load(sp, 31 + 6 * g + c // 2, c % 2, w_ffn[8 + 12 * g + c])
        for c in range(4):
            load(sp, C_LAST // 2 + c // 2, c % 2, w_ffn[C_LAST - C_UP0 + c])
        sp.wait_ge(cnew_done, 2 * NPAIR)
        sp.dma_start(conv_new, cnew[:, :, :]).then_inc(y_out, 16)
        for p in range(NPC):
            for h in range(2):
                sp.wait_ge(y_done, KT * p + 4 * (h + 1))
                sp.dma_start(y[:, 4 * h:4 * h + 4, pcs(p)], X1[:, 4 * h:4 * h + 4, pcs(p)]).then_inc(y_out, 16)
        sp.wait_ge(gm_out, 32)
        sp.wait_ge(k_out, 16)
        sp.wait_ge(v_out, 16)
        sp.wait_ge(s_out, 48)
        sp.wait_ge(y_out, 16 * (1 + 2 * NPC))

    @block.scalar
    def _(act):
        A = nc.scalar.activation
        act.dma_start(colsb[:, :, :], cols).then_inc(cols_in, 16)
        for dst, src in ((ident, eye), (lnvb, lnv), (wdiag, ws_first), (snk, sink_rows), (snS, sink_cols),
                         (bmask, same_sample)):
            act.dma_start(dst.ap(), src).then_inc(small_in, 16)
        act.wait_ge(cols_in, 16)
        for k in range(KT):
            if k in (0, 1, 3, 5):
                c = {0: 0, 1: 1, 3: 2, 5: 3}[k]
                split_hi(act, c // 2, c % 2, gmv_dst(c)[0], used=False)
            act.wait_ge(x_in[k], 16)
            A(Hh[:, k, :], x_raw[:, k, :], ACT.Copy, scale=colsb[:, 0, k:k + 1]).then_inc(h_hi, 1)
            if k >= 3:
                act.wait_ge(ss_done, k - 2)
            A(ssq[:, :] if k == 0 else sqx[:, k % 2, :], x_raw[:, k, :], ACT.Square).then_inc(sq_done, 1)
        for c in (4, 5):
            split_hi(act, c // 2, c % 2, used=False)
        for p in range(NPC):
            act.wait_ge(v_done, p + 1)
            A(nsq[:, :], nv[:, :], ACT.Sqrt).then_inc(root_done, 1)
        for t in range(NB + 1):
            n, bank = (P, (0, 1, 2, 3, 4, 5, 7, 6)[t]) if t < NB else (NS, 0)
            if t == 0:
                act.wait_ge(rtok_done, 2)
            if t < NB:
                act.wait_ge(tok_done, t + 1)
            else:
                act.wait_ge(w_used, 4)
            A(gv[0:n, t, :], PS[0:n, bank, :], ACT.Gelu_apprx_tanh, scale=rtok[0:n, t:t + 1]).then_inc(gv_done, 1)
        act.wait_ge(lnv_done, 1)
        A(lnr[:, 1, :], lnr[:, 0, :], ACT.Sqrt).then_inc(lns_done, 1)
        r = 0
        for n in range(6):
            if 6 + n < 10:
                split_hi(act, 3 + n // 2, n % 2)
            if rotating(n):
                act.wait_ge(z_ev, n + 1)
                if r >= 2:
                    act.wait_ge(rot_done, r - 1)
                for i in range(4):
                    last = A(sw[32 * i:32 * i + 32, r % 2, :], zt[32 * (i ^ 1):32 * (i ^ 1) + 32, n % 2, :], ACT.Copy)
                last.then_inc(swapped, 1)
                r += 1
                if n == 2:
                    for i in range(2):
                        act.wait_ge(vt_done, i + 1)
                        A(Vh[:, 4 * i:4 * i + 4, :].rearrange("p b c -> p (b c)"), PS[:, 6 + i, :],
                          ACT.Copy).then_inc(vt_hi, 1)
                    act.wait_ge(mix_done, 2)
                    act.wait_ge(gm_out, 32)
                act.wait_ge(rot_done, r)
                A(kh[:, :] if n == 0 else QYh[:, n - 2, :], zt[:, n % 2, :], ACT.Copy).then_inc(rot_hi, 1)
        for c in (10, 11):
            split_hi(act, c // 2, c % 2)
        for i in range(UNITS + 2):
            if i in (3, 7):
                c = 12 + (i - 3) // 4
                split_hi(act, c // 2, c % 2)
            if i == 11:
                split_hi(act, 7, 0)
            if i == 15:
                split_hi(act, 7, 1, n=CH // 2)
            if 2 <= i:
                u = i - 2
                act.wait_ge(pt_done, u + 1)
                if u >= 1:
                    act.wait_ge(pv_done, u)
                for kt in ((1,) if u < 2 else (0, 1)):
                    last = A(PTh[:, kt, :], PS[:, 4 + kt, :], ACT.Copy)
                last.then_inc(pt_hi, 1)
            if i < UNITS:
                lo = P if i < 2 else 0
                act.wait_ge(nm_done, i + 1)
                for h in range(GRP):
                    last = A(Pb[:, i % 2, h, lo:], Pb[:, i % 2, h, lo:], ACT.Exp, scale=SCALE,
                             bias=nm[:, i % 2, h:h + 1], accum_out=sm[:, i % 2, h:h + 1])
                last.then_inc(exp_done, 1)
                act.wait_ge(esin_done, i + 1)
                A(es[:, i % 2, :], es[:, i % 2, :], ACT.Exp).then_inc(es_done, 1)
            if 2 <= i:
                u, b, g = i - 2, (i - 2) // 2, (i - 2) % 2
                act.wait_ge(pv_done, u + 1)
                A(QYh[64 * g:64 * g + 64, :, blk(b)],
                  PS[64 * g:64 * g + 64, 6, :].rearrange("p (r t) -> p r t", r=GRP), ACT.Copy).then_inc(o_hi, 1)
        act.wait_ge(sn_done, 1)
        A(Ps[:, :], PS[0:64, 3, 0:P + 1], ACT.Exp, scale=SCALE, bias=st[:, 1:2], accum_out=st[:, 3:4])
        A(st[:, 4:5], st[:, 2:3], ACT.Exp).then_inc(sx_done, 1)
        for b in range(NB):
            A(vnh[:, b, :], vnf[:, b, :], ACT.Copy).then_inc(vn_hi, 1)
        act.wait_ge(tri_done, 1)
        A(wsh[:, :, :], ws_raw[:, :, :], ACT.Copy).then_inc(ws_hi, 1)
        act.wait_ge(spt_done, 1)
        A(PTs[:, :], PS[:, 4, 0:64], ACT.Copy)
        A(Dt[:, :], PS[0:NS, 4, 64:128], ACT.Copy).then_inc(sptc_done, 1)
        act.wait_ge(spv_done, 1)
        for g in range(KVH):
            last = A(QYh[64 * g:64 * g + 64, :, SEQ:T],
                     PS[64 * g:64 * g + 64, 6, 0:64].rearrange("p (b h) -> p h b", h=HEADS)[:, GRP * g:GRP * g + GRP, :],
                     ACT.Copy)
        last.then_inc(so_hi, 1)
        for t in range(4):
            act.wait_ge(u_ev, 3 * t + 3)
            A(U[:, t, :], U[:, t, :], ACT.Gelu_apprx_tanh).then_inc(ug_done, 1)
        act.wait_ge(g_ev, 1)
        A(sig[:, :], sig[:, :], ACT.Tanh, scale=0.5).then_inc(th_done, 1)
        split_hi(act, 8, 0)
        for t in range(4):
            act.wait_ge(ya_done, t + 1)
            A(YAh[:, t, :], U[:, t, :], ACT.Copy).then_inc(ya_hi, 1)
        split_hi(act, 8, 1, n=CH // 2)

        def gate(q):
            act.wait_ge(g_ev, q + 1)
            A(sig[:, :], sig[:, :], ACT.Tanh, scale=0.5).then_inc(th_done, 1)

        with act.Fori(1, 15) as q:
            split_hi(act, q + 8, 0)
            gate(q)
            split_hi(act, q + 8, 1, n=CH // 2)
        def merged_hi(p):
            if p == 0:
                act.wait_ge(w_used, 46)
            if p == 2:
                act.wait_ge(wo_done, KT)
            for h in range(2):
                if p == 0 and h == 1:
                    act.wait_ge(p_ev, 16)
                elif p == 0:
                    act.wait_ge(p_ev, 15)
                A(MSh[p % 2][:, 4 * h:4 * h + 4, :], MG[:, 4 * h:4 * h + 4, pcs(p)], ACT.Copy, scale=0.5)\
                    .then_inc(mg_hi, 1)

        split_hi(act, 23, 0, WOh[:, 0, :], used=45)
        gate(15)
        split_hi(act, 23, 1, WOh[:, 1, :], used=45)
        merged_hi(0)
        for w in range(NPC * KT):
            m, p = w % KT, w // KT
            if w + 2 < KT:
                split_hi(act, 24 + w // 2, w % 2, WOh[:, w + 2, :], used=45)
            if w == 4:
                merged_hi(1)
            if w == 9:
                merged_hi(2)
            if w in (10, 12):
                split_hi(act, 27, (w - 10) // 2, used=46)
            act.wait_ge(x1_ev, w + 1)
            A(rstd[:, pcs(p)] if m == 0 else MG[:, m, pcs(p)], X1[:, m, pcs(p)], ACT.Square).then_inc(sq_done, 1)
        act.wait_ge(w_used, 54)
        for k in range(KT):
            A(Hh[:, k, :], X1[:, k, :], ACT.Copy, scale=colsb[:, 1, k:k + 1]).then_inc(h_hi, 1)
        for p in range(NPC):
            act.wait_ge(v_done, NPC + p + 1)
            A(nsm[:, :], nvm[:, :], ACT.Sqrt).then_inc(root_done, 1)
        act.wait_ge(par_in, 32)

        def after_a(pair):
            act.wait_ge(z_rdy, 2 * pair + 1)
            act.wait_ge(g_done, pair)
            A(ca[:, :], zb[0][:, 2:ZW], ACT.Identity, scale=cpar[:, bass.ds(2 * pair, 1), 2],
              bias=cpar[:, bass.ds(2 * pair, 1), 3]).then_inc(c0_done, 1)

        def after_b(pair, gated=True):
            act.wait_ge(conv_done, 2 * pair + 1)
            A(ca[:, :], ca[:, :], ACT.Gelu_apprx_tanh).then_inc(gelu_done, 1)
            act.wait_ge(z_rdy, 2 * pair + 2)
            act.wait_ge(g_lo, pair)
            A(cb[:, :], zb[1][:, 2:ZW], ACT.Identity, scale=cpar[:, bass.ds(2 * pair + 1, 1), 2],
              bias=cpar[:, bass.ds(2 * pair + 1, 1), 3]).then_inc(c0_done, 1)
            if gated:
                gate_hi(pair, None)

        def gate_hi(pair, slot):
            slot = gate_slot[0] if slot is None else slot
            act.wait_ge(g_done, pair + 1)
            A(Gh[:, slot, 0:SEQ], cb[:, 0:SEQ], ACT.Copy)
            A(Gh[:, slot, SEQ:T], cb[:, SEQ + 2:CW:3], ACT.Copy).then_inc(g_hi, 1)

        gate_slot = [0]
        for j in range(8):
            split_hi(act, 28 + j // 2, j % 2)
            gate_slot[0] = j // 2
            (after_b if j % 2 else after_a)(j // 2)
        with act.Fori(0, NG - 1) as g:
            for j in range(12):
                split_hi(act, 32 + 6 * g + j // 2, j % 2)
                if j == 0:
                    after_a(4 * g + 4)
                elif j == 1:
                    after_b(4 * g + 4, gated=False)
                elif j == 5:
                    act.wait_ge(w_used, C_LOOP + 12 * g + 6)
                    gate_hi(4 * g + 4, 0)
                elif j >= 6:
                    gate_slot[0] = (j - 4) // 2
                    (after_b if j % 2 else after_a)(4 * g + 4 + (j - 4) // 2)
        for c in (2, 3):
            split_hi(act, C_LAST // 2 + 1, c - 2, WDh[:, c - 2, :], used=False)
        for w in range(NPC * KT):
            p, i = w // KT, w % KT
            m = LAST_ORDER[p][i]
            act.wait_ge(y_ev, w + 1)
            if i >= 1 and w >= 3:
                act.wait_ge(ss_done, 7 * (NPC + 1 + p) + max(i - 2, 0))
            A(rstd[:, pcs(p)] if i == 0 else sqe[:, i % 2, :], X1[:, m, pcs(p)], ACT.Square).then_inc(sq_done, 1)
            if (p, i) in LAST_ROOT:
                act.wait_ge(v_done, 2 * NPC + LAST_ROOT[p, i] + 1)
                A(nsq2[:, :], nv2[:, :], ACT.Sqrt).then_inc(root_done, 1)

    @block.gpsimd
    def _(pool):
        TT = nc.gpsimd.tensor_tensor

        def add_squares(p, i, own, sq, buf):
            pool.wait_ge(sq_done, sq)
            if i > 1:
                pool.wait_ge(ss_done, own)
            TT(rstd[:, pcs(p)], rstd[:, pcs(p)], buf, ALU.add).then_inc(ss_done, 1)

        for k in range(KT):
            if k in (0, 1, 3, 5):
                c = {0: 0, 1: 1, 3: 2, 5: 3}[k]
                split_lo(pool, c // 2, c % 2, gmv_dst(c))
            if k:
                pool.wait_ge(sq_done, k + 1)
                if k > 1:
                    pool.wait_ge(ss_done, k - 1)
                TT(ssq[:, :], ssq[:, :], sqx[:, k % 2, :], ALU.add).then_inc(ss_done, 1)
        for c in (4, 5):
            split_lo(pool, c // 2, c % 2)
        pool.wait_ge(gv_done, NB + 1)
        nc.gpsimd.memset(Qz[:, :, :], 0.0).then_inc(qz_zero, 1)
        r = 0
        for n in range(6):
            if 6 + n < 10:
                split_lo(pool, 3 + n // 2, n % 2)
            if rotating(n):
                pool.wait_ge(swapped, r + 1)
                if r == 0:
                    pool.wait_ge(rope_in, 16)
                TT(sw[:, r % 2, :], sw[:, r % 2, :], rope_sb[:, 1, :], ALU.mult).then_inc(sw_sin, 1)
                r += 1
        for c in (10, 11):
            split_lo(pool, c // 2, c % 2)
        for i in range(UNITS):
            if i in (3, 7):
                split_lo(pool, (12 + (i - 3) // 4) // 2, (12 + (i - 3) // 4) % 2)
            if i == 11:
                split_lo(pool, 7, 0)
            if i == 15:
                split_lo(pool, 7, 1, n=CH // 2)
            lo = P if i < 2 else 0
            pool.wait_ge(ri_done, i + 1)
            for h in range(GRP):
                last = nc.gpsimd.tensor_scalar(Pb[:, i % 2, h, lo:], Pb[:, i % 2, h, lo:], ri[:, i % 2, h:h + 1],
                                               None, ALU.mult)
            last.then_inc(pn_done, 1)
        pool.wait_ge(ws_in, 16)
        nc.gpsimd.affine_select(out=ws_raw[:, :, :], in_=ws_raw[:, :, :], compare_op=ALU.is_ge, fill=0.0, base=0,
                                pattern=[[0, HEADS], [1, P]], channel_multiplier=-1).then_inc(tri_done, 1)
        pool.wait_ge(ws_hi, 1)
        TT(wsl[:, :, :], ws_raw[:, :, :], F(wsh[:, :, :]), ALU.subtract).then_inc(ws_lo, 1)
        split_lo(pool, 8, 0)
        split_lo(pool, 8, 1, n=CH // 2)
        with pool.Fori(1, 15) as q:
            split_lo(pool, q + 8, 0)
            split_lo(pool, q + 8, 1, n=CH // 2)
        for m in range(2):
            split_lo(pool, 23, m, (WOh[:, m, :], WOl[:, m, :]))
        for w in range(NPC * KT):
            m, p = w % KT, w // KT
            if w + 2 < KT:
                split_lo(pool, 24 + w // 2, w % 2, (WOh[:, w + 2, :], WOl[:, w + 2, :]))
            if w in (10, 12):
                split_lo(pool, 27, (w - 10) // 2)
            if m:
                add_squares(p, m, 7 * (p + 1) + m - 1, KT + w + 1, MG[:, m, pcs(p)])

        def keep_conv(tile, z, count):
            zs = z[:, SEQ + 2:ZW].rearrange("p (b c) -> p b c", c=3)
            pool.wait_ge(z_rdy, count)
            nc.gpsimd.tensor_copy(cnew[:, bass.ds(tile, 1), 0:2], z[:, SEQ:SEQ + 2].rearrange("p (a c) -> p a c", a=1))
            nc.gpsimd.tensor_copy(cnew[:, bass.ds(tile, 1), 2:2 + 2 * NS].rearrange("p a (b c) -> p (a b) c", c=2),
                                  zs[:, :, 1:3]).then_inc(cnew_done, 1)

        def gate_lo(pair, slot):
            pool.wait_ge(g_hi, pair + 1)
            TT(Gl[:, slot, 0:SEQ], cb[:, 0:SEQ], F(Gh[:, slot, 0:SEQ]), ALU.subtract)
            TT(Gl[:, slot, SEQ:T], cb[:, SEQ + 2:CW:3], F(Gh[:, slot, SEQ:T]), ALU.subtract).then_inc(g_lo, 1)

        pool.wait_ge(par_in, 32)
        for j in range(8):
            split_lo(pool, 28 + j // 2, j % 2)
            keep_conv(j, zb[j % 2], j + 1)
            if j % 2:
                gate_lo(j // 2, j // 2)
        with pool.Fori(0, NG - 1) as g:
            for j in range(12):
                split_lo(pool, 32 + 6 * g + j // 2, j % 2)
                if j in (0, 1):
                    keep_conv(8 * g + 8 + j, zb[j], 8 * g + 9 + j)
                elif j == 5:
                    gate_lo(4 * g + 4, 0)
                elif j >= 6:
                    keep_conv(8 * g + 8 + j - 4, zb[j % 2], 8 * g + 9 + j - 4)
                    if j % 2:
                        gate_lo(4 * g + 4 + (j - 4) // 2, (j - 4) // 2)
        for c in range(2):
            split_lo(pool, C_LAST // 2 + 1, c, (WDh[:, c, :], WDl[:, c, :]))
        for w in range(NPC * KT):
            p, i = w // KT, w % KT
            if i:
                add_squares(p, i, 7 * (NPC + 1 + p) + i - 1, KT + NPC * KT + w + 1, sqe[:, i % 2, :])

    @block.vector
    def _(dve):
        V = nc.vector
        TT, STT, TS = V.tensor_tensor, V.scalar_tensor_tensor, V.tensor_scalar
        link = Link(dve, dve_step)

        def newton(v, s, t, out, step, steps):
            dve.wait_ge(step, steps)
            link(V.reciprocal(s, s))
            link(TT(t, s, s, ALU.mult))
            link(TT(t, t, v, ALU.mult))
            link(TS(t, t, -0.5, 1.5, ALU.mult, ALU.add))
            return TT(out, t, s, ALU.mult)

        def root(p, bank, v, s, t, n):
            dve.wait_ge(stat_done, n + 1)
            TS(v[:, :], PS[:, bank, 0:PC], 1.0 / D, EPS, ALU.mult, ALU.add).then_inc(v_done, 1)
            dve.wait_ge(v_done, n + 1)
            newton(v[:, :], s[:, :], t[:, :], rstd[:, pcs(p)], root_done, n + 1).then_inc(rstd_done, 1)

        V.memset(ones[:, :], 1.0).then_inc(ones_set, 1)
        link(V.memset(mv[:, :, :], 1.0))
        dve.wait_ge(cols_in, 16)
        for k in range(KT):
            dve.wait_ge(x_in[k], 16)
            dve.wait_ge(h_hi, k + 1)
            STT(Hl[:, k, :], x_raw[:, k, :], colsb[:, 0, k:k + 1], F(Hh[:, k, :]), ALU.mult, ALU.subtract)\
                .then_inc(h_lo, 1)
        for p in range(NPC):
            root(p, (6, 7, 6)[p], nv, nsq, nt, p)
        dve.wait_ge(rt_done, 1)
        V.tensor_copy(rtok[:, 0:NB], PS[:, 6, 0:NB]).then_inc(rtok_done, 1)
        V.tensor_copy(rtok[0:NS, NB:NB + 1], PS[0:NS, 6, NB:NB + 1]).then_inc(rtok_done, 1)
        for t in range(NB + 1):
            n = P if t < NB else NS
            dve.wait_ge(gv_done, t + 1)
            link(V.bn_stats(bst[0:n, t, :], gv[0:n, t, :]))
            link(V.bn_aggr(mv[0:n, t, :], bst[0:n, t, :]))
        TS(lnr[:, 0, :], mv[:, :, 1], EPS, None, ALU.add).then_inc(lnv_done, 1)
        dve.wait_ge(lnv_done, 1)
        link(newton(lnr[:, 0, :], lnr[:, 1, :], lnr[:, 2, :], lnr[:, 2, :], lns_done, 1))
        dve.wait_ge(small_in, 96)
        for t in range(NB + 1):
            n = P if t < NB else NS
            link(TS(gv[0:n, t, :], gv[0:n, t, :], mv[0:n, t, 0:1], lnr[0:n, 2, t:t + 1], ALU.subtract, ALU.mult))
            link(TT(gv[0:n, t, :], gv[0:n, t, :], lnvb[0:n, 0, :], ALU.mult))
            TT(vnf[:, t, :] if t < NB else gv[0:NS, NB, :], gv[0:n, t, :], lnvb[0:n, 1, :], ALU.add)\
                .then_inc(ln_done, 1)
        link(TS(snk[:, 0, :], snk[:, 0, :], -1.0, None, ALU.mult))
        link(TS(snS[:, 0:1], snS[:, 0:1], -1.0, None, ALU.mult))
        dve.wait_ge(rope_in, 16)
        r = 0
        for n in range(6):
            dve.wait_ge(w_used, 5 + n)
            if n == 2:
                dve.wait_ge(k_out, 16)
            if n == 3:
                dve.wait_ge(v_out, 16)
                dve.wait_ge(vt_done, 3)
            if n >= 2:
                dve.wait_ge(rot_hi, (n - 2) if n > 2 else 1)
                dve.wait_ge(rot_lo, (n - 2) if n > 2 else 1)
            TT(thirds(zt[:, n % 2, :]), PS[:, 3 * (n % 2):3 * (n % 2) + 3, 0:PC], rstd3, ALU.mult).then_inc(z_ev, 1)
            if n == 3:
                V.tensor_copy(vS[:, :], PS[0:NS, 6, 0:P]).then_inc(vs_done, 1)
            if not rotating(n):
                continue
            r += 1
            dve.wait_ge(z_ev, n + 1)
            dve.wait_ge(swapped, r)
            link(TT(zt[:, n % 2, :], zt[:, n % 2, :], rope_sb[:, 0, :], ALU.mult))
            dve.wait_ge(sw_sin, r)
            TT(zt[:, n % 2, :], zt[:, n % 2, :], sw[:, r % 2 ^ 1, :], ALU.add).then_inc(rot_done, 1)
            dve.wait_ge(rot_done, r)
            if n == 0:
                link(V.tensor_copy(kS[:, :], zt[:, 0, SEQ:T]))
                dve.wait_ge(mixp_done, 1)
                for e in range(2):
                    V.tensor_copy(mixS[64 * e:64 * e + 64, :, :],
                                  PS[64 * e:64 * e + 64, 7, 0:64].rearrange("p (a e b) -> p a e b", e=2, b=NS)[:, :, e, :]
                                  ).then_inc(mix_done, 1)
            else:
                dve.wait_ge(qz_zero, 1)
                Qf = Qz[:, :, :].rearrange("p b c -> p (b c)")
                for g in range(KVH):
                    h = GRP * g + n - 2
                    V.tensor_copy(Qf[64 * g:64 * g + 64, h:h + 72 * (NS - 1) + 1:72],
                                  zt[64 * g:64 * g + 64, n % 2, SEQ:T])
            dve.wait_ge(rot_hi, r)
            hi, lo = (kh[:, :], kl[:, :]) if n == 0 else (QYh[:, n - 2, :], QYl[:, n - 2, :])
            TT(lo, zt[:, n % 2, :], F(hi), ALU.subtract).then_inc(rot_lo, 1)
            if n == 2:
                for i in range(2):
                    dve.wait_ge(vt_hi, i + 1)
                    TT(Vl[:, 4 * i:4 * i + 4, :].rearrange("p b c -> p (b c)"), PS[:, 6 + i, :],
                       F(Vh[:, 4 * i:4 * i + 4, :].rearrange("p b c -> p (b c)")), ALU.subtract).then_inc(vt_lo, 1)
        dve.wait_ge(band_in, 16)

        def fill_ev(f):
            t, p = f // NPC, f % NPC
            if p < 2:
                dve.wait_ge(u_done, 2 * t + p + 1)
            else:
                dve.wait_ge(w_used, C_U + t + 1)
            TT(U[:, t, pcs(p)], PS[:, f % 2, 0:PC], rstd[:, pcs(p)], ALU.mult).then_inc(u_ev, 1)

        for i in range(UNITS + 2):
            if 2 <= i:
                u = i - 2
                dve.wait_ge(pt_hi, u + 1)
                for kt in ((1,) if u < 2 else (0, 1)):
                    last = TT(PTl[:, kt, :], PS[:, 4 + kt, :], F(PTh[:, kt, :]), ALU.subtract)
                last.then_inc(pt_lo, 1)
            if i < UNITS:
                g, lo = i % 2, P if i < 2 else 0
                dve.wait_ge(s_done, i + 1)
                if i >= 2:
                    dve.wait_ge(pt_done, i - 1)
                for h in range(GRP):
                    last = V.tensor_tensor_reduce(
                        out=Pb[:, i % 2, h, lo:], in0=PS[:, 2 + h // 2, (h % 2) * 256 + lo:(h % 2) * 256 + 256],
                        in1=band[:, lo:], scale=1.0, scalar=-3.0e38, op0=ALU.add, op1=ALU.max,
                        accum_out=mx[:, i % 2, h:h + 1])
                last.then_inc(masked, 1)
                dve.wait_ge(masked, i + 1)
                STT(nm[:, i % 2, :], mx[:, i % 2, :], -SCALE, snk[:, 0, GRP * g:GRP * g + GRP], ALU.mult, ALU.min)\
                    .then_inc(nm_done, 1)
                dve.wait_ge(nm_done, i + 1)
                TT(es[:, i % 2, :], nm[:, i % 2, :], snk[:, 1, GRP * g:GRP * g + GRP], ALU.add).then_inc(esin_done, 1)
            if i in FILL:
                fill_ev(FILL[i])
            if i < UNITS:
                dve.wait_ge(exp_done, i + 1)
                dve.wait_ge(es_done, i + 1)
                link(TT(ri[:, i % 2, :], sm[:, i % 2, :], es[:, i % 2, :], ALU.add))
                V.reciprocal(ri[:, i % 2, :], ri[:, i % 2, :]).then_inc(ri_done, 1)
            if 2 <= i:
                u, b, g = i - 2, (i - 2) // 2, (i - 2) % 2
                dve.wait_ge(o_hi, u + 1)
                TT(QYl[64 * g:64 * g + 64, :, blk(b)],
                   PS[64 * g:64 * g + 64, 6, :].rearrange("p (r t) -> p r t", r=GRP),
                   F(QYh[64 * g:64 * g + 64, :, blk(b)]), ALU.subtract).then_inc(o_ev, 1)
        dve.wait_ge(kc_in, 16)
        V.tensor_copy(Kc[:, :, P:P + 1].rearrange("p b a -> p (b a)"), kS[:, :]).then_inc(kn_done, 1)
        dve.wait_ge(ss_sc, 1)
        link(V.tensor_reduce(st[:, 0:1], PS[0:64, 3, 0:P + 1], AX.X, ALU.max))
        link(STT(st[:, 1:2], st[:, 0:1], -SCALE, snS[:, 0:1], ALU.mult, ALU.min))
        TT(st[:, 2:3], st[:, 1:2], snS[:, 1:2], ALU.add).then_inc(sn_done, 1)
        dve.wait_ge(sx_done, 1)
        link(TT(st[:, 5:6], st[:, 3:4], st[:, 4:5], ALU.add))
        link(V.reciprocal(st[:, 5:6], st[:, 5:6]))
        link(TS(Ps[:, :], Ps[:, :], st[:, 5:6], None, ALU.mult))
        TS(Dm[:, :], bmask[:, :], Ps[:, P:P + 1], None, ALU.mult).then_inc(sp_done, 1)
        for b in range(NB):
            dve.wait_ge(vn_hi, b + 1)
            TT(vnl[:, b, :], vnf[:, b, :], F(vnh[:, b, :]), ALU.subtract).then_inc(vn_lo, 1)
        dve.wait_ge(so_hi, 1)
        for g in range(KVH):
            last = TT(QYl[64 * g:64 * g + 64, :, SEQ:T],
                      PS[64 * g:64 * g + 64, 6, 0:64].rearrange("p (b h) -> p h b", h=HEADS)[:, GRP * g:GRP * g + GRP, :],
                      F(QYh[64 * g:64 * g + 64, :, SEQ:T]), ALU.subtract)
        last.then_inc(so_lo, 1)
        dve.wait_ge(w_used, C_A + 1)
        TT(thirds(sig[:, :]), PS[:, 0:3, 0:PC], rstd3, ALU.mult).then_inc(g_ev, 1)
        dve.wait_ge(s_out, 48)
        dve.wait_ge(ws_lo, 1)
        dve.wait_ge(bs_in, 16)
        for u in range(2 * NB):
            hp, b, bank = u // NB, u % NB, 4 + u % 4
            dve.wait_ge(sp_mm, u + 1)
            for e in range(2):
                last = TT(YAt[64 * e:64 * e + 64, 2 * hp:2 * hp + 2, blk(b)],
                          PS[64 * e:64 * e + 64, bank, :].rearrange("p (r e t) -> p r e t", r=2, e=2)[:, :, e, :],
                          bsb[64 * e:64 * e + 64, 2 * hp:2 * hp + 2, :], ALU.add)
            last.then_inc(sp_ev, 1)
            if b == NB - 1:
                for t in (2 * hp, 2 * hp + 1):
                    link(TS(YAt[:, t, SEQ:T], mixS[:, t, :], bsb[:, t, 0:1], None, ALU.add))
                    dve.wait_ge(sp_ev, u + 1)
                    dve.wait_ge(ug_done, t + 1)
                    TT(U[:, t, :], YAt[:, t, :], U[:, t, :], ALU.mult).then_inc(ya_done, 1)
                    dve.wait_ge(ya_hi, t + 1)
                    TT(YAl[:, t, :], U[:, t, :], F(YAh[:, t, :]), ALU.subtract).then_inc(ya_lo, 1)

        def gate_ev(q):
            dve.wait_ge(w_used, C_A + 1 + 2 * q)
            dve.wait_ge(p_ev, q)
            TT(thirds(sig[:, :]), PS[:, 0:3, 0:PC], rstd3, ALU.mult).then_inc(g_ev, 1)

        def branch_a(q):
            dve.wait_ge(th_done, q + 1)
            dve.wait_ge(w_used, C_A + 2 + 2 * q)
            STT(MGv[:, bass.ds(3 * q, 3), :], thirds(sig[:, :]), 1.0, PS[:, 3:6, 0:PC], ALU.add, ALU.mult)\
                .then_inc(p_ev, 1)

        def branch_b(q, m):
            dve.wait_ge(th_done, q + 1)
            dve.wait_ge(w_used, C_A + 2 + 2 * q)
            link(STT(thirds(sig[:, :]), thirds(sig[:, :]), 1.0, PS[:, 3:6, 0:PC], ALU.add, ALU.mult))
            TT(MGv[:, bass.ds(3 * m, 3), :], MGv[:, bass.ds(3 * m, 3), :], thirds(sig[:, :]), ALU.add)\
                .then_inc(p_ev, 1)

        branch_a(0)
        with dve.Fori(1, KT) as q:
            gate_ev(q)
            branch_a(q)
        n0 = link.n
        with dve.Fori(0, KT - 1) as m:
            link.off = m
            gate_ev(m + 8)
            branch_b(m + 8, m)
        link.off = 0
        link.n = n0 + KT - 1
        gate_ev(15)
        branch_b(15, 7)
        def merged_lo(p):
            for h in range(2):
                dve.wait_ge(mg_hi, 2 * p + h + 1)
                STT(MSl[p % 2][:, 4 * h:4 * h + 4, :], MG[:, 4 * h:4 * h + 4, pcs(p)], 0.5,
                    F(MSh[p % 2][:, 4 * h:4 * h + 4, :]), ALU.mult, ALU.subtract).then_inc(mg_lo, 1)

        merged_lo(0)
        for w in range(NPC * KT):
            m, p = w % KT, w // KT
            if w == 5:
                merged_lo(1)
            if w == 10:
                merged_lo(2)
            dve.wait_ge(xr_in[w % 3], 16 * (w // 3 + 1))
            if w < NPC * KT - 1:
                dve.wait_ge(wo_done, w + 1)
            else:
                dve.wait_ge(w_used, C_UP0)
            TT(X1[:, m, pcs(p)], PS[:, w % 6, 0:PC], xr[:, w % 3, :], ALU.add).then_inc(x1_ev, 1)
        for k in range(KT):
            dve.wait_ge(h_hi, KT + k + 1)
            STT(Hl[:, k, :], X1[:, k, :], colsb[:, 1, k:k + 1], F(Hh[:, k, :]), ALU.mult, ALU.subtract)\
                .then_inc(h_lo, 1)
        for p in range(NPC):
            root(p, 6 + p % 2, nvm, nsm, ntm, NPC + p)
        for i in range(2):
            link(V.memset(zb[i][:, 0:2], 0.0))
        dve.wait_ge(par_in, 32)

        def up_ev(s, tile, used, count):
            z = zb[s]
            zs = z[:, SEQ + 2:ZW].rearrange("p (b c) -> p b c", c=3)
            dve.wait_ge(w_used, used)
            dve.wait_ge(rstd_done, 2 * NPC)
            if count is not None:
                dve.wait_ge(cnew_done, count)
            link(TT(thirds(z[:, 2:2 + T]), PS[:, 3 * s:3 * s + 3, 0:PC], rstd3, ALU.mult))
            TT(zs[:, :, 2:3].rearrange("p b c -> p (b c)"), PS[:, 3 * s + 2, PC - NS:PC], rstd[:, SEQ:T], ALU.mult)\
                .then_inc(f_ev, 1)
            V.tensor_copy(zs[:, :, 0:2], cst[:, bass.ds(tile, 1), :, :].rearrange("p a b c -> p (a b) c"))\
                .then_inc(z_rdy, 1)

        def conv(s, tile, count):
            z, c = zb[s], (ca, cb)[s]
            dve.wait_ge(z_rdy, count)
            dve.wait_ge(c0_done, count)
            link(STT(c[:, :], z[:, 1:ZW - 1], cpar[:, bass.ds(tile, 1), 1], c[:, :], ALU.mult, ALU.add))
            STT(c[:, :], z[:, 0:ZW - 2], cpar[:, bass.ds(tile, 1), 0], c[:, :], ALU.mult, ALU.add)\
                .then_inc(conv_done, 1)

        def gated(pair):
            dve.wait_ge(conv_done, 2 * pair + 2)
            dve.wait_ge(gelu_done, pair + 1)
            TT(cb[:, :], ca[:, :], cb[:, :], ALU.mult).then_inc(g_done, 1)

        def down_ev(m):
            s = m % 2
            X = X1v[:, 3 * m:3 * m + 3, :]
            TT(X, X, PS[:, 3 * s:3 * s + 3, 0:PC], ALU.add).then_inc(f_ev, 1)

        for j in range(8):
            up_ev(j % 2, j, C_UP0 + j + 1, j - 1 if j >= 2 else None)
            conv(j % 2, j, j + 1)
            if j % 2:
                gated(j // 2)
        n0 = link.n
        with dve.Fori(0, NG - 1) as g:
            link.off = 16 * g
            for j in range(12):
                used = C_LOOP + 12 * g + j + 1
                if 2 <= j < 6:
                    dve.wait_ge(dn_half, 4 * g + j - 1)
                    down_ev(2 * (j - 2))
                    dve.wait_ge(w_used, used)
                    down_ev(2 * (j - 2) + 1)
                    continue
                i = j if j < 2 else j - 4
                up_ev(j % 2, 8 * g + 8 + i, used, 8 * g + 7 + i)
                conv(j % 2, 8 * g + 8 + i, 8 * g + 9 + i)
                if j % 2:
                    gated(4 * g + 4 + i // 2)
        assert link.n - n0 == 16
        link.off = 0
        link.n = n0 + 16 * (NG - 1)

        def scale(p, m):
            X = X1[:, m, pcs(p)]
            STT(X, X, colsb[:, 2, m:m + 1], rstd[:, pcs(p)], ALU.mult, ALU.mult).then_inc(y_done, 1)

        for w in range(NPC * KT):
            p, i = w // KT, w % KT
            m = LAST_ORDER[p][i]
            dve.wait_ge(last_mm, w + 1)
            X = X1[:, m, pcs(p)]
            TT(X, X, PS[:, m, 0:PC], ALU.add).then_inc(y_ev, 1)
            if (p, i) in LAST_ROOT:
                q = LAST_ROOT[p, i]
                dve.wait_ge(sq_done, KT + NPC * KT + KT * (q + 1))
                root(q, (0, 0, 1)[q], nv2, nsq2, nt2, 2 * NPC + q)
                dve.wait_ge(rstd_done, 2 * NPC + q + 1)
                dve.wait_ge(y_ev, w + 1)
            if p == 2 and 1 <= i <= 4:
                for m in (2 * i - 2, 2 * i - 1):
                    scale(0, m)
            if p == 2 and 5 <= i:
                for m in ((0, 1, 2), (3, 4, 5), (6, 7))[i - 5]:
                    scale(1, m)
        for m in range(KT):
            scale(2, m)

    @block.tensor
    def _(pe):
        MM = nc.tensor.matmul

        def block_of(slot, i):
            return Wh[:, slot, i * P:(i + 1) * P], Wl[:, slot, i * P:(i + 1) * P]

        def tile(s, slot, rh, rl, first=0, n=KT):
            for k in range(n):
                wh, wl = block_of(slot, first + k)
                for p in range(NPC):
                    last = mm3(PS[:, 3 * s + p, 0:PC], wh, wl, rh[:, k, pcs(p)], rl[:, k, pcs(p)], k == 0, k == n - 1)
            return last

        def piece(bank, slot, p):
            for k in range(KT):
                wh, wl = block_of(slot, k)
                last = mm3(PS[:, bank, 0:PC], wh, wl, Hh[:, k, pcs(p)], Hl[:, k, pcs(p)], k == 0, k == KT - 1)
            return last

        def gmv(t, k, bank):
            rows = blk(t) if t < NB else slice(SEQ, T)
            n = P if t < NB else NS
            return mm3(PS[0:n, bank, :], Hh[:, k, rows], Hl[:, k, rows], Wgh[:, k, :], Wgl[:, k, :],
                       k == 0, k == KT - 1)

        for k in range(KT):
            pe.wait_ge(h_lo, k + 1)
            if k % 2 == 0:
                pe.wait_ge(w_lo, k // 2 + 1)
            for t in range(6):
                last = gmv(t, k, t)
                if k == KT - 1:
                    last.then_inc(tok_done, 1)
        pe.wait_ge(ones_set, 1)
        pe.wait_ge(ss_done, KT - 1)
        for p in range(NPC):
            if p == 2:
                pe.wait_ge(v_done, 1)
            MM(PS[:, (6, 7, 6)[p], 0:PC], ones[:, :], ssq[:, pcs(p)], start=True, stop=True).then_inc(stat_done, 1)
        pe.wait_ge(v_done, 2)
        for k in range(KT):
            last = gmv(6, k, 7)
        last.then_inc(tok_done, 1)
        pe.wait_ge(v_done, 3)
        pe.wait_ge(rstd_done, 3)
        for t in range(NB + 1):
            n = P if t < NB else NS
            last = MM(PS[0:n, 6, t:t + 1], rstd[0:1, t * P:t * P + n], ones[0:1, 0:1], start=True, stop=True)
        last.then_inc(rt_done, 1)
        pe.wait_ge(rtok_done, 2)
        for k in range(KT):
            last = gmv(7, k, 6)
        last.then_inc(tok_done, 1)
        pe.wait_ge(gv_done, 1)
        for k in range(KT):
            last = gmv(8, k, 0)
        last.then_inc(w_used, 4)
        for n in range(6):
            pe.wait_ge(w_lo, 5 + n)
            if n == 0:
                pe.wait_ge(gv_done, NB + 1)
            if n >= 2:
                pe.wait_ge(z_ev, n - 1)
            tile(n % 2, n % 2, Hh, Hl).then_inc(w_used, 1)
            if n == 0:
                pe.wait_ge(ln_done, NB + 1)
                for a in range(4):
                    last = MM(PS[:, 7, 16 * a:16 * a + 16], gv[0:NS, NB, blk(a)],
                              wdiag[:, 2 * a:2 * a + 2, :].rearrange("p h b -> p (h b)"), start=True, stop=True)
                last.then_inc(mixp_done, 1)
            if n == 2:
                pe.wait_ge(z_ev, 2)
                pe.wait_ge(mix_done, 2)
                pe.wait_ge(small_in, 96)
                for i in range(2):
                    for b in range(4):
                        last = nc.tensor.transpose(PS[:, 6 + i, blk(b)], zt[:, 1, blk(4 * i + b)], ident[:, :])
                    last.then_inc(vt_done, 1)
            if n == 3:
                pe.wait_ge(vt_lo, 1)
                nc.tensor.transpose(PS[0:NS, 6, 0:P], zt[:, 1, SEQ:T], ident[:, :]).then_inc(vt_done, 1)
        def scores(i):
            b, g = i // 2, i % 2
            rows = slice(64 * g, 64 * g + 64)
            lo = P if b == 0 else 0
            keys = slice((b - 1) * P + lo, (b + 1) * P)
            if i:
                pe.wait_ge(masked, i)
            for h in range(GRP):
                last = mm3(PS[:, 2 + h // 2, (h % 2) * 256 + lo:(h % 2) * 256 + 256],
                           QYh[rows, h, blk(b)], QYl[rows, h, blk(b)], kh[rows, keys], kl[rows, keys], True, True)
            last.then_inc(s_done, 1)

        def fill(f):
            t, p = f // NPC, f % NPC
            if p == 0:
                pe.wait_ge(w_lo, C_U + t + 1)
            if f >= 2:
                pe.wait_ge(u_ev, f - 1)
            piece(f % 2, t % 2, p).then_inc(u_done if p < 2 else w_used, 1)

        pe.wait_ge(z_ev, 6)
        pe.wait_ge(rot_lo, 5)
        pe.wait_ge(vs_done, 1)
        for i in range(UNITS + 2):
            if i < UNITS:
                scores(i)
            if i in FILL:
                fill(FILL[i])
            if 2 <= i:
                u, b = i - 2, (i - 2) // 2
                pe.wait_ge(pt_lo, u + 1)
                if u:
                    pe.wait_ge(o_ev, u)
                kts = (1,) if b == 0 else (0, 1)
                for kt in kts:
                    last = mm3(PS[:, 6, :], Vh[:, b - 1 + kt, :], Vl[:, b - 1 + kt, :], PTh[:, kt, :], PTl[:, kt, :],
                               kt == kts[0], kt == 1)
                last.then_inc(pv_done, 1)
            if 1 <= i <= UNITS:
                u, b = i - 1, (i - 1) // 2
                pe.wait_ge(pn_done, u + 1)
                if u:
                    pe.wait_ge(pt_lo, u)
                for kt in ((1,) if b == 0 else (0, 1)):
                    for h in range(GRP):
                        last = nc.tensor.transpose(PS[:, 4 + kt, blk(h)], Pb[:, u % 2, h, blk(kt)], ident[:, :])
                last.then_inc(pt_done, 1)
        pe.wait_ge(w_lo, C_A + 1)
        pe.wait_ge(u_ev, 12)
        pe.wait_ge(masked, UNITS)
        piece(0, 0, 0)
        pe.wait_ge(kn_done, 1)
        for b in range(NS):
            last = MM(PS[0:64, 3, 0:P + 1], Qz[:, b, :], Kc[:, b, :], start=b == 0, stop=b == NS - 1)
        last.then_inc(ss_sc, 1)
        piece(1, 0, 1)
        pe.wait_ge(sp_done, 1)
        nc.tensor.transpose(PS[:, 4, 0:64], Ps[:, 0:P], ident[0:64, 0:64])
        nc.tensor.transpose(PS[0:NS, 4, 64:128], Dm[:, :], ident[0:64, 0:64]).then_inc(spt_done, 1)
        piece(2, 0, 2).then_inc(w_used, 1)
        pe.wait_ge(sptc_done, 1)
        pe.wait_ge(vc_in, 16)
        pe.wait_ge(o_ev, UNITS)
        MM(PS[:, 6, 0:64], vS[:, :], Dt[:, :], start=True, stop=False)
        for b in range(NS):
            last = MM(PS[:, 6, 8 * b:8 * b + 8], Vc[:, b, :], PTs[:, 8 * b:8 * b + 8], start=False, stop=b == NS - 1)
        last.then_inc(spv_done, 1)
        pe.wait_ge(ws_lo, 1)
        pe.wait_ge(so_lo, 1)
        for u in range(2 * NB):
            hp, b, bank = u // NB, u % NB, 4 + u % 4
            pe.wait_ge(vn_lo, b + 1)
            if u >= 4:
                pe.wait_ge(sp_ev, u - 3)
            for r in range(2):
                a = 2 * hp + r
                last = mm3(PS[:, bank, 256 * r:256 * r + 256], vnh[:, b, blk(a)], vnl[:, b, blk(a)],
                           wsh[:, 2 * a:2 * a + 2, :].rearrange("p h t -> p (h t)"),
                           wsl[:, 2 * a:2 * a + 2, :].rearrange("p h t -> p (h t)"), True, True)
            last.then_inc(sp_mm, 1)

        def gate_mm(q):
            pe.wait_ge(w_lo, C_A + 1 + 2 * q)
            pe.wait_ge(g_ev, q)
            tile(0, 0, Hh, Hl).then_inc(w_used, 1)

        def proj_mm(q, rh, rl):
            pe.wait_ge(w_lo, C_A + 2 + 2 * q)
            tile(1, 1, rh, rl, n=4).then_inc(w_used, 1)

        pe.wait_ge(ya_lo, 4)
        proj_mm(0, YAh, YAl)
        with pe.Fori(1, KT) as q:
            gate_mm(q)
            pe.wait_ge(p_ev, q)
            proj_mm(q, YAh, YAl)
        with pe.Fori(KT, 2 * KT) as q:
            gate_mm(q)
            pe.wait_ge(p_ev, q)
            proj_mm(q, QYh, QYl)
        for w in range(NPC * KT):
            m, p = w % KT, w // KT
            if w >= 6:
                pe.wait_ge(x1_ev, w - 5)
            if p == 0:
                pe.wait_ge(w_lo, C_WO + m + 1)
            for k in range(KT):
                if m == 0 and k % 4 == 0:
                    pe.wait_ge(mg_lo, 2 * p + k // 4 + 1)
                last = mm3(PS[:, w % 6, 0:PC], WOh[:, m, blk(k)], WOl[:, m, blk(k)], MSh[p % 2][:, k, :],
                           MSl[p % 2][:, k, :], k == 0, k == KT - 1)
            if w < NPC * KT - 1:
                last.then_inc(wo_done, 1)
            else:
                last.then_inc(w_used, KT)
            if w in (16, 23):
                q = (w - 16) // 7
                pe.wait_ge(ss_done, 7 * (q + 2))
                MM(PS[:, 6 + q, 0:PC], ones[:, :], rstd[:, pcs(q)], start=True, stop=True).then_inc(stat_done, 1)

        for j in range(8):
            pe.wait_ge(w_lo, C_UP0 + j + 1)
            if j >= 2:
                pe.wait_ge(f_ev, j - 1)
            else:
                pe.wait_ge(x1_ev, NPC * KT)
            for k in range(KT):
                if j == 0:
                    pe.wait_ge(h_lo, KT + k + 1)
                wh, wl = block_of(j % 2, k)
                for p in range(NPC):
                    last = mm3(PS[:, 3 * (j % 2) + p, 0:PC], wh, wl, Hh[:, k, pcs(p)], Hl[:, k, pcs(p)],
                               k == 0, k == KT - 1)
            last.then_inc(w_used, 1)
            if j == 0:
                pe.wait_ge(ss_done, 7 * (NPC + 1))
                pe.wait_ge(v_done, NPC + 1)
                MM(PS[:, 6, 0:PC], ones[:, :], rstd[:, pcs(2)], start=True, stop=True).then_inc(stat_done, 1)
        with pe.Fori(0, NG - 1) as g:
            n = 0
            for j in range(12):
                pe.wait_ge(w_lo, C_LOOP + 12 * g + j + 1)
                if 2 <= j < 6:
                    if j == 2:
                        pe.wait_ge(g_lo, 4 * g + 4)
                    for h in range(2):
                        pe.wait_ge(f_ev, 16 * g + 7 + n)
                        tile(h, j % 2, Gh, Gl, first=GP * h, n=GP).then_inc(w_used if h else dn_half, 1)
                        n += 1
                else:
                    pe.wait_ge(f_ev, 16 * g + 7 + n)
                    tile(j % 2, j % 2, Hh, Hl).then_inc(w_used, 1)
                    n += 1
        assert n == 16
        def last_block(m, k):
            if m < 4:
                return block_of(m // 2, (m % 2) * GP + k)
            i = ((m % 2) * GP + k) * P
            return WDh[:, m // 2 - 2, i:i + P], WDl[:, m // 2 - 2, i:i + P]

        def last_tile(m, k, p):
            wh, wl = last_block(m, k)
            return mm3(PS[:, m, 0:PC], wh, wl, Gh[:, k, pcs(p)], Gl[:, k, pcs(p)], k == 0, k == GP - 1)

        pe.wait_ge(f_ev, 16 * (NG - 1) + 8)
        pe.wait_ge(g_lo, NPAIR - 1)
        for h in range(2):
            pe.wait_ge(w_lo, C_LAST + 2 * h + 2)
            for k in range(GP - 1):
                for m in range(4 * h, 4 * h + 4):
                    last_tile(m, k, 0)
        pe.wait_ge(g_lo, NPAIR)
        for m in range(KT):
            last_tile(m, GP - 1, 0).then_inc(last_mm, 1)
        n = KT
        for p in (1, 2):
            for i, m in enumerate(LAST_ORDER[p]):
                pe.wait_ge(y_ev, KT * (p - 1) + LAST_ORDER[p - 1].index(m) + 1)
                if (p, m) == (2, 0):
                    pe.wait_ge(v_done, 2 * NPC + 2)
                for k in range(GP):
                    last = last_tile(m, k, p)
                last.then_inc(last_mm, 1)
                if (p, i) == (1, 7) or (p, i) == (2, 2):
                    q = p - 1
                    pe.wait_ge(ss_done, 7 * (NPC + 2 + q))
                    pe.wait_ge(y_ev, KT + 1)
                    if q:
                        pe.wait_ge(v_done, 2 * NPC + 1)
                    MM(PS[:, 0, 0:PC], ones[:, :], rstd[:, pcs(q)], start=True, stop=True).then_inc(stat_done, 1)
        pe.wait_ge(ss_done, 7 * (2 * NPC + 1))
        pe.wait_ge(y_ev, 2 * KT + 1)
        MM(PS[:, 1, 0:PC], ones[:, :], rstd[:, pcs(2)], start=True, stop=True).then_inc(stat_done, 1)

    block_cm.__exit__(None, None, None)


def tiles_of(w, cols=None):
    K, N = w.shape
    return np.ascontiguousarray(w.reshape(K // P, P, N // P, P).transpose(2, 1, 0, 3).reshape(N // P, P, K))


def kernel(**inputs):
    import concourse.bacc as bacc
    from concourse.bass_utils import run_bass_kernel_spmd

    a = {k: np.asarray(v) for k, v in inputs.items()}
    f = np.float32
    x = np.concatenate([a["x_prompt"][0], a["x_sample"][:, 0]], axis=0)
    w_in = a["w_in"][0]
    o_q, o_k = 2 * GMW, 2 * GMW + HEADS * HD
    o_v = o_k + KVH * HD
    o_ga = o_v + KVH * HD
    head_order = [h for r in range(GRP) for h in (r, GRP + r)]
    rows_b = np.concatenate([np.arange(h * HD, (h + 1) * HD) for h in head_order])
    gm = w_in[:, GMW:2 * GMW].reshape(4, 2, P, GMW).transpose(0, 2, 1, 3).reshape(4, P, CH)
    w_main = np.concatenate([gm, tiles_of(w_in[:, o_k:o_v]), tiles_of(w_in[:, o_v:o_ga]),
                             tiles_of(w_in[:, o_q:o_k][:, rows_b]), tiles_of(w_in[:, 0:GMW]),
                             tiles_of(w_in[:, o_ga:]), tiles_of(a["w_o"][0])], axis=0)
    w_half = np.concatenate([tiles_of(a["w_pa"][0]), tiles_of(a["w_pb"][0][rows_b])], axis=0)
    up = tiles_of(a["w_up"][0])
    up = np.stack([up[:NPAIR], up[NPAIR:]], axis=1).reshape(NG, 2 * GP, P, CH)
    dn = a["w_down"][0].reshape(NG, GP, P, KT // 2, 2, P).transpose(0, 3, 2, 4, 1, 5).reshape(NG, 4, P, CH)
    parts = [up[0]]
    for g in range(1, NG):
        parts += [up[g][0:2], dn[g - 1], up[g][2:]]
    w_ffn = np.concatenate(parts + [dn[NG - 1]], axis=0)
    cols = np.stack([a["g_mix"][0], a["g_ffn"][0], a["g_final"]]).reshape(3, KT, P).transpose(2, 0, 1)

    half = HD // 2
    inv = (f(10000.0) ** (-np.arange(half, dtype=f) / f(half))).astype(f)
    pos = np.concatenate([np.arange(SEQ), np.full(NS, 8192)]).astype(f)
    ang = (pos[:, None] * inv[None, :]).astype(f)
    cos = np.tile(np.cos(ang).astype(f).T, (4, 1))
    sin = np.sin(ang).astype(f).T
    rope = np.stack([cos, np.tile(np.concatenate([-sin, sin]), (2, 1))], axis=1)
    i = np.arange(P)
    mask = np.zeros((P, 2 * P), f)
    mask[:, :P][i[None, :] < i[:, None]] = MASKED
    mask[:, P:][i[None, :] > i[:, None]] = MASKED
    sinks = a["sinks"][0]
    same = np.repeat(np.eye(NS, dtype=f), HEADS, axis=0)
    by_tile = lambda v: v.reshape(v.shape[:-1] + (2, NPAIR, P))
    par = np.concatenate([a["conv_w"][0], a["conv_b"]], axis=0)
    par = by_tile(par).transpose(3, 2, 1, 0).reshape(P, 2 * NPAIR, 4)
    state = by_tile(a["state_ffn_conv"][0]).transpose(4, 3, 2, 0, 1).reshape(P, 2 * NPAIR, NS, 2)
    w_s = a["w_s"][0]

    ins = {
        "x_t": x.T.reshape(KT, P, T).transpose(1, 0, 2),
        "w_main": w_main, "w_half": w_half, "w_ffn": w_ffn,
        "cols": cols, "rope": rope, "eye": np.eye(P, dtype=f),
        "lnv": np.broadcast_to(np.stack([a["ln_v_g"][0], a["ln_v_b"][0]])[None], (P, 2, GMW)),
        "ws_t": w_s.transpose(2, 0, 1),
        "bs_t": np.repeat(a["b_s"][0], 64, axis=0).reshape(4, P, P).transpose(1, 0, 2),
        "ws_first": np.where(np.eye(NS, dtype=bool)[:, None, :], w_s[:, 0, 0][None, :, None], f(0)),
        "mask": mask,
        "sink_rows": np.broadcast_to(np.stack([sinks, sinks])[None], (P, 2, HEADS)),
        "sink_cols": np.tile(np.stack([sinks, sinks], axis=1), (NS, 1)),
        "same_sample": same,
        "k_cache": a["cache_swa_k"][0].transpose(2, 3, 0, 1).reshape(P, NS, P),
        "v_cache": a["cache_swa_v"][0].transpose(1, 0, 2, 3).reshape(P, NS, P),
        "conv_par": par, "conv_state": state,
    }
    outs = {
        "y": (P, KT, T), "kv_prompt": (2, P, P), "gm_prompt": (P, GMW), "gm_sample": (NS, GMW),
        "k_sample": (P, NS, P), "v_sample": (P - 1, NS, P), "v_new": (NS, P), "conv_new": (P, 2 * NPAIR, 2 + 2 * NS),
    }
    nc = bacc.Bacc("TRN2", target_bir_lowering=False, num_devices=1)
    arrays, aps = {}, {}
    for name, v in ins.items():
        arrays[f"in_{name}"] = np.ascontiguousarray(v)
        aps[name] = nc.dram_tensor(f"in_{name}", v.shape, F32, kind="ExternalInput").ap()
    for name, shape in outs.items():
        aps[name] = nc.dram_tensor(f"out_{name}", shape, F32, kind="ExternalOutput").ap()
    build(nc, **aps)
    r = run_bass_kernel_spmd(nc, [arrays], core_ids=[0]).results[0]
    o = {name: np.asarray(r[f"out_{name}"]).reshape(shape) for name, shape in outs.items()}

    yt = o["y"].transpose(2, 1, 0).reshape(T, D)
    heads = lambda v: v.T.reshape(1, 1, P, KVH, HD)
    k_s = o["k_sample"].transpose(1, 2, 0).reshape(1, NS, P, KVH, HD)
    v_s = np.concatenate([o["v_sample"].transpose(1, 0, 2), o["v_new"][:, None, :]], axis=1)
    conv = o["conv_new"].reshape(P, NPAIR, 2, 2 + 2 * NS).transpose(3, 2, 1, 0).reshape(2 + 2 * NS, 2 * DFF)
    return (yt[None, :SEQ], yt[SEQ:, None], heads(o["kv_prompt"][0]), heads(o["kv_prompt"][1]),
            o["gm_prompt"].reshape(1, 1, P, 8, 64), conv[None, None, 0:2],
            k_s, v_s.reshape(1, NS, P, KVH, HD), o["gm_sample"].reshape(1, NS, 1, 8, 64),
            conv[2:].reshape(1, NS, 2, 2 * DFF))
```

```python
import math
import numpy as np
import concourse.bass as bass
from concourse import mybir

F32 = mybir.dt.float32
F32R = mybir.dt.float32r
ALU = mybir.AluOpType
ACT = mybir.ActivationFunctionType
AX = mybir.AxisListType

P = 128
D = 1024
SEQ = 1024
NS = 8
T = SEQ + NS
NPC = 3
PC = T // NPC
KT = D // P
GMW = 512
NB = SEQ // P
HEADS, KVH, HD = 8, 2, 64
GRP = HEADS // KVH
SCALE = HD ** -0.5
DFF = 3 * D
EPS = 1e-6
NPAIR = DFF // P
GP = 4
NG = NPAIR // GP
ZW = 2 + SEQ + 3 * NS
CW = ZW - 2
CH = 8 * P
MASKED = -1.0e30
LAST_PC = (0, 416, 800, T)
LW = 416
X0 = 4 * P

C_GMV = 0
C_K, C_Q, C_V, C_U = 4, 5, 9, 10
C_G = 14
C_WO = 46
C_UP0 = 54
C_LOOP = 62
C_LAST = 62 + 12 * (NG - 1)


def build(nc, x_t, w_main, w_half, w_ffn, cols, rope, eye, lnv, ws_t, bs_t, ws_first, mask, sink_rows, sink_cols,
          same_sample, k_cache, v_cache, conv_par, conv_state,
          y, kv_prompt, gm_prompt, gm_sample, k_sample, v_sample, v_new, conv_new):
    base = (nc.sbuf_base + 31) // 32 * 32
    arena_bytes = 212800
    nc.alloc_sbuf_tensor("arena", [P, arena_bytes // 4], F32)
    row = T * 4
    R_H = base
    R_QY = R_H + 16 * row
    R_KV = R_QY + 8 * row
    R_M = R_KV + 4 * row
    R_YA = R_M + 8 * row
    R_RSTD = R_YA + 8 * row
    R_RAW = R_RSTD + row
    R_HL = R_RAW + 2 * CH * 4
    R_SMALL = R_HL + 4 * CH * 4
    small_at = [R_SMALL]

    def at(name, shape, dt, offset):
        return nc.alloc_sbuf_tensor_at(name, shape, dt, offset=offset)

    def small(name, shape, dt=F32):
        words = 1
        for s in shape[1:]:
            words *= s
        t = at(name, shape, dt, small_at[0])
        small_at[0] += (words * 4 + 31) // 32 * 32
        assert small_at[0] <= base + arena_bytes, small_at[0] - base - arena_bytes
        return t

    Hh = at("Hh", [P, KT, T], F32R, R_H)
    Hl = at("Hl", [P, KT, T], F32R, R_H + 8 * row)
    WOh = at("WOh", [P, KT, CH], F32R, R_H)
    WOl = at("WOl", [P, KT, CH], F32R, R_H + 8 * CH * 4)
    QYh = at("QYh", [P, GRP, T], F32R, R_QY)
    QYl = at("QYl", [P, GRP, T], F32R, R_QY + 4 * row)
    gv = at("gv", [P, NB + 1, GMW], F32, R_QY)
    lnvb = at("lnvb", [P, 2, GMW], F32, R_QY + 18432)
    bst = at("bst", [P, NB + 1, 6], F32, R_QY + 30784)
    wdiag = at("wdiag", [NS, HEADS, NS], F32, R_QY + 31008)
    sqx = at("sqx", [P, 2, T], F32, R_QY + 22528)
    kh = at("kh", [P, T], F32R, R_KV)
    kl = at("kl", [P, T], F32R, R_KV + row)
    Vh = at("Vh", [P, NB, P], F32R, R_KV + 2 * row)
    Vl = at("Vl", [P, NB, P], F32R, R_KV + 2 * row + NB * P * 4)
    ssq = at("ssq", [P, T], F32, R_KV)
    nsq = at("nsq", [P, T], F32, R_KV + row)
    nt = at("nt", [P, T], F32, R_KV + 2 * row)
    bsb = at("bsb", [P, 4, P], F32, R_KV)
    wsh = at("wsh", [P, HEADS, P], F32R, R_KV + row)
    wsl = at("wsl", [P, HEADS, P], F32R, R_KV + row + 4096)
    sig = at("sig", [P, T], F32, R_KV + row + 8192)
    x_raw = at("x_raw", [P, KT, T], F32, R_M)
    vnf = at("vnf", [P, NB, GMW], F32, R_M)
    vnl = at("vnl", [P, NB, GMW], F32R, R_M)
    vnh = at("vnh", [P, NB, GMW], F32R, R_M + NB * GMW * 4)
    band = at("band", [P, 2 * P], F32, R_M + NB * GMW * 4)
    Qz = at("Qz", [P, NS, 64], F32, R_M + NB * GMW * 4 + 1024)
    R_SA = R_M + NB * GMW * 4 + 3072
    Kc = at("Kc", [P, NS, P + 1], F32, R_SA)
    Vc = at("Vc", [P, NS, P], F32, R_SA + 4128)
    Ps = at("Ps", [64, P + 1], F32, R_SA + 8224)
    PTs = at("PTs", [P, 64], F32, R_SA + 8768)
    Dm = at("Dm", [64, NS], F32, R_SA + 9024)
    ws_raw = at("ws_raw", [P, HEADS, P], F32, R_SA)
    Dt = at("Dt", [NS, 64], F32, R_M + 2 * NB * GMW * 4)
    MG = at("MG", [P, KT, T], F32, R_M)
    Wgh = at("Wgh", [P, KT, GMW], F32R, R_YA)
    Wgl = at("Wgl", [P, KT, GMW], F32R, R_YA + KT * GMW * 4)
    YAh = at("YAh", [P, 4, T], F32R, R_YA)
    YAl = at("YAl", [P, 4, T], F32R, R_YA + 4 * row)
    YAt = at("YAt", [P, 4, T], F32, R_YA)
    U = at("U", [P, 4, T], F32, R_YA + 4 * row)
    rope_sb = at("rope_sb", [P, 2, T], F32, R_YA)
    zt = at("zt", [P, 2, T], F32, R_YA + 2 * row)
    sw = at("sw", [P, 2, T], F32, R_YA + 6 * row)
    Pb = [at(f"Pb{i}", [P, GRP, 2 * P], F32, a) for i, a in enumerate(
        (R_YA, R_YA + 4096, R_M + 2 * NB * GMW * 4 - 4096))]
    PTh = at("PTh", [P, 2, GRP * P], F32R, R_YA + 8192)
    PTl = at("PTl", [P, 2, GRP * P], F32R, R_YA + 12288)
    X1 = at("X1", [P, KT, T], F32, R_YA)
    rstd = at("rstd", [P, T], F32, R_RSTD)
    raw = at("raw", [P, 2, CH], F32, R_RAW)
    Wh = at("Wh", [P, 2, CH], F32R, R_HL)
    Wl = at("Wl", [P, 2, CH], F32R, R_HL + 2 * CH * 4)
    MSh = [at(f"MSh{i}", [P, KT, PC], F32R, R_QY + 2 * i * KT * PC * 4) for i in range(2)]
    MSl = [at(f"MSl{i}", [P, KT, PC], F32R, (R_QY + KT * PC * 4, R_KV)[i]) for i in range(2)]
    xr = at("xr", [P, 3, PC], F32, R_KV + row + 8192)
    Gh = at("Gh", [P, GP, T], F32R, R_QY)
    Gl = at("Gl", [P, GP, T], F32R, R_QY + 4 * row)
    R_Z = R_QY + 8 * row
    zb = [at(f"zb{i}", [P, ZW], F32, R_Z + i * 4224) for i in range(2)]
    ca = at("ca", [P, CW], F32, R_Z + 2 * 4224)
    cb = at("cb", [P, CW], F32, R_Z + 3 * 4224)
    R_WD = R_Z + 4 * 4224
    WDh = at("WDh", [P, 2, CH], F32R, R_WD)
    WDl = at("WDl", [P, 2, CH], F32R, R_WD + 2 * CH * 4)
    WDr = at("WDr", [P, 2, CH], F32, R_WD + 2 * CH * 4)
    R_PAR = R_WD + 4 * CH * 4
    cpar = at("cpar", [P, 2 * NPAIR, 4], F32, R_PAR)
    cst = at("cst", [P, 2 * NPAIR, NS, 2], F32, R_PAR + 768)
    cnew = at("cnew", [P, 2 * NPAIR, 2 + 2 * NS], F32, R_PAR + 768 + 3072)
    sqe = at("sqe", [P, 2, LW], F32, R_PAR + 768 + 3072 + 3456)
    assert R_PAR + 768 + 3072 + 3456 + 2 * LW * 4 <= R_YA
    R_N2 = R_Z
    nv2 = at("nv2", [P, LW], F32, R_N2)
    nsq2 = at("nsq2", [P, LW], F32, R_N2 + LW * 4)
    nt2 = at("nt2", [P, LW], F32, R_N2 + 2 * LW * 4)
    nsm = at("nsm", [P, T], F32, R_QY)
    ntm = at("ntm", [P, T], F32, R_QY + row)
    colsb = small("colsb", [P, 3, KT])
    ident = small("ident", [P, P])
    ones = small("ones", [P, P])
    vS = small("vS", [NS, P])
    mixS = small("mixS", [P, 4, NS])
    rtok = small("rtok", [P, NB + 1])
    mv = small("mv", [P, NB + 1, 2])
    lnr = small("lnr", [P, 3, NB + 1])
    kS = small("kS", [P, NS])
    snk = small("snk", [P, 2, HEADS])
    snS = small("snS", [64, 2])
    mx = small("mx", [P, 2, GRP])
    nm = small("nm", [P, 2, GRP])
    sm = small("sm", [P, 2, GRP])
    es = small("es", [P, 2, GRP])
    ri = small("ri", [P, 2, GRP])
    st = small("st", [64, 6])
    bmask = small("bmask", [64, NS])

    PS = nc.alloc_psum_tensor("PS", [P, 8, 512], F32)
    MGv = MG[:, :, :].rearrange("p k (c t) -> p (k c) t", c=NPC)
    X1v = X1[:, :, :].rearrange("p k (c t) -> p (k c) t", c=NPC)
    rstd3 = rstd[:, :].rearrange("p (c t) -> p c t", c=NPC)

    def thirds(ap):
        return ap.rearrange("p (c t) -> p c t", c=NPC)

    def pcs(p):
        return slice(p * PC, (p + 1) * PC)

    def blk(b):
        return slice(b * P, (b + 1) * P)

    def sem(name):
        return nc.alloc_semaphore(name)

    raw_full = [sem("raw_full0"), sem("raw_full1")]
    w_hi, w_lo, w_used = sem("w_hi"), sem("w_lo"), sem("w_used")
    x_in = [sem(f"x_in{k}") for k in range(KT)]
    x0_in, w0_in, h0_hi, h0_lo, w0_hi, w0_lo = (sem("x0_in"), sem("w0_in"), sem("h0_hi"), sem("h0_lo"), sem("w0_hi"),
                                                sem("w0_lo"))
    cols_in, small_in, rope_in, band_in = sem("cols_in"), sem("small_in"), sem("rope_in"), sem("band_in")
    wd_in, wd_hi, wd_lo = sem("wd_in"), sem("wd_hi"), sem("wd_lo")
    kc_in, vc_in, ws_in, bs_in, par_in = sem("kc_in"), sem("vc_in"), sem("ws_in"), sem("bs_in"), sem("par_in")
    xr_in = [sem(f"xr_in{k}") for k in range(3)]
    k_out, v_out, gm_out, s_out, y_out = sem("k_out"), sem("v_out"), sem("gm_out"), sem("s_out"), sem("y_out")
    ones_set, h_hi, h_lo, sq_done, ss_done = sem("ones_set"), sem("h_hi"), sem("h_lo"), sem("sq_done"), sem("ss_done")
    stat_done, v_done, root_done, rstd_done = sem("stat_done"), sem("v_done"), sem("root_done"), sem("rstd_done")
    tok_done, rt_done, rtok_done, gv_done = sem("tok_done"), sem("rt_done"), sem("rtok_done"), sem("gv_done")
    lnv_done, lns_done, ln_done, mixp_done, mix_done = (sem("lnv_done"), sem("lns_done"), sem("ln_done"),
                                                        sem("mixp_done"), sem("mix_done"))
    ln_sub, ln_mul = sem("ln_sub"), sem("ln_mul")
    z_ev, swapped, sw_sin, rot_done, rot_hi, rot_lo = (sem("z_ev"), sem("swapped"), sem("sw_sin"), sem("rot_done"),
                                                       sem("rot_hi"), sem("rot_lo"))
    vt_done, vt_hi, vt_lo, vs_done, qz_zero = sem("vt_done"), sem("vt_hi"), sem("vt_lo"), sem("vs_done"), sem("qz_zero")
    s_done, masked, nm_done, esin_done, exp_done, es_done, ri_done, pn_done = (
        sem("s_done"), sem("masked"), sem("nm_done"), sem("esin_done"), sem("exp_done"), sem("es_done"),
        sem("ri_done"), sem("pn_done"))
    pt_done, pt_hi, pt_lo, pv_done, o_hi, o_ev, u_done, u_ev = (
        sem("pt_done"), sem("pt_hi"), sem("pt_lo"), sem("pv_done"), sem("o_hi"), sem("o_ev"), sem("u_done"), sem("u_ev"))
    kn_done, ss_sc, sn_done, sx_done, sp_done, spt_done, sptc_done, spv_done, so_hi, so_lo = (
        sem("kn_done"), sem("ss_sc"), sem("sn_done"), sem("sx_done"), sem("sp_done"), sem("spt_done"),
        sem("sptc_done"), sem("spv_done"), sem("so_hi"), sem("so_lo"))
    tri_done, ws_hi, ws_lo, vn_hi, vn_lo, ug_done = (sem("tri_done"), sem("ws_hi"), sem("ws_lo"), sem("vn_hi"),
                                                     sem("vn_lo"), sem("ug_done"))
    sp_mm, sp_ev, ya_done, ya_hi, ya_lo = sem("sp_mm"), sem("sp_ev"), sem("ya_done"), sem("ya_hi"), sem("ya_lo")
    g_ev, th_done, p_ev, mg_hi, mg_lo, wo_done, x1_ev = (sem("g_ev"), sem("th_done"), sem("p_ev"), sem("mg_hi"),
                                                         sem("mg_lo"), sem("wo_done"), sem("x1_ev"))
    f_ev, z_rdy, c0_done, conv_done, cnew_done, gelu_done, g_done, g_hi, g_lo, dn_half = (
        sem("f_ev"), sem("z_rdy"), sem("c0_done"), sem("conv_done"), sem("cnew_done"), sem("gelu_done"),
        sem("g_done"), sem("g_hi"), sem("g_lo"), sem("dn_half"))
    last_mm, y_ev, sum_done, yg_done, y_done, y_done_p = (sem("last_mm"), sem("y_ev"), sem("sum_done"), sem("yg_done"),
                                                          sem("y_done"), sem("y_done_p"))
    dve_step, pool_step = sem("dve_step"), sem("pool_step")

    class Link:

        def __init__(self, eng, s):
            self.eng, self.s, self.n, self.off = eng, s, 0, 0

        def __call__(self, ins):
            self.n += 1
            ins.then_inc(self.s, 1)
            self.eng.wait_ge(self.s, self.off + self.n)

    def mm3(out, ah, al, bh, bl, first, last):
        nc.tensor.matmul(out, ah, bh, start=first, stop=False)
        nc.tensor.matmul(out, ah, bl, start=False, stop=False)
        return nc.tensor.matmul(out, al, bh, start=False, stop=last)

    F = lambda ap: ap.bitcast(F32)

    def load(sp, half, j, src, n=CH, wait=True):
        if wait:
            sp.wait_ge(w_lo, 2 * half + j - 1)
        sp.dma_start(raw[:, j, 0:n], src).then_inc(raw_full[j], 16)

    def split_hi(act, half, j, dst=None, n=CH, used=None):
        act.wait_ge(raw_full[j], 16 * half + 16)
        if used is None:
            used = 2 * half + j - 1
        if used is not False:
            act.wait_ge(w_used, used)
        nc.scalar.activation(Wh[:, j, 0:n] if dst is None else dst, raw[:, j, 0:n], ACT.Copy).then_inc(w_hi, 1)

    def split_lo(pool, half, j, dst=None, n=CH):
        h, l = (Wh[:, j, 0:n], Wl[:, j, 0:n]) if dst is None else dst
        pool.wait_ge(w_hi, 2 * half + j + 1)
        nc.gpsimd.tensor_tensor(l, raw[:, j, 0:n], F(h), ALU.subtract).then_inc(w_lo, 1)

    def gmv_dst(c):
        return (Wgh[:, 2 * c:2 * c + 2, :].rearrange("p k n -> p (k n)"),
                Wgl[:, 2 * c:2 * c + 2, :].rearrange("p k n -> p (k n)"))

    UNITS = 2 * NB
    HALVES = [2, 2, 2] + [1] * 13 + [2, 1]
    FILL = [[2 + sum(HALVES[:i]) + n for n in range(HALVES[i])] for i in range(UNITS + 2)]
    U_END = [[i for i in range(UNITS + 2) if 2 * NPC * (t + 1) - 1 in FILL[i]][0] for t in range(4)]

    VN_ORDER = [0, 4, 5, 6, 7, 1, 2, 3]

    def filled(i):
        return [n // 2 for n in FILL[i] if n % 2]

    LAST_ORDER = [list(range(KT)), list(range(KT)), [1, 2, 3, 4, 5, 6, 7, 0]]
    LAST_ROOT = {(1, 3): 0, (2, 3): 1, (2, 7): 2}
    YP = 3

    def lcs(p):
        return slice(LAST_PC[p], LAST_PC[p + 1])

    def lw(p):
        return LAST_PC[p + 1] - LAST_PC[p]

    block_cm = nc.Block()
    block = block_cm.__enter__()

    @block.sync
    def _(sp):
        def x_load(k):
            sp.dma_start(x_raw[:, k, :], x_t[:, k, :]).then_inc(x_in[k], 16)

        sp.dma_start(raw[:, 0, 0:GMW], w_main[0, :, 0:GMW]).then_inc(w0_in, 16)
        sp.dma_start(x_raw[:, 0, 0:X0], x_t[:, 0, 0:X0]).then_inc(x0_in, 16)
        sp.dma_start(x_raw[:, 0, X0:T], x_t[:, 0, X0:T]).then_inc(x_in[0], 16)
        sp.dma_start(raw[:, 0, GMW:CH], w_main[0, :, GMW:CH]).then_inc(raw_full[0], 16)
        x_load(1)
        load(sp, 0, 1, w_main[1], wait=False)
        for k in range(2, KT):
            x_load(k)
        for c in (2, 3, 4, 5):
            load(sp, c // 2, c % 2, w_main[c])
        sp.wait_ge(w_used, 4)
        sp.dma_start(rope_sb[:, :, :], rope).then_inc(rope_in, 16)
        load(sp, 3, 0, w_main[6])
        load(sp, 3, 1, w_main[7])
        sp.wait_ge(gv_done, NB + 1)
        sp.dma_start(band[:, :], mask).then_inc(band_in, 16)
        sp.dma_start(Kc[:, :, 0:P], k_cache).then_inc(kc_in, 16)
        sp.dma_start(Vc[:, :, :], v_cache).then_inc(vc_in, 16)
        sp.wait_ge(ln_done, NB + 1)
        sp.dma_start(gm_prompt, vnf[:, NB - 1, :]).then_inc(gm_out, 16)
        sp.dma_start(gm_sample, gv[0:NS, NB, :]).then_inc(gm_out, 16)
        sp.wait_ge(vc_in, 16)
        sp.dma_start(v_sample, Vc[:, :, :]).then_inc(s_out, 16)
        sp.wait_ge(rot_done, 1)
        sp.dma_start(kv_prompt[0], zt[:, 0, SEQ - P:SEQ]).then_inc(k_out, 16)
        load(sp, 4, 0, w_main[8])
        sp.wait_ge(kn_done, 1)
        sp.dma_start(k_sample, Kc[:, :, 1:P + 1]).then_inc(s_out, 16)
        for c in (9, 10, 11):
            load(sp, c // 2, c % 2, w_main[c])
        sp.wait_ge(z_ev, 6)
        sp.dma_start(kv_prompt[1], zt[:, 1, SEQ - P:SEQ]).then_inc(v_out, 16)
        sp.wait_ge(vs_done, 1)
        sp.dma_start(v_new, vS[:, :]).then_inc(s_out, 16)
        load(sp, 6, 0, w_main[12])
        sp.wait_ge(ss_sc, 1)
        sp.wait_ge(s_out, 48)
        sp.dma_start(ws_raw[:, :, :], ws_t).then_inc(ws_in, 16)
        for c in (13, 14):
            load(sp, c // 2, c % 2, w_main[c])
        load(sp, 7, 1, w_half[0], n=CH // 2)
        sp.wait_ge(pv_done, UNITS)
        sp.dma_start(bsb[:, :, :], bs_t).then_inc(bs_in, 16)
        load(sp, 8, 0, w_main[15])
        load(sp, 8, 1, w_half[1], n=CH // 2)
        with sp.Fori(2, 16) as q:
            load(sp, q + 7, 0, w_main[q + 14])
            load(sp, q + 7, 1, w_half[q], n=CH // 2)
        for m in range(4):
            load(sp, 23 + m // 2, m % 2, w_main[30 + m])
        sp.wait_ge(p_ev, 16)
        for w in range(NPC * KT):
            if w >= 3:
                sp.wait_ge(x1_ev, w - 2)
            sp.dma_start(xr[:, w % 3, :], x_t[:, w % KT, pcs(w // KT)]).then_inc(xr_in[w % 3], 16)
            if w + 4 < KT:
                load(sp, 25 + w // 2, w % 2, w_main[34 + w])
            if w == KT - 2:
                load(sp, 27, 0, w_ffn[0])
            if w == KT - 1:
                load(sp, 27, 1, w_ffn[1])
        sp.wait_ge(ss_done, 7 * (NPC + 1))
        for dst, src in ((cpar, conv_par), (cst, conv_state)):
            sp.dma_start(dst.ap(), src).then_inc(par_in, 16)
        for c in range(2, 8):
            load(sp, 27 + c // 2, c % 2, w_ffn[c])
        for c in range(2):
            sp.dma_start(WDr[:, c, :], w_ffn[C_LAST - C_UP0 + 2 + c]).then_inc(wd_in, 16)
        with sp.Fori(0, NG - 1) as g:
            for c in range(12):
                load(sp, 31 + 6 * g + c // 2, c % 2, w_ffn[8 + 12 * g + c])
        for c in range(2):
            load(sp, C_LAST // 2 + c // 2, c % 2, w_ffn[C_LAST - C_UP0 + c])
        sp.wait_ge(cnew_done, 2 * NPAIR)
        sp.dma_start(conv_new, cnew[:, :, :]).then_inc(y_out, 16)
        for p in (0, 1):
            for h in range(2):
                sp.wait_ge(y_done_p, KT * p + 4 * (h + 1))
                rows = slice(4 * h, 4 * h + 4)
                sp.dma_start(y[:, rows, lcs(p)], X1[:, rows, lcs(p)]).then_inc(y_out, 16)
        sp.wait_ge(y_done_p, 2 * KT + YP)
        sp.dma_start(y[:, KT - YP:KT, lcs(2)], X1[:, KT - YP:KT, lcs(2)]).then_inc(y_out, 16)
        sp.wait_ge(y_done, KT - YP)
        sp.dma_start(y[:, 0:KT - YP, lcs(2)], X1[:, 0:KT - YP, lcs(2)]).then_inc(y_out, 16)
        sp.wait_ge(gm_out, 32)
        sp.wait_ge(k_out, 16)
        sp.wait_ge(v_out, 16)
        sp.wait_ge(s_out, 48)
        sp.wait_ge(y_out, 16 * 7)

    @block.scalar
    def _(act):
        A = nc.scalar.activation
        act.dma_start(colsb[:, :, :], cols).then_inc(cols_in, 16)
        for dst, src in ((ident, eye), (lnvb, lnv), (wdiag, ws_first), (snk, sink_rows), (snS, sink_cols),
                         (bmask, same_sample)):
            act.dma_start(dst.ap(), src).then_inc(small_in, 16)
        act.wait_ge(w0_in, 16)
        A(Wgh[:, 0, :], raw[:, 0, 0:GMW], ACT.Copy).then_inc(w0_hi, 1)
        act.wait_ge(cols_in, 16)
        act.wait_ge(x0_in, 16)
        A(Hh[:, 0, 0:X0], x_raw[:, 0, 0:X0], ACT.Copy, scale=colsb[:, 0, 0:1]).then_inc(h0_hi, 1)
        for k in range(KT):
            act.wait_ge(x_in[k], 16)
            c0 = X0 if k == 0 else 0
            A(Hh[:, k, c0:T], x_raw[:, k, c0:T], ACT.Copy, scale=colsb[:, 0, k:k + 1]).then_inc(h_hi, 1)
            if k == 0:
                act.wait_ge(raw_full[0], 16)
                A(Wgh[:, 1, :], raw[:, 0, GMW:CH], ACT.Copy).then_inc(w_hi, 1)
            elif k in (1, 3, 5):
                c = {1: 1, 3: 2, 5: 3}[k]
                split_hi(act, c // 2, c % 2, gmv_dst(c)[0], used=False)
            if k >= 3:
                act.wait_ge(ss_done, k - 2)
            A(ssq[:, :] if k == 0 else sqx[:, k % 2, :], x_raw[:, k, :], ACT.Square).then_inc(sq_done, 1)
        for c in (4, 5):
            split_hi(act, c // 2, c % 2, used=False)
        act.wait_ge(v_done, NPC)
        A(nsq[:, :], ssq[:, :], ACT.Sqrt).then_inc(root_done, 1)
        for t in range(NB + 1):
            n, bank = P if t < NB else NS, t % 7
            if t == 0:
                act.wait_ge(rtok_done, 2)
            if t < NB:
                act.wait_ge(tok_done, t + 1)
            else:
                act.wait_ge(w_used, 4)
            A(gv[0:n, t, :], PS[0:n, bank, :], ACT.Gelu_apprx_tanh, scale=rtok[0:n, t:t + 1]).then_inc(gv_done, 1)
        act.wait_ge(lnv_done, 1)
        A(lnr[:, 1, :], lnr[:, 0, :], ACT.Sqrt).then_inc(lns_done, 1)
        for n in range(6):
            split_hi(act, 3 + n // 2, n % 2)
            if n < 5:
                act.wait_ge(z_ev, n + 1)
                if n >= 2:
                    act.wait_ge(rot_done, n - 1)
                for i in range(4):
                    last = A(sw[32 * i:32 * i + 32, n % 2, :], zt[32 * (i ^ 1):32 * (i ^ 1) + 32, n % 2, :], ACT.Copy)
                last.then_inc(swapped, 1)
                if n == 1:
                    act.wait_ge(mix_done, 2)
                    act.wait_ge(gm_out, 32)
                act.wait_ge(rot_done, n + 1)
                A(kh[:, :] if n == 0 else QYh[:, n - 1, :], zt[:, n % 2, :], ACT.Copy).then_inc(rot_hi, 1)
        for i in range(2):
            act.wait_ge(vt_done, i + 1)
            A(Vh[:, 4 * i:4 * i + 4, :].rearrange("p b c -> p (b c)"), PS[:, 6 + i, :], ACT.Copy).then_inc(vt_hi, 1)

        def vn_round(b):
            A(vnh[:, b, :], vnf[:, b, :], ACT.Copy).then_inc(vn_hi, 1)

        for i in range(UNITS + 2):
            for t in range(3):
                if i == U_END[t] + 1:
                    split_hi(act, (12 + t) // 2, t % 2)
            if 2 <= i:
                u = i - 2
                act.wait_ge(pt_done, u + 1)
                if u >= 1:
                    act.wait_ge(pv_done, u)
                else:
                    act.wait_ge(v_out, 16)
                for kt in ((1,) if u < 2 else (0, 1)):
                    last = A(PTh[:, kt, :], PS[:, 4 + kt, :], ACT.Copy)
                last.then_inc(pt_hi, 1)
            if i < UNITS:
                lo = P if i < 2 else 0
                act.wait_ge(nm_done, i + 1)
                for h in range(GRP):
                    last = A(Pb[i % 3][:, h, lo:], Pb[i % 3][:, h, lo:], ACT.Exp, scale=SCALE,
                             bias=nm[:, i % 2, h:h + 1], accum_out=sm[:, i % 2, h:h + 1])
                last.then_inc(exp_done, 1)
                act.wait_ge(esin_done, i + 1)
                A(es[:, i % 2, :], es[:, i % 2, :], ACT.Exp).then_inc(es_done, 1)
            if 2 <= i:
                u, b, g = i - 2, (i - 2) // 2, (i - 2) % 2
                act.wait_ge(pv_done, u + 1)
                A(QYh[64 * g:64 * g + 64, :, blk(b)],
                  PS[64 * g:64 * g + 64, 6, :].rearrange("p (r t) -> p r t", r=GRP), ACT.Copy).then_inc(o_hi, 1)
            if i == 2:
                act.wait_ge(sn_done, 1)
                A(Ps[:, :], PS[0:64, 7, 0:P + 1], ACT.Exp, scale=SCALE, bias=st[:, 1:2], accum_out=st[:, 3:4])
                A(st[:, 4:5], st[:, 2:3], ACT.Exp).then_inc(sx_done, 1)
            if i == 4:
                act.wait_ge(spt_done, 1)
                A(PTs[:, :], PS[:, 7, 256:320], ACT.Copy)
                A(Dt[:, :], PS[0:NS, 7, 320:384], ACT.Copy).then_inc(sptc_done, 1)
            if i == 6:
                act.wait_ge(spv_done, 1)
                for g in range(KVH):
                    last = A(QYh[64 * g:64 * g + 64, :, SEQ:T],
                             PS[64 * g:64 * g + 64, 7, 384:448].rearrange("p (b h) -> p h b", h=HEADS)
                             [:, GRP * g:GRP * g + GRP, :], ACT.Copy)
                last.then_inc(so_hi, 1)
            if i == UNITS:
                act.wait_ge(masked, UNITS)
                act.wait_ge(s_out, 48)
                act.wait_ge(spv_done, 1)
                for b in VN_ORDER[:3]:
                    vn_round(b)
        act.wait_ge(tri_done, 1)
        A(wsh[:, :, :], ws_raw[:, :, :], ACT.Copy).then_inc(ws_hi, 1)
        for b in VN_ORDER[3:]:
            if b == 1:
                act.wait_ge(ws_lo, 1)
            vn_round(b)
        split_hi(act, 7, 1, n=CH // 2)
        for t in range(4):
            act.wait_ge(u_ev, 3 * t + 3)
            A(U[:, t, :], U[:, t, :], ACT.Gelu_apprx_tanh).then_inc(ug_done, 1)
        act.wait_ge(g_ev, 1)
        A(sig[:, :], sig[:, :], ACT.Tanh, scale=0.5).then_inc(th_done, 1)
        split_hi(act, 8, 0)
        for t in range(4):
            act.wait_ge(ya_done, t + 1)
            A(YAh[:, t, :], U[:, t, :], ACT.Copy).then_inc(ya_hi, 1)
        split_hi(act, 8, 1, n=CH // 2)

        def ffn_in_hi(act, k):
            if k < 6:
                act.wait_ge(wo_done, 2 * KT + k + 2)
            else:
                act.wait_ge(w_used, C_UP0)
            A(Hh[:, k, :], X1[:, k, :], ACT.Copy, scale=colsb[:, 1, k:k + 1]).then_inc(h_hi, 1)

        def gate(q):
            act.wait_ge(g_ev, q + 1)
            A(sig[:, :], sig[:, :], ACT.Tanh, scale=0.5).then_inc(th_done, 1)

        with act.Fori(1, 15) as q:
            split_hi(act, q + 8, 0)
            gate(q)
            split_hi(act, q + 8, 1, n=CH // 2)
        def merged_hi(p, k0, k1):
            A(MSh[p % 2][:, k0:k1, :], MG[:, k0:k1, pcs(p)], ACT.Copy, scale=0.5).then_inc(mg_hi, 1)

        act.wait_ge(p_ev, 15)
        merged_hi(0, 0, KT - 1)
        split_hi(act, 23, 0, WOh[:, 0, :], used=45)
        gate(15)
        split_hi(act, 23, 1, WOh[:, 1, :], used=45)
        split_hi(act, 24, 0, WOh[:, 2, :], used=45)
        act.wait_ge(p_ev, 16)
        merged_hi(0, KT - 1, KT)
        for w in range(NPC * KT):
            m, p = w % KT, w // KT
            if w + 3 < KT:
                split_hi(act, 23 + (w + 3) // 2, (w + 3) % 2, WOh[:, w + 3, :], used=45)
            if w == 4:
                merged_hi(1, 0, KT)
            if w == 9:
                act.wait_ge(wo_done, KT)
                merged_hi(2, 0, KT)
            if w in (10, 12):
                split_hi(act, 27, (w - 10) // 2, used=46)
            act.wait_ge(x1_ev, w + 1)
            A(rstd[:, pcs(p)] if m == 0 else MG[:, m, pcs(p)], X1[:, m, pcs(p)], ACT.Square).then_inc(sq_done, 1)
            if w >= 18:
                ffn_in_hi(act, w - 18)
        for k in (6, 7):
            ffn_in_hi(act, k)
        act.wait_ge(v_done, 2 * NPC)
        A(nsm[:, :], rstd[:, :], ACT.Sqrt).then_inc(root_done, 1)
        act.wait_ge(par_in, 32)

        def after_a(pair):
            act.wait_ge(z_rdy, 2 * pair + 1)
            act.wait_ge(g_done, pair)
            A(ca[:, :], zb[0][:, 2:ZW], ACT.Identity, scale=cpar[:, bass.ds(2 * pair, 1), 2],
              bias=cpar[:, bass.ds(2 * pair, 1), 3]).then_inc(c0_done, 1)

        def after_b(pair, gated=True):
            act.wait_ge(conv_done, 2 * pair + 1)
            A(ca[:, :], ca[:, :], ACT.Gelu_apprx_tanh).then_inc(gelu_done, 1)
            act.wait_ge(z_rdy, 2 * pair + 2)
            act.wait_ge(g_lo, pair)
            A(cb[:, :], zb[1][:, 2:ZW], ACT.Identity, scale=cpar[:, bass.ds(2 * pair + 1, 1), 2],
              bias=cpar[:, bass.ds(2 * pair + 1, 1), 3]).then_inc(c0_done, 1)
            if gated:
                gate_hi(pair, None)

        def gate_hi(pair, slot):
            slot = gate_slot[0] if slot is None else slot
            act.wait_ge(g_done, pair + 1)
            A(Gh[:, slot, 0:SEQ], cb[:, 0:SEQ], ACT.Copy)
            A(Gh[:, slot, SEQ:T], cb[:, SEQ + 2:CW:3], ACT.Copy).then_inc(g_hi, 1)

        gate_slot = [0]
        for j in range(8):
            split_hi(act, 28 + j // 2, j % 2)
            gate_slot[0] = j // 2
            (after_b if j % 2 else after_a)(j // 2)
        act.wait_ge(wd_in, 32)
        for c in range(2):
            A(WDh[:, c, :], WDr[:, c, :], ACT.Copy).then_inc(wd_hi, 1)
        with act.Fori(0, NG - 1) as g:
            for j in range(12):
                split_hi(act, 32 + 6 * g + j // 2, j % 2)
                if j == 0:
                    after_a(4 * g + 4)
                elif j == 1:
                    after_b(4 * g + 4, gated=False)
                elif j == 5:
                    act.wait_ge(w_used, C_LOOP + 12 * g + 6)
                    gate_hi(4 * g + 4, 0)
                elif j >= 6:
                    gate_slot[0] = (j - 4) // 2
                    (after_b if j % 2 else after_a)(4 * g + 4 + (j - 4) // 2)
        for w in range(NPC * KT):
            p, i = w // KT, w % KT
            m = LAST_ORDER[p][i]
            X = X1[:, m, lcs(p)]
            act.wait_ge(y_ev, w + 1)
            if i >= 1 and w >= 3:
                act.wait_ge(sum_done, 7 * p + max(i - 2, 0))
            A(rstd[:, lcs(p)] if i == 0 else sqe[:, i % 2, 0:lw(p)], X, ACT.Square).then_inc(sq_done, 1)
            act.wait_ge(sq_done, KT + NPC * KT + w + 1)
            A(X, X, ACT.Copy, scale=colsb[:, 2, m:m + 1]).then_inc(yg_done, 1)
            if (p, i) in LAST_ROOT:
                q = LAST_ROOT[p, i]
                act.wait_ge(v_done, 2 * NPC + q + 1)
                A(nsq2[:, 0:lw(q)], nv2[:, 0:lw(q)], ACT.Sqrt).then_inc(root_done, 1)

    @block.gpsimd
    def _(pool):
        TT = nc.gpsimd.tensor_tensor

        def add_squares(p, i, own, sq, buf):
            pool.wait_ge(sq_done, sq)
            if i > 1:
                pool.wait_ge(ss_done, own)
            TT(rstd[:, pcs(p)], rstd[:, pcs(p)], buf, ALU.add).then_inc(ss_done, 1)

        for k in range(KT):
            if k == 0:
                pool.wait_ge(w0_hi, 1)
                TT(Wgl[:, 0, :], raw[:, 0, 0:GMW], F(Wgh[:, 0, :]), ALU.subtract).then_inc(w0_lo, 1)
                pool.wait_ge(w_hi, 1)
                TT(Wgl[:, 1, :], raw[:, 0, GMW:CH], F(Wgh[:, 1, :]), ALU.subtract).then_inc(w_lo, 1)
            elif k in (1, 3, 5):
                c = {1: 1, 3: 2, 5: 3}[k]
                split_lo(pool, c // 2, c % 2, gmv_dst(c))
            if k:
                pool.wait_ge(sq_done, k + 1)
                if k > 1:
                    pool.wait_ge(ss_done, k - 1)
                TT(ssq[:, :], ssq[:, :], sqx[:, k % 2, :], ALU.add).then_inc(ss_done, 1)
        for c in (4, 5):
            split_lo(pool, c // 2, c % 2)
        pool.wait_ge(gv_done, NB + 1)
        nc.gpsimd.memset(Qz[:, :, :], 0.0).then_inc(qz_zero, 1)
        pool.wait_ge(small_in, 96)
        for t in range(NB + 1):
            n = P if t < NB else NS
            pool.wait_ge(ln_sub, t + 1)
            TT(gv[0:n, t, :], gv[0:n, t, :], lnvb[0:n, 0, :], ALU.mult).then_inc(ln_mul, 1)
        for n in range(6):
            split_lo(pool, 3 + n // 2, n % 2)
            if n < 5:
                pool.wait_ge(swapped, n + 1)
                if n == 0:
                    pool.wait_ge(rope_in, 16)
                TT(sw[:, n % 2, :], sw[:, n % 2, :], rope_sb[:, 1, :], ALU.mult).then_inc(sw_sin, 1)
        for i in range(UNITS):
            for t in range(3):
                if i == U_END[t] + 1:
                    split_lo(pool, (12 + t) // 2, t % 2)
            lo = P if i < 2 else 0
            pool.wait_ge(ri_done, i + 1)
            for h in range(GRP):
                last = nc.gpsimd.tensor_scalar(Pb[i % 3][:, h, lo:], Pb[i % 3][:, h, lo:], ri[:, i % 2, h:h + 1],
                                               None, ALU.mult)
            last.then_inc(pn_done, 1)
            if i == UNITS - 4:
                pool.wait_ge(ws_in, 16)
                nc.gpsimd.affine_select(out=ws_raw[:, :, :], in_=ws_raw[:, :, :], compare_op=ALU.is_ge, fill=0.0,
                                        base=0, pattern=[[0, HEADS], [1, P]], channel_multiplier=-1)\
                    .then_inc(tri_done, 1)
        pool.wait_ge(ws_hi, 1)
        TT(wsl[:, :, :], ws_raw[:, :, :], F(wsh[:, :, :]), ALU.subtract).then_inc(ws_lo, 1)
        split_lo(pool, 7, 1, n=CH // 2)
        split_lo(pool, 8, 0)
        split_lo(pool, 8, 1, n=CH // 2)
        with pool.Fori(1, 15) as q:
            split_lo(pool, q + 8, 0)
            split_lo(pool, q + 8, 1, n=CH // 2)
        for m in range(3):
            split_lo(pool, 23 + m // 2, m % 2, (WOh[:, m, :], WOl[:, m, :]))
        for w in range(NPC * KT):
            m, p = w % KT, w // KT
            if w + 3 < KT:
                split_lo(pool, 23 + (w + 3) // 2, (w + 3) % 2, (WOh[:, w + 3, :], WOl[:, w + 3, :]))
            if w in (10, 12):
                split_lo(pool, 27, (w - 10) // 2)
            if m:
                add_squares(p, m, 7 * (p + 1) + m - 1, KT + w + 1, MG[:, m, pcs(p)])

        def keep_conv(tile, z, count):
            zs = z[:, SEQ + 2:ZW].rearrange("p (b c) -> p b c", c=3)
            pool.wait_ge(z_rdy, count)
            nc.gpsimd.tensor_copy(cnew[:, bass.ds(tile, 1), 0:2], z[:, SEQ:SEQ + 2].rearrange("p (a c) -> p a c", a=1))
            nc.gpsimd.tensor_copy(cnew[:, bass.ds(tile, 1), 2:2 + 2 * NS].rearrange("p a (b c) -> p (a b) c", c=2),
                                  zs[:, :, 1:3]).then_inc(cnew_done, 1)

        def gate_lo(pair, slot):
            pool.wait_ge(g_hi, pair + 1)
            TT(Gl[:, slot, 0:SEQ], cb[:, 0:SEQ], F(Gh[:, slot, 0:SEQ]), ALU.subtract)
            TT(Gl[:, slot, SEQ:T], cb[:, SEQ + 2:CW:3], F(Gh[:, slot, SEQ:T]), ALU.subtract).then_inc(g_lo, 1)

        pool.wait_ge(par_in, 32)
        for j in range(8):
            split_lo(pool, 28 + j // 2, j % 2)
            keep_conv(j, zb[j % 2], j + 1)
            if j % 2:
                gate_lo(j // 2, j // 2)
        for c in range(2):
            pool.wait_ge(wd_hi, c + 1)
            TT(WDl[:, c, :], WDr[:, c, :], F(WDh[:, c, :]), ALU.subtract).then_inc(wd_lo, 1)
        with pool.Fori(0, NG - 1) as g:
            for j in range(12):
                split_lo(pool, 32 + 6 * g + j // 2, j % 2)
                if j in (0, 1):
                    keep_conv(8 * g + 8 + j, zb[j], 8 * g + 9 + j)
                elif j == 5:
                    gate_lo(4 * g + 4, 0)
                elif j >= 6:
                    keep_conv(8 * g + 8 + j - 4, zb[j % 2], 8 * g + 9 + j - 4)
                    if j % 2:
                        gate_lo(4 * g + 4 + (j - 4) // 2, (j - 4) // 2)
        for q in range(NPC):
            pool.wait_ge(rstd_done, 3 + q)
            pool.wait_ge(yg_done, KT * (q + 1))
            for m in range(KT - YP if q == 2 else 0, KT):
                TT(X1[:, m, lcs(q)], X1[:, m, lcs(q)], rstd[:, lcs(q)], ALU.mult).then_inc(y_done_p, 1)

    @block.vector
    def _(dve):
        V = nc.vector
        TT, STT, TS = V.tensor_tensor, V.scalar_tensor_tensor, V.tensor_scalar
        link = Link(dve, dve_step)

        def newton(v, s, t, out, step, steps):
            dve.wait_ge(step, steps)
            link(V.reciprocal(s, s))
            link(TT(t, s, s, ALU.mult))
            link(TT(t, t, v, ALU.mult))
            link(TS(t, t, -0.5, 1.5, ALU.mult, ALU.add))
            return TT(out, t, s, ALU.mult)

        def mean(v, bank, n):
            dve.wait_ge(stat_done, n + 1)
            w = v.shape[-1]
            TS(v, PS[:, bank, 0:w], 1.0 / D, EPS, ALU.mult, ALU.add).then_inc(v_done, 1)

        V.memset(ones[:, :], 1.0).then_inc(ones_set, 1)
        link(V.memset(mv[:, :, :], 1.0))
        dve.wait_ge(cols_in, 16)
        dve.wait_ge(x0_in, 16)
        dve.wait_ge(h0_hi, 1)
        STT(Hl[:, 0, 0:X0], x_raw[:, 0, 0:X0], colsb[:, 0, 0:1], F(Hh[:, 0, 0:X0]), ALU.mult, ALU.subtract)\
            .then_inc(h0_lo, 1)
        for k in range(KT):
            c0 = X0 if k == 0 else 0
            dve.wait_ge(x_in[k], 16)
            dve.wait_ge(h_hi, k + 1)
            STT(Hl[:, k, c0:T], x_raw[:, k, c0:T], colsb[:, 0, k:k + 1], F(Hh[:, k, c0:T]), ALU.mult, ALU.subtract)\
                .then_inc(h_lo, 1)
        for p in range(NPC):
            mean(ssq[:, pcs(p)], 5 + p, p)
        dve.wait_ge(v_done, NPC)
        newton(ssq[:, :], nsq[:, :], nt[:, :], rstd[:, :], root_done, 1).then_inc(rstd_done, 1)
        dve.wait_ge(rt_done, 1)
        V.tensor_copy(rtok[:, 0:NB], PS[:, 7, 0:NB]).then_inc(rtok_done, 1)
        V.tensor_copy(rtok[0:NS, NB:NB + 1], PS[0:NS, 7, NB:NB + 1]).then_inc(rtok_done, 1)
        for t in range(NB + 1):
            n = P if t < NB else NS
            dve.wait_ge(gv_done, t + 1)
            link(V.bn_stats(bst[0:n, t, :], gv[0:n, t, :]))
            link(V.bn_aggr(mv[0:n, t, :], bst[0:n, t, :]))
        TS(lnr[:, 0, :], mv[:, :, 1], EPS, None, ALU.add).then_inc(lnv_done, 1)
        dve.wait_ge(lnv_done, 1)
        link(newton(lnr[:, 0, :], lnr[:, 1, :], lnr[:, 2, :], lnr[:, 2, :], lns_done, 1))
        dve.wait_ge(small_in, 96)
        for t in range(NB + 1):
            n = P if t < NB else NS
            TS(gv[0:n, t, :], gv[0:n, t, :], mv[0:n, t, 0:1], lnr[0:n, 2, t:t + 1], ALU.subtract, ALU.mult)\
                .then_inc(ln_sub, 1)
        for t in range(NB + 1):
            n = P if t < NB else NS
            dve.wait_ge(ln_mul, t + 1)
            TT(vnf[:, t, :] if t < NB else gv[0:NS, NB, :], gv[0:n, t, :], lnvb[0:n, 1, :], ALU.add)\
                .then_inc(ln_done, 1)
        link(TS(snk[:, 0, :], snk[:, 0, :], -1.0, None, ALU.mult))
        link(TS(snS[:, 0:1], snS[:, 0:1], -1.0, None, ALU.mult))
        dve.wait_ge(rope_in, 16)
        def tile_ev(n):
            dve.wait_ge(w_used, 5 + n)
            if n == 2:
                dve.wait_ge(k_out, 16)
            if n >= 2:
                dve.wait_ge(rot_hi, n - 1)
                dve.wait_ge(rot_lo, n - 1)
            TT(thirds(zt[:, n % 2, :]), PS[:, 3 * (n % 2):3 * (n % 2) + 3, 0:PC], rstd3, ALU.mult).then_inc(z_ev, 1)

        def rotated_lo(n):
            dve.wait_ge(rot_done, n + 1)
            if n == 0:
                link(V.tensor_copy(kS[:, :], zt[:, 0, SEQ:T]))
                dve.wait_ge(kc_in, 16)
                V.tensor_copy(Kc[:, :, P:P + 1].rearrange("p b a -> p (b a)"), kS[:, :]).then_inc(kn_done, 1)
            else:
                dve.wait_ge(qz_zero, 1)
                Qf = Qz[:, :, :].rearrange("p b c -> p (b c)")
                for g in range(KVH):
                    h = GRP * g + n - 1
                    V.tensor_copy(Qf[64 * g:64 * g + 64, h:h + 72 * (NS - 1) + 1:72],
                                  zt[64 * g:64 * g + 64, n % 2, SEQ:T])
            dve.wait_ge(rot_hi, n + 1)
            hi, lo = (kh[:, :], kl[:, :]) if n == 0 else (QYh[:, n - 1, :], QYl[:, n - 1, :])
            TT(lo, zt[:, n % 2, :], F(hi), ALU.subtract).then_inc(rot_lo, 1)

        for n in range(5):
            tile_ev(n)
            if n == 1:
                dve.wait_ge(mixp_done, 1)
                for e in range(2):
                    V.tensor_copy(mixS[64 * e:64 * e + 64, :, :],
                                  PS[64 * e:64 * e + 64, 7, 0:64].rearrange("p (a e b) -> p a e b", e=2, b=NS)[:, :, e, :]
                                  ).then_inc(mix_done, 1)
            if n:
                rotated_lo(n - 1)
            dve.wait_ge(z_ev, n + 1)
            dve.wait_ge(swapped, n + 1)
            link(TT(zt[:, n % 2, :], zt[:, n % 2, :], rope_sb[:, 0, :], ALU.mult))
            dve.wait_ge(sw_sin, n + 1)
            TT(zt[:, n % 2, :], zt[:, n % 2, :], sw[:, n % 2, :], ALU.add).then_inc(rot_done, 1)
        tile_ev(5)
        rotated_lo(4)
        dve.wait_ge(vt_done, 3)
        V.tensor_copy(vS[:, :], PS[0:NS, 1, 0:P]).then_inc(vs_done, 1)
        for i in range(2):
            dve.wait_ge(vt_hi, i + 1)
            TT(Vl[:, 4 * i:4 * i + 4, :].rearrange("p b c -> p (b c)"), PS[:, 6 + i, :],
               F(Vh[:, 4 * i:4 * i + 4, :].rearrange("p b c -> p (b c)")), ALU.subtract).then_inc(vt_lo, 1)
        dve.wait_ge(band_in, 16)

        def fill_ev(f):
            t, p = f // NPC, f % NPC
            if p < 2:
                dve.wait_ge(u_done, 2 * t + p + 1)
            else:
                dve.wait_ge(w_used, C_U + t + 1)
            TT(U[:, t, pcs(p)], PS[:, f % 2, 0:PC], rstd[:, pcs(p)], ALU.mult).then_inc(u_ev, 1)

        def vn_rest(b):
            dve.wait_ge(vn_hi, VN_ORDER.index(b) + 1)
            TT(vnl[:, b, :], vnf[:, b, :], F(vnh[:, b, :]), ALU.subtract).then_inc(vn_lo, 1)

        fill_ev(0)
        for i in range(UNITS + 2):
            if i < UNITS:
                g, lo = i % 2, P if i < 2 else 0
                dve.wait_ge(s_done, i + 1)
                if i >= 3:
                    dve.wait_ge(pt_done, i - 2)
                for h in range(GRP):
                    last = V.tensor_tensor_reduce(
                        out=Pb[i % 3][:, h, lo:], in0=PS[:, 2 + h // 2, (h % 2) * 256 + lo:(h % 2) * 256 + 256],
                        in1=band[:, lo:], scale=1.0, scalar=-3.0e38, op0=ALU.add, op1=ALU.max,
                        accum_out=mx[:, i % 2, h:h + 1])
                last.then_inc(masked, 1)
                dve.wait_ge(masked, i + 1)
                STT(nm[:, i % 2, :], mx[:, i % 2, :], -SCALE, snk[:, 0, GRP * g:GRP * g + GRP], ALU.mult, ALU.min)\
                    .then_inc(nm_done, 1)
                dve.wait_ge(nm_done, i + 1)
                TT(es[:, i % 2, :], nm[:, i % 2, :], snk[:, 1, GRP * g:GRP * g + GRP], ALU.add).then_inc(esin_done, 1)
            if 2 <= i:
                u = i - 2
                dve.wait_ge(pt_hi, u + 1)
                for kt in ((1,) if u < 2 else (0, 1)):
                    last = TT(PTl[:, kt, :], PS[:, 4 + kt, :], F(PTh[:, kt, :]), ALU.subtract)
                last.then_inc(pt_lo, 1)
            for f in filled(i):
                fill_ev(f)
            if i < UNITS:
                dve.wait_ge(exp_done, i + 1)
                dve.wait_ge(es_done, i + 1)
                link(TT(ri[:, i % 2, :], sm[:, i % 2, :], es[:, i % 2, :], ALU.add))
                V.reciprocal(ri[:, i % 2, :], ri[:, i % 2, :]).then_inc(ri_done, 1)
            if 2 <= i:
                u, b, g = i - 2, (i - 2) // 2, (i - 2) % 2
                dve.wait_ge(o_hi, u + 1)
                TT(QYl[64 * g:64 * g + 64, :, blk(b)],
                   PS[64 * g:64 * g + 64, 6, :].rearrange("p (r t) -> p r t", r=GRP),
                   F(QYh[64 * g:64 * g + 64, :, blk(b)]), ALU.subtract).then_inc(o_ev, 1)
            if i == 1:
                dve.wait_ge(ss_sc, 1)
                link(V.tensor_reduce(st[:, 0:1], PS[0:64, 7, 0:P + 1], AX.X, ALU.max))
                link(STT(st[:, 1:2], st[:, 0:1], -SCALE, snS[:, 0:1], ALU.mult, ALU.min))
                TT(st[:, 2:3], st[:, 1:2], snS[:, 1:2], ALU.add).then_inc(sn_done, 1)
            if i == 3:
                dve.wait_ge(sx_done, 1)
                link(TT(st[:, 5:6], st[:, 3:4], st[:, 4:5], ALU.add))
                link(V.reciprocal(st[:, 5:6], st[:, 5:6]))
                link(TS(Ps[:, :], Ps[:, :], st[:, 5:6], None, ALU.mult))
                TS(Dm[:, :], bmask[:, :], Ps[:, P:P + 1], None, ALU.mult).then_inc(sp_done, 1)
            if i == 7:
                dve.wait_ge(so_hi, 1)
                for g in range(KVH):
                    last = TT(QYl[64 * g:64 * g + 64, :, SEQ:T],
                              PS[64 * g:64 * g + 64, 7, 384:448].rearrange("p (b h) -> p h b", h=HEADS)
                              [:, GRP * g:GRP * g + GRP, :], F(QYh[64 * g:64 * g + 64, :, SEQ:T]), ALU.subtract)
                last.then_inc(so_lo, 1)
            if i == UNITS:
                for b in VN_ORDER[:3]:
                    vn_rest(b)
        for b in VN_ORDER[3:]:
            vn_rest(b)
        dve.wait_ge(w_used, C_G + 1)
        TT(thirds(sig[:, :]), PS[:, 0:3, 0:PC], rstd3, ALU.mult).then_inc(g_ev, 1)
        dve.wait_ge(ws_lo, 1)
        dve.wait_ge(bs_in, 16)
        for u in range(2 * NB):
            hp, b, bank = u // NB, VN_ORDER[u % NB], 4 + u % 4
            dve.wait_ge(sp_mm, u + 1)
            for e in range(2):
                last = TT(YAt[64 * e:64 * e + 64, 2 * hp:2 * hp + 2, blk(b)],
                          PS[64 * e:64 * e + 64, bank, :].rearrange("p (r e t) -> p r e t", r=2, e=2)[:, :, e, :],
                          bsb[64 * e:64 * e + 64, 2 * hp:2 * hp + 2, :], ALU.add)
            last.then_inc(sp_ev, 1)
        for t in range(4):
            link(TS(YAt[:, t, SEQ:T], mixS[:, t, :], bsb[:, t, 0:1], None, ALU.add))
        dve.wait_ge(sp_ev, 2 * NB)
        for t in range(4):
            dve.wait_ge(ug_done, t + 1)
            TT(U[:, t, :], YAt[:, t, :], U[:, t, :], ALU.mult).then_inc(ya_done, 1)

        def gate_ev(q):
            dve.wait_ge(w_used, C_G + 1 + 2 * q)
            dve.wait_ge(p_ev, q)
            TT(thirds(sig[:, :]), PS[:, 0:3, 0:PC], rstd3, ALU.mult).then_inc(g_ev, 1)

        def branch_a(q):
            dve.wait_ge(th_done, q + 1)
            dve.wait_ge(w_used, C_G + 2 + 2 * q)
            STT(MGv[:, bass.ds(3 * q, 3), :], thirds(sig[:, :]), 1.0, PS[:, 3:6, 0:PC], ALU.add, ALU.mult)\
                .then_inc(p_ev, 1)

        def branch_b(q, m):
            dve.wait_ge(th_done, q + 1)
            dve.wait_ge(w_used, C_G + 2 + 2 * q)
            link(STT(thirds(sig[:, :]), thirds(sig[:, :]), 1.0, PS[:, 3:6, 0:PC], ALU.add, ALU.mult))
            TT(MGv[:, bass.ds(3 * m, 3), :], MGv[:, bass.ds(3 * m, 3), :], thirds(sig[:, :]), ALU.add)\
                .then_inc(p_ev, 1)

        branch_a(0)
        for t in range(4):
            dve.wait_ge(ya_hi, t + 1)
            TT(YAl[:, t, :], U[:, t, :], F(YAh[:, t, :]), ALU.subtract).then_inc(ya_lo, 1)
        with dve.Fori(1, KT) as q:
            gate_ev(q)
            branch_a(q)
        n0 = link.n
        with dve.Fori(0, KT - 1) as m:
            link.off = m
            gate_ev(m + 8)
            branch_b(m + 8, m)
        link.off = 0
        link.n = n0 + KT - 1

        def merged_lo(p, k0, k1, n):
            dve.wait_ge(mg_hi, n)
            STT(MSl[p % 2][:, k0:k1, :], MG[:, k0:k1, pcs(p)], 0.5, F(MSh[p % 2][:, k0:k1, :]),
                ALU.mult, ALU.subtract).then_inc(mg_lo, 1)

        def ffn_in_lo(k):
            dve.wait_ge(h_hi, KT + k + 1)
            STT(Hl[:, k, :], X1[:, k, :], colsb[:, 1, k:k + 1], F(Hh[:, k, :]), ALU.mult, ALU.subtract)\
                .then_inc(h_lo, 1)

        merged_lo(0, 0, KT - 1, 1)
        gate_ev(15)
        branch_b(15, 7)
        merged_lo(0, KT - 1, KT, 2)
        for w in range(NPC * KT):
            m, p = w % KT, w // KT
            if w == 5:
                merged_lo(1, 0, KT, 3)
            if w == 10:
                merged_lo(2, 0, KT, 4)
            dve.wait_ge(xr_in[w % 3], 16 * (w // 3 + 1))
            if w < NPC * KT - 1:
                dve.wait_ge(wo_done, w + 1)
            else:
                dve.wait_ge(w_used, C_UP0)
            TT(X1[:, m, pcs(p)], PS[:, w % 6, 0:PC], xr[:, w % 3, :], ALU.add).then_inc(x1_ev, 1)
            if w == 19:
                mean(rstd[:, pcs(0)], 6, NPC)
            if w >= 19:
                ffn_in_lo(w - 19)
        mean(rstd[:, pcs(1)], 7, NPC + 1)
        for k in (5, 6, 7):
            ffn_in_lo(k)
        mean(rstd[:, pcs(2)], 6, NPC + 2)
        dve.wait_ge(v_done, 2 * NPC)
        newton(rstd[:, :], nsm[:, :], ntm[:, :], rstd[:, :], root_done, 2).then_inc(rstd_done, 1)
        for i in range(2):
            link(V.memset(zb[i][:, 0:2], 0.0))
        dve.wait_ge(par_in, 32)

        def up_ev(s, tile, used, count):
            z = zb[s]
            zs = z[:, SEQ + 2:ZW].rearrange("p (b c) -> p b c", c=3)
            dve.wait_ge(w_used, used)
            dve.wait_ge(rstd_done, 2)
            if count is not None:
                dve.wait_ge(cnew_done, count)
            link(TT(thirds(z[:, 2:2 + T]), PS[:, 3 * s:3 * s + 3, 0:PC], rstd3, ALU.mult))
            TT(zs[:, :, 2:3].rearrange("p b c -> p (b c)"), PS[:, 3 * s + 2, PC - NS:PC], rstd[:, SEQ:T], ALU.mult)\
                .then_inc(f_ev, 1)
            V.tensor_copy(zs[:, :, 0:2], cst[:, bass.ds(tile, 1), :, :].rearrange("p a b c -> p (a b) c"))\
                .then_inc(z_rdy, 1)

        def conv(s, tile, count):
            z, c = zb[s], (ca, cb)[s]
            dve.wait_ge(z_rdy, count)
            dve.wait_ge(c0_done, count)
            link(STT(c[:, :], z[:, 1:ZW - 1], cpar[:, bass.ds(tile, 1), 1], c[:, :], ALU.mult, ALU.add))
            STT(c[:, :], z[:, 0:ZW - 2], cpar[:, bass.ds(tile, 1), 0], c[:, :], ALU.mult, ALU.add)\
                .then_inc(conv_done, 1)

        def gated(pair):
            dve.wait_ge(conv_done, 2 * pair + 2)
            dve.wait_ge(gelu_done, pair + 1)
            TT(cb[:, :], ca[:, :], cb[:, :], ALU.mult).then_inc(g_done, 1)

        def down_ev(m):
            s = m % 2
            X = X1v[:, 3 * m:3 * m + 3, :]
            TT(X, X, PS[:, 3 * s:3 * s + 3, 0:PC], ALU.add).then_inc(f_ev, 1)

        for j in range(8):
            up_ev(j % 2, j, C_UP0 + j + 1, j - 1 if j >= 2 else None)
            conv(j % 2, j, j + 1)
            if j % 2:
                gated(j // 2)
        n0 = link.n
        with dve.Fori(0, NG - 1) as g:
            link.off = 16 * g
            for j in range(12):
                used = C_LOOP + 12 * g + j + 1
                if 2 <= j < 6:
                    dve.wait_ge(dn_half, 4 * g + j - 1)
                    down_ev(2 * (j - 2))
                    dve.wait_ge(w_used, used)
                    down_ev(2 * (j - 2) + 1)
                    continue
                i = j if j < 2 else j - 4
                up_ev(j % 2, 8 * g + 8 + i, used, 8 * g + 7 + i)
                conv(j % 2, 8 * g + 8 + i, 8 * g + 9 + i)
                if j % 2:
                    gated(4 * g + 4 + i // 2)
        assert link.n - n0 == 16
        link.off = 0
        link.n = n0 + 16 * (NG - 1)

        def add_square(p, i):
            dve.wait_ge(sq_done, KT + NPC * KT + KT * p + i + 1)
            if i > 1:
                dve.wait_ge(sum_done, 7 * p + i - 1)
            TT(rstd[:, lcs(p)], rstd[:, lcs(p)], sqe[:, i % 2, 0:lw(p)], ALU.add).then_inc(sum_done, 1)

        for w in range(NPC * KT):
            p, i = w // KT, w % KT
            m = LAST_ORDER[p][i]
            dve.wait_ge(last_mm, w + 1)
            X = X1[:, m, lcs(p)]
            TT(X, X, PS[:, m, 0:lw(p)], ALU.add).then_inc(y_ev, 1)
            if i >= 2:
                add_square(p, i - 1)
            if i == KT - 1:
                add_square(p, i)
            if (p, i) in LAST_ROOT:
                q = LAST_ROOT[p, i]
                n = 2 * NPC + q
                mean(nv2[:, 0:lw(q)], (0, 0, 1)[q], n)
                dve.wait_ge(v_done, n + 1)
                newton(nv2[:, 0:lw(q)], nsq2[:, 0:lw(q)], nt2[:, 0:lw(q)], rstd[:, lcs(q)], root_done, 3 + q)\
                    .then_inc(rstd_done, 1)
        dve.wait_ge(rstd_done, 5)
        dve.wait_ge(yg_done, NPC * KT)
        for m in range(KT - YP):
            TT(X1[:, m, lcs(2)], X1[:, m, lcs(2)], rstd[:, lcs(2)], ALU.mult).then_inc(y_done, 1)

    @block.tensor
    def _(pe):
        MM = nc.tensor.matmul

        def block_of(slot, i):
            return Wh[:, slot, i * P:(i + 1) * P], Wl[:, slot, i * P:(i + 1) * P]

        def tile(s, slot, rh, rl, first=0, n=KT):
            for k in range(n):
                wh, wl = block_of(slot, first + k)
                for p in range(NPC):
                    last = mm3(PS[:, 3 * s + p, 0:PC], wh, wl, rh[:, k, pcs(p)], rl[:, k, pcs(p)], k == 0, k == n - 1)
            return last

        def piece(bank, slot, p):
            for k in range(KT):
                wh, wl = block_of(slot, k)
                last = mm3(PS[:, bank, 0:PC], wh, wl, Hh[:, k, pcs(p)], Hl[:, k, pcs(p)], k == 0, k == KT - 1)
            return last

        def gmv(t, k, bank):
            rows = blk(t) if t < NB else slice(SEQ, T)
            n = P if t < NB else NS
            return mm3(PS[0:n, bank, :], Hh[:, k, rows], Hl[:, k, rows], Wgh[:, k, :], Wgl[:, k, :],
                       k == 0, k == KT - 1)

        pe.wait_ge(h0_lo, 1)
        pe.wait_ge(w0_lo, 1)
        for t in range(4):
            gmv(t, 0, t)
        for k in range(KT):
            pe.wait_ge(h_lo, k + 1)
            if k % 2 or k == 2:
                pe.wait_ge(w_lo, (k + 1) // 2)
            if k == 2:
                pe.wait_ge(w_lo, 2)
            elif k and k % 2 == 0:
                pe.wait_ge(w_lo, k // 2 + 1)
            for t in range(4 if k == 0 else 0, 5):
                last = gmv(t, k, t)
                if k == KT - 1:
                    last.then_inc(tok_done, 1)
        pe.wait_ge(ones_set, 1)
        pe.wait_ge(ss_done, KT - 1)
        for p in range(NPC):
            MM(PS[:, 5 + p, 0:PC], ones[:, :], ssq[:, pcs(p)], start=True, stop=True).then_inc(stat_done, 1)
        for t in (5, 6):
            pe.wait_ge(v_done, t - 4)
            for k in range(KT):
                last = gmv(t, k, t)
            last.then_inc(tok_done, 1)
        pe.wait_ge(v_done, 3)
        pe.wait_ge(rstd_done, 1)
        for t in range(NB + 1):
            n = P if t < NB else NS
            last = MM(PS[0:n, 7, t:t + 1], rstd[0:1, t * P:t * P + n], ones[0:1, 0:1], start=True, stop=True)
        last.then_inc(rt_done, 1)
        for t in (7, 8):
            pe.wait_ge(gv_done, t - 6)
            for k in range(KT):
                last = gmv(t, k, t - 7)
            last.then_inc(*((tok_done, 1) if t == 7 else (w_used, 4)))
        for n in range(6):
            pe.wait_ge(w_lo, 5 + n)
            if n == 0:
                pe.wait_ge(gv_done, NB + 1)
            if n >= 2:
                pe.wait_ge(z_ev, n - 1)
            tile(n % 2, n % 2, Hh, Hl).then_inc(w_used, 1)
            if n == 1:
                pe.wait_ge(ln_done, NB + 1)
                for a in range(4):
                    last = MM(PS[:, 7, 16 * a:16 * a + 16], gv[0:NS, NB, blk(a)],
                              wdiag[:, 2 * a:2 * a + 2, :].rearrange("p h b -> p (h b)"), start=True, stop=True)
                last.then_inc(mixp_done, 1)
        def scores(i):
            b, g = i // 2, i % 2
            rows = slice(64 * g, 64 * g + 64)
            lo = P if b == 0 else 0
            keys = slice((b - 1) * P + lo, (b + 1) * P)
            if i:
                pe.wait_ge(masked, i)
            for h in range(GRP):
                last = mm3(PS[:, 2 + h // 2, (h % 2) * 256 + lo:(h % 2) * 256 + 256],
                           QYh[rows, h, blk(b)], QYl[rows, h, blk(b)], kh[rows, keys], kl[rows, keys], True, True)
            last.then_inc(s_done, 1)

        def fill(n):
            f, h = n // 2, n % 2
            t, p = f // NPC, f % NPC
            if n == 2 * NPC * t:
                pe.wait_ge(w_lo, C_U + t + 1)
            if n == 2:
                pe.wait_ge(vs_done, 1)
            elif h == 0 and f:
                pe.wait_ge(u_ev, f - 1)
            for k in range(4 * h, 4 * h + 4):
                wh, wl = block_of(t % 2, k)
                last = mm3(PS[:, f % 2, 0:PC], wh, wl, Hh[:, k, pcs(p)], Hl[:, k, pcs(p)], k == 0, k == KT - 1)
            if h:
                last.then_inc(u_done if p < 2 else w_used, 1)

        pe.wait_ge(z_ev, 5)
        fill(0)
        fill(1)
        pe.wait_ge(z_ev, 6)
        pe.wait_ge(mix_done, 2)
        pe.wait_ge(small_in, 96)
        for i in range(2):
            for b in range(4):
                last = nc.tensor.transpose(PS[:, 6 + i, blk(b)], zt[:, 1, blk(4 * i + b)], ident[:, :])
            last.then_inc(vt_done, 1)
        nc.tensor.transpose(PS[0:NS, 1, 0:P], zt[:, 1, SEQ:T], ident[:, :]).then_inc(vt_done, 1)
        pe.wait_ge(rot_lo, 5)
        for i in range(UNITS + 2):
            if i < UNITS:
                scores(i)
            if 2 <= i:
                u, b = i - 2, (i - 2) // 2
                pe.wait_ge(pn_done, u + 1)
                if u:
                    pe.wait_ge(pt_lo, u)
                for kt in ((1,) if b == 0 else (0, 1)):
                    for h in range(GRP):
                        last = nc.tensor.transpose(PS[:, 4 + kt, blk(h)], Pb[u % 3][:, h, blk(kt)], ident[:, :])
                last.then_inc(pt_done, 1)
            for n in FILL[i]:
                fill(n)
            if i == 1:
                pe.wait_ge(kn_done, 1)
                pe.wait_ge(vt_lo, 2)
                for b in range(NS):
                    last = MM(PS[0:64, 7, 0:P + 1], Qz[:, b, :], Kc[:, b, :], start=b == 0, stop=b == NS - 1)
                last.then_inc(ss_sc, 1)
            if i == 4:
                pe.wait_ge(sp_done, 1)
                nc.tensor.transpose(PS[:, 7, 256:320], Ps[:, 0:P], ident[0:64, 0:64])
                nc.tensor.transpose(PS[0:NS, 7, 320:384], Dm[:, :], ident[0:64, 0:64]).then_inc(spt_done, 1)
            if i == 6:
                pe.wait_ge(sptc_done, 1)
                pe.wait_ge(vc_in, 16)
                MM(PS[:, 7, 384:448], vS[:, :], Dt[:, :], start=True, stop=False)
                for b in range(NS):
                    last = MM(PS[:, 7, 384 + 8 * b:392 + 8 * b], Vc[:, b, :], PTs[:, 8 * b:8 * b + 8],
                              start=False, stop=b == NS - 1)
                last.then_inc(spv_done, 1)
            if i == UNITS + 1:
                pe.wait_ge(w_lo, C_G + 1)
                pe.wait_ge(u_ev, 11)
                piece(0, 0, 0)
            if 2 <= i:
                u, b = i - 2, (i - 2) // 2
                pe.wait_ge(pt_lo, u + 1)
                if u:
                    pe.wait_ge(o_ev, u)
                else:
                    pe.wait_ge(vt_lo, 2)
                kts = (1,) if b == 0 else (0, 1)
                for kt in kts:
                    last = mm3(PS[:, 6, :], Vh[:, b - 1 + kt, :], Vl[:, b - 1 + kt, :], PTh[:, kt, :], PTl[:, kt, :],
                               kt == kts[0], kt == 1)
                last.then_inc(pv_done, 1)
        pe.wait_ge(u_ev, 12)
        pe.wait_ge(masked, UNITS)
        piece(1, 0, 1)
        piece(2, 0, 2).then_inc(w_used, 1)
        pe.wait_ge(ws_lo, 1)
        pe.wait_ge(o_ev, UNITS)
        pe.wait_ge(so_lo, 1)
        for u in range(2 * NB):
            hp, b, bank = u // NB, VN_ORDER[u % NB], 4 + u % 4
            pe.wait_ge(vn_lo, u % NB + 1)
            if u >= 4:
                pe.wait_ge(sp_ev, u - 3)
            for r in range(2):
                a = 2 * hp + r
                last = mm3(PS[:, bank, 256 * r:256 * r + 256], vnh[:, b, blk(a)], vnl[:, b, blk(a)],
                           wsh[:, 2 * a:2 * a + 2, :].rearrange("p h t -> p (h t)"),
                           wsl[:, 2 * a:2 * a + 2, :].rearrange("p h t -> p (h t)"), True, True)
            last.then_inc(sp_mm, 1)

        def gate_mm(q):
            pe.wait_ge(w_lo, C_G + 1 + 2 * q)
            pe.wait_ge(g_ev, q)
            tile(0, 0, Hh, Hl).then_inc(w_used, 1)

        def proj_mm(q, rh, rl):
            pe.wait_ge(w_lo, C_G + 2 + 2 * q)
            tile(1, 1, rh, rl, n=4).then_inc(w_used, 1)

        pe.wait_ge(sp_ev, 2 * NB)
        proj_mm(0, QYh, QYl)
        with pe.Fori(1, KT) as q:
            gate_mm(q)
            pe.wait_ge(p_ev, q)
            proj_mm(q, QYh, QYl)
        pe.wait_ge(ya_lo, 4)
        with pe.Fori(KT, 2 * KT) as q:
            gate_mm(q)
            pe.wait_ge(p_ev, q)
            proj_mm(q, YAh, YAl)
        def wo_rows(w, k0, k1):
            m, p = w % KT, w // KT
            for k in range(k0, k1):
                last = mm3(PS[:, w % 6, 0:PC], WOh[:, m, blk(k)], WOl[:, m, blk(k)], MSh[p % 2][:, k, :],
                           MSl[p % 2][:, k, :], k == 0, k == KT - 1)
            return last

        for w in range(3):
            pe.wait_ge(w_lo, C_WO + w + 1)
            if w == 0:
                pe.wait_ge(mg_lo, 1)
                pe.wait_ge(g_ev, 2 * KT)
            wo_rows(w, 0, KT - 1)
        for w in range(NPC * KT):
            m, p = w % KT, w // KT
            if w >= 6:
                pe.wait_ge(x1_ev, w - 5)
            if 3 <= w < KT:
                pe.wait_ge(w_lo, C_WO + m + 1)
            if m == 0:
                pe.wait_ge(mg_lo, p + 2)
            last = wo_rows(w, KT - 1 if w < 3 else 0, KT)
            if w < NPC * KT - 1:
                last.then_inc(wo_done, 1)
            else:
                last.then_inc(w_used, KT)
            if w in (17, 23):
                q = (w - 17) // 6
                pe.wait_ge(ss_done, 7 * (q + 2))
                MM(PS[:, 6 + q, 0:PC], ones[:, :], rstd[:, pcs(q)], start=True, stop=True).then_inc(stat_done, 1)

        for j in range(8):
            pe.wait_ge(w_lo, C_UP0 + j + 1)
            if j >= 2:
                pe.wait_ge(f_ev, j - 1)
            else:
                pe.wait_ge(x1_ev, NPC * KT)
            for k in range(KT):
                if j == 0:
                    pe.wait_ge(h_lo, KT + k + 1)
                wh, wl = block_of(j % 2, k)
                for p in range(NPC):
                    last = mm3(PS[:, 3 * (j % 2) + p, 0:PC], wh, wl, Hh[:, k, pcs(p)], Hl[:, k, pcs(p)],
                               k == 0, k == KT - 1)
                if (j, k) != (0, 5):
                    continue
                pe.wait_ge(ss_done, 7 * (NPC + 1))
                pe.wait_ge(v_done, NPC + 1)
                MM(PS[:, 6, 0:PC], ones[:, :], rstd[:, pcs(2)], start=True, stop=True).then_inc(stat_done, 1)
            last.then_inc(w_used, 1)
        with pe.Fori(0, NG - 1) as g:
            n = 0
            for j in range(12):
                pe.wait_ge(w_lo, C_LOOP + 12 * g + j + 1)
                if 2 <= j < 6:
                    if j == 2:
                        pe.wait_ge(g_lo, 4 * g + 4)
                    for h in range(2):
                        pe.wait_ge(f_ev, 16 * g + 7 + n)
                        tile(h, j % 2, Gh, Gl, first=GP * h, n=GP).then_inc(w_used if h else dn_half, 1)
                        n += 1
                else:
                    pe.wait_ge(f_ev, 16 * g + 7 + n)
                    tile(j % 2, j % 2, Hh, Hl).then_inc(w_used, 1)
                    n += 1
        assert n == 16
        def last_block(m, k):
            if m < 4:
                return block_of(m // 2, (m % 2) * GP + k)
            i = ((m % 2) * GP + k) * P
            return WDh[:, m // 2 - 2, i:i + P], WDl[:, m // 2 - 2, i:i + P]

        def last_tile(m, k, p):
            wh, wl = last_block(m, k)
            return mm3(PS[:, m, 0:lw(p)], wh, wl, Gh[:, k, lcs(p)], Gl[:, k, lcs(p)], k == 0, k == GP - 1)

        def last_stat(p, bank):
            pe.wait_ge(sum_done, 7 * (p + 1))
            MM(PS[:, bank, 0:lw(p)], ones[:, :], rstd[:, lcs(p)], start=True, stop=True).then_inc(stat_done, 1)

        pe.wait_ge(f_ev, 16 * (NG - 1) + 8)
        pe.wait_ge(g_lo, NPAIR - 1)
        pe.wait_ge(wd_lo, 2)
        for c in (2, 3, 0, 1):
            if c < 2:
                pe.wait_ge(w_lo, C_LAST + c + 1)
            for k in range(GP - 1):
                for m in (2 * c, 2 * c + 1):
                    last_tile(m, k, 0)
        pe.wait_ge(g_lo, NPAIR)
        for m in range(KT):
            last_tile(m, GP - 1, 0).then_inc(last_mm, 1)
        for p in (1, 2):
            for i, m in enumerate(LAST_ORDER[p]):
                pe.wait_ge(y_ev, KT * (p - 1) + LAST_ORDER[p - 1].index(m) + 1)
                if (p, m) == (2, 0):
                    pe.wait_ge(v_done, 2 * NPC + 2)
                for k in range(GP):
                    last = last_tile(m, k, p)
                last.then_inc(last_mm, 1)
                if i == 2:
                    pe.wait_ge(y_ev, KT + 1)
                    if p == 2:
                        pe.wait_ge(v_done, 2 * NPC + 1)
                    last_stat(p - 1, 0)
        pe.wait_ge(y_ev, 2 * KT + 1)
        last_stat(2, 1)

    block_cm.__exit__(None, None, None)


def tiles_of(w, cols=None):
    K, N = w.shape
    return np.ascontiguousarray(w.reshape(K // P, P, N // P, P).transpose(2, 1, 0, 3).reshape(N // P, P, K))


def kernel(**inputs):
    import concourse.bacc as bacc
    from concourse.bass_utils import run_bass_kernel_spmd

    a = {k: np.asarray(v) for k, v in inputs.items()}
    f = np.float32
    x = np.concatenate([a["x_prompt"][0], a["x_sample"][:, 0]], axis=0)
    w_in = a["w_in"][0]
    o_q, o_k = 2 * GMW, 2 * GMW + HEADS * HD
    o_v = o_k + KVH * HD
    o_ga = o_v + KVH * HD
    o_gb = o_ga + D
    head_order = [h for r in range(GRP) for h in (r, GRP + r)]
    rows_b = np.concatenate([np.arange(h * HD, (h + 1) * HD) for h in head_order])
    gm = w_in[:, GMW:2 * GMW].reshape(4, 2, P, GMW).transpose(0, 2, 1, 3).reshape(4, P, CH)
    w_main = np.concatenate([gm, tiles_of(w_in[:, o_k:o_v]), tiles_of(w_in[:, o_q:o_k][:, rows_b]),
                             tiles_of(w_in[:, o_v:o_ga]), tiles_of(w_in[:, 0:GMW]),
                             tiles_of(w_in[:, o_gb:]), tiles_of(w_in[:, o_ga:o_gb]),
                             tiles_of(a["w_o"][0])], axis=0)
    w_half = np.concatenate([tiles_of(a["w_pb"][0][rows_b]), tiles_of(a["w_pa"][0])], axis=0)
    up = tiles_of(a["w_up"][0])
    up = np.stack([up[:NPAIR], up[NPAIR:]], axis=1).reshape(NG, 2 * GP, P, CH)
    dn = a["w_down"][0].reshape(NG, GP, P, KT // 2, 2, P).transpose(0, 3, 2, 4, 1, 5).reshape(NG, 4, P, CH)
    parts = [up[0]]
    for g in range(1, NG):
        parts += [up[g][0:2], dn[g - 1], up[g][2:]]
    w_ffn = np.concatenate(parts + [dn[NG - 1]], axis=0)
    cols = np.stack([a["g_mix"][0], a["g_ffn"][0], a["g_final"]]).reshape(3, KT, P).transpose(2, 0, 1)

    half = HD // 2
    inv = (10000.0 ** (-np.arange(half) / half)).astype(f)
    pos = np.concatenate([np.arange(SEQ), np.full(NS, 8192)]).astype(f)
    ang = (pos[:, None] * inv[None, :]).astype(f)
    cos = np.tile(np.cos(ang).astype(f).T, (4, 1))
    sin = np.sin(ang).astype(f).T
    rope = np.stack([cos, np.tile(np.concatenate([-sin, sin]), (2, 1))], axis=1)
    i = np.arange(P)
    mask = np.zeros((P, 2 * P), f)
    mask[:, :P][i[None, :] < i[:, None]] = MASKED
    mask[:, P:][i[None, :] > i[:, None]] = MASKED
    sinks = a["sinks"][0]
    same = np.repeat(np.eye(NS, dtype=f), HEADS, axis=0)
    by_tile = lambda v: v.reshape(v.shape[:-1] + (2, NPAIR, P))
    par = np.concatenate([a["conv_w"][0], a["conv_b"]], axis=0)
    par = by_tile(par).transpose(3, 2, 1, 0).reshape(P, 2 * NPAIR, 4)
    state = by_tile(a["state_ffn_conv"][0]).transpose(4, 3, 2, 0, 1).reshape(P, 2 * NPAIR, NS, 2)
    w_s = a["w_s"][0]

    ins = {
        "x_t": x.T.reshape(KT, P, T).transpose(1, 0, 2),
        "w_main": w_main, "w_half": w_half, "w_ffn": w_ffn,
        "cols": cols, "rope": rope, "eye": np.eye(P, dtype=f),
        "lnv": np.broadcast_to(np.stack([a["ln_v_g"][0], a["ln_v_b"][0]])[None], (P, 2, GMW)),
        "ws_t": w_s.transpose(2, 0, 1),
        "bs_t": np.repeat(a["b_s"][0], 64, axis=0).reshape(4, P, P).transpose(1, 0, 2),
        "ws_first": np.where(np.eye(NS, dtype=bool)[:, None, :], w_s[:, 0, 0][None, :, None], f(0)),
        "mask": mask,
        "sink_rows": np.broadcast_to(np.stack([sinks, sinks])[None], (P, 2, HEADS)),
        "sink_cols": np.tile(np.stack([sinks, sinks], axis=1), (NS, 1)),
        "same_sample": same,
        "k_cache": a["cache_swa_k"][0].transpose(2, 3, 0, 1).reshape(P, NS, P),
        "v_cache": a["cache_swa_v"][0].transpose(1, 0, 2, 3).reshape(P, NS, P),
        "conv_par": par, "conv_state": state,
    }
    outs = {
        "y": (P, KT, T), "kv_prompt": (2, P, P), "gm_prompt": (P, GMW), "gm_sample": (NS, GMW),
        "k_sample": (P, NS, P), "v_sample": (P, NS, P), "v_new": (NS, P), "conv_new": (P, 2 * NPAIR, 2 + 2 * NS),
    }
    nc = bacc.Bacc("TRN2", target_bir_lowering=False, num_devices=1)
    arrays, aps = {}, {}
    for name, v in ins.items():
        arrays[f"in_{name}"] = np.ascontiguousarray(v)
        aps[name] = nc.dram_tensor(f"in_{name}", v.shape, F32, kind="ExternalInput").ap()
    for name, shape in outs.items():
        aps[name] = nc.dram_tensor(f"out_{name}", shape, F32, kind="ExternalOutput").ap()
    build(nc, **aps)
    r = run_bass_kernel_spmd(nc, [arrays], core_ids=[0]).results[0]
    o = {name: np.asarray(r[f"out_{name}"]).reshape(shape) for name, shape in outs.items()}

    yt = o["y"].transpose(2, 1, 0).reshape(T, D)
    heads = lambda v: v.T.reshape(1, 1, P, KVH, HD)
    k_s = o["k_sample"].transpose(1, 2, 0).reshape(1, NS, P, KVH, HD)
    v_s = np.concatenate([o["v_sample"][1:].transpose(1, 0, 2), o["v_new"][:, None, :]], axis=1)
    conv = o["conv_new"].reshape(P, NPAIR, 2, 2 + 2 * NS).transpose(3, 2, 1, 0).reshape(2 + 2 * NS, 2 * DFF)
    return (yt[None, :SEQ], yt[SEQ:, None], heads(o["kv_prompt"][0]), heads(o["kv_prompt"][1]),
            o["gm_prompt"].reshape(1, 1, P, 8, 64), conv[None, None, 0:2],
            k_s, v_s.reshape(1, NS, P, KVH, HD), o["gm_sample"].reshape(1, NS, 1, 8, 64),
            conv[2:].reshape(1, NS, 2, 2 * DFF))
```

```python
import numpy as np
import concourse.bass as bass
from concourse import mybir

F32 = mybir.dt.float32
F32R = mybir.dt.float32r
ALU = mybir.AluOpType
ACT = mybir.ActivationFunctionType
AX = mybir.AxisListType

P = 128
D = 1024
SEQ = 1024
NS = 8
T = SEQ + NS
NPC = 3
PC = T // NPC
KT = D // P
GMW = 512
NB = SEQ // P
HEADS, KVH, HD = 8, 2, 64
GRP = HEADS // KVH
SCALE = HD ** -0.5
DFF = 3 * D
EPS = 1e-6
NPAIR = DFF // P
GP = 4
NG = NPAIR // GP
ZW = 2 + SEQ + 3 * NS
CW = ZW - 2
CH = 8 * P
MASKED = -1.0e30
WARM_UP = 20
LAST_PC = (0, 384, 768, T)
LW = 384
X0 = 4 * P

C_U = 10
C_G = 14
C_WO = 46
C_UP0 = 54
C_LOOP = 62
C_LAST = 62 + 12 * (NG - 1)


def build(nc, x_t, w_main, w_half, w_ffn, cols, rope, eye, lnv, ws_t, bs_t, ws_first, mask, sink_rows, sink_cols,
          same_sample, k_cache, v_cache, conv_par, conv_state,
          y, kv_prompt, gm_prompt, gm_sample, k_sample, v_sample, v_new, conv_new):
    base = (nc.sbuf_base + 31) // 32 * 32
    arena_bytes = 212800
    nc.alloc_sbuf_tensor("arena", [P, arena_bytes // 4], F32)
    row = T * 4
    R_H = base
    R_QY = R_H + 16 * row
    R_KV = R_QY + 8 * row
    R_M = R_KV + 4 * row
    R_YA = R_M + 8 * row
    R_RSTD = R_YA + 8 * row
    R_RAW = R_RSTD + row
    R_HL = R_RAW + 2 * CH * 4
    R_SMALL = R_HL + 4 * CH * 4
    small_at = [R_SMALL]

    def at(name, shape, dt, offset):
        return nc.alloc_sbuf_tensor_at(name, shape, dt, offset=offset)

    def small(name, shape, dt=F32):
        words = 1
        for s in shape[1:]:
            words *= s
        t = at(name, shape, dt, small_at[0])
        small_at[0] += (words * 4 + 31) // 32 * 32
        assert small_at[0] <= base + arena_bytes, small_at[0] - base - arena_bytes
        return t

    Hh = at("Hh", [P, KT, T], F32R, R_H)
    Hl = at("Hl", [P, KT, T], F32R, R_H + 8 * row)
    WOh = at("WOh", [P, KT, CH], F32R, R_H)
    WOl = at("WOl", [P, KT, CH], F32R, R_H + 8 * CH * 4)
    QYh = at("QYh", [P, GRP, T], F32R, R_QY)
    QYl = at("QYl", [P, GRP, T], F32R, R_QY + 4 * row)
    gv = at("gv", [P, NB + 1, GMW], F32, R_QY)
    lnvb = at("lnvb", [P, 2, GMW], F32, R_QY + 18432)
    bst = at("bst", [P, NB + 1, 6], F32, R_QY + 30784)
    wdiag = at("wdiag", [NS, HEADS, NS], F32, R_QY + 31008)
    sqx = at("sqx", [P, 2, T], F32, R_QY + 22528)
    kh = at("kh", [P, T], F32R, R_KV)
    kl = at("kl", [P, T], F32R, R_KV + row)
    Vh = at("Vh", [P, NB, P], F32R, R_KV + 2 * row)
    Vl = at("Vl", [P, NB, P], F32R, R_KV + 2 * row + NB * P * 4)
    ssq = at("ssq", [P, T], F32, R_KV)
    rdiag = at("rdiag", [P, NB + 1, P], F32, R_KV + row)
    bsb = at("bsb", [P, 4, P], F32, R_KV)
    wsh = at("wsh", [P, HEADS, P], F32R, R_KV + row)
    wsl = at("wsl", [P, HEADS, P], F32R, R_KV + row + 4096)
    sig = at("sig", [P, T], F32, R_KV + row + 8192)
    x_raw = at("x_raw", [P, KT, T], F32, R_M)
    vnf = at("vnf", [P, NB, GMW], F32, R_M)
    vnl = at("vnl", [P, NB, GMW], F32R, R_M)
    vnh = at("vnh", [P, NB, GMW], F32R, R_M + NB * GMW * 4)
    band = at("band", [P, 2 * P], F32, R_M + NB * GMW * 4)
    Qz = at("Qz", [P, NS, 64], F32, R_M + NB * GMW * 4 + 1024)
    R_SA = R_M + NB * GMW * 4 + 3072
    Kc = at("Kc", [P, NS, P + 1], F32, R_SA)
    Vc = at("Vc", [P, NS, P], F32, R_SA + 4128)
    Ps = at("Ps", [64, P + 1], F32, R_SA + 8224)
    PTs = at("PTs", [P, 64], F32, R_SA + 8768)
    Dm = at("Dm", [64, NS], F32, R_SA + 9024)
    ws_raw = at("ws_raw", [P, HEADS, P], F32, R_SA)
    Dt = at("Dt", [NS, 64], F32, R_M + 2 * NB * GMW * 4)
    MG = at("MG", [P, KT, T], F32, R_M)
    Wgh = at("Wgh", [P, KT, GMW], F32R, R_YA)
    Wgl = at("Wgl", [P, KT, GMW], F32R, R_YA + KT * GMW * 4)
    YAh = at("YAh", [P, 4, T], F32R, R_YA)
    YAl = at("YAl", [P, 4, T], F32R, R_YA + 4 * row)
    YAt = at("YAt", [P, 4, T], F32, R_YA)
    U = at("U", [P, 4, T], F32, R_YA + 4 * row)
    rope_sb = at("rope_sb", [P, 2, T], F32, R_YA)
    zt = at("zt", [P, 2, T], F32, R_YA + 2 * row)
    sw = at("sw", [P, 2, T], F32, R_YA + 6 * row)
    Pb = [at(f"Pb{i}", [P, GRP, 2 * P], F32, a) for i, a in enumerate(
        (R_YA, R_YA + 4096, R_M + 2 * NB * GMW * 4 - 4096))]
    PTh = at("PTh", [P, 2, GRP * P], F32R, R_YA + 8192)
    PTl = at("PTl", [P, 2, GRP * P], F32R, R_YA + 12288)
    X1 = at("X1", [P, KT, T], F32, R_YA)
    rstd = at("rstd", [P, T], F32, R_RSTD)
    raw = at("raw", [P, 2, CH], F32, R_RAW)
    Wh = at("Wh", [P, 2, CH], F32R, R_HL)
    Wl = at("Wl", [P, 2, CH], F32R, R_HL + 2 * CH * 4)
    MSh = [at(f"MSh{i}", [P, KT, PC], F32R, R_QY + 2 * i * KT * PC * 4) for i in range(2)]
    MSl = [at(f"MSl{i}", [P, KT, PC], F32R, (R_QY + KT * PC * 4, R_KV)[i]) for i in range(2)]
    xr = at("xr", [P, 3, PC], F32, R_KV + row + 8192)
    Gh = at("Gh", [P, GP, T], F32R, R_QY)
    Gl = at("Gl", [P, GP, T], F32R, R_QY + 4 * row)
    R_Z = R_QY + 8 * row
    zb = [at(f"zb{i}", [P, ZW], F32, R_Z + i * 4224) for i in range(2)]
    ca = at("ca", [P, CW], F32, R_Z + 2 * 4224)
    cb = at("cb", [P, CW], F32, R_Z + 3 * 4224)
    R_WD = R_Z + 4 * 4224
    WDh = at("WDh", [P, 2, CH], F32R, R_WD)
    WDl = at("WDl", [P, 2, CH], F32R, R_WD + 2 * CH * 4)
    WDr = at("WDr", [P, 2, CH], F32, R_WD + 2 * CH * 4)
    R_PAR = R_WD + 4 * CH * 4
    cpar = at("cpar", [P, 2 * NPAIR, 4], F32, R_PAR)
    cst = at("cst", [P, 2 * NPAIR, NS, 2], F32, R_PAR + 768)
    cnew = at("cnew", [P, 2 * NPAIR, 2 + 2 * NS], F32, R_PAR + 768 + 3072)
    sqe = at("sqe", [P, 2, LW], F32, R_PAR + 768 + 3072 + 3456)
    assert R_PAR + 768 + 3072 + 3456 + 2 * LW * 4 <= R_YA
    dg = at("dg", [P, LW], F32, R_Z)
    nsm = at("nsm", [P, T], F32, R_QY)
    ntm = at("ntm", [P, T], F32, R_QY + row)
    colsb = small("colsb", [P, 3, KT])
    ident = small("ident", [P, P])
    ones = small("ones", [P, P])
    vS = small("vS", [NS, P])
    mixS = small("mixS", [P, 4, NS])
    rtok = small("rtok", [P, NB + 1])
    mv = small("mv", [P, NB + 1, 2])
    lnr = small("lnr", [P, 3, NB + 1])
    kS = small("kS", [P, NS])
    snk = small("snk", [P, 2, HEADS])
    snS = small("snS", [64, 2])
    mx = small("mx", [P, 2, GRP])
    nm = small("nm", [P, 2, GRP])
    sm = small("sm", [P, 2, GRP])
    es = small("es", [P, 2, GRP])
    ri = small("ri", [P, 2, GRP])
    st = small("st", [64, 6])
    bmask = small("bmask", [64, NS])

    PS = nc.alloc_psum_tensor("PS", [P, 8, 512], F32)
    MGv = MG[:, :, :].rearrange("p k (c t) -> p (k c) t", c=NPC)
    X1v = X1[:, :, :].rearrange("p k (c t) -> p (k c) t", c=NPC)
    rstd3 = rstd[:, :].rearrange("p (c t) -> p c t", c=NPC)

    def thirds(ap):
        return ap.rearrange("p (c t) -> p c t", c=NPC)

    def pcs(p):
        return slice(p * PC, (p + 1) * PC)

    def blk(b):
        return slice(b * P, (b + 1) * P)

    def sem(name):
        return nc.alloc_semaphore(name)

    raw_full = [sem("raw_full0"), sem("raw_full1")]
    w_hi, w_lo, w_used = sem("w_hi"), sem("w_lo"), sem("w_used")
    x_in = [sem(f"x_in{k}") for k in range(KT)]
    x0_in, w0_in, h0_hi, h0_lo, w0_hi, w0_lo = (sem("x0_in"), sem("w0_in"), sem("h0_hi"), sem("h0_lo"), sem("w0_hi"),
                                                sem("w0_lo"))
    cols_in, small_in, rope_in, band_in = sem("cols_in"), sem("small_in"), sem("rope_in"), sem("band_in")
    wd_in, wd_hi, wd_lo = sem("wd_in"), sem("wd_hi"), sem("wd_lo")
    kc_in, vc_in, ws_in, bs_in, par_in = sem("kc_in"), sem("vc_in"), sem("ws_in"), sem("bs_in"), sem("par_in")
    xr_in = [sem(f"xr_in{k}") for k in range(3)]
    k_out, v_out, gm_out, s_out, y_out = sem("k_out"), sem("v_out"), sem("gm_out"), sem("s_out"), sem("y_out")
    ones_set, h_hi, h_lo, sq_done, ss_done = sem("ones_set"), sem("h_hi"), sem("h_lo"), sem("sq_done"), sem("ss_done")
    stat_done, v_done, root_done, rstd_done = sem("stat_done"), sem("v_done"), sem("root_done"), sem("rstd_done")
    tok_done, gv_done = sem("tok_done"), sem("gv_done")
    tsum_done, tmean_done, rtok_done, rdiag_done, bcast_done = (sem("tsum_done"), sem("tmean_done"), sem("rtok_done"),
                                                                sem("rdiag_done"), sem("bcast_done"))
    lnv_done, lns_done, ln_done, mixp_done, mix_done = (sem("lnv_done"), sem("lns_done"), sem("ln_done"),
                                                        sem("mixp_done"), sem("mix_done"))
    ln_sub, ln_mul = sem("ln_sub"), sem("ln_mul")
    z_ev, swapped, sw_sin, rot_done, rot_hi, rot_lo = (sem("z_ev"), sem("swapped"), sem("sw_sin"), sem("rot_done"),
                                                       sem("rot_hi"), sem("rot_lo"))
    vt_done, vt_hi, vt_lo, vs_done, qz_zero = sem("vt_done"), sem("vt_hi"), sem("vt_lo"), sem("vs_done"), sem("qz_zero")
    s_done, masked, nm_done, esin_done, exp_done, es_done, ri_done, pn_done = (
        sem("s_done"), sem("masked"), sem("nm_done"), sem("esin_done"), sem("exp_done"), sem("es_done"),
        sem("ri_done"), sem("pn_done"))
    pt_done, pt_hi, pt_lo, pv_done, o_hi, o_ev, u_done, u_ev = (
        sem("pt_done"), sem("pt_hi"), sem("pt_lo"), sem("pv_done"), sem("o_hi"), sem("o_ev"), sem("u_done"), sem("u_ev"))
    kn_done, ss_sc, sn_done, sx_done, sp_done, spt_done, sptc_done, spv_done, so_hi, so_lo = (
        sem("kn_done"), sem("ss_sc"), sem("sn_done"), sem("sx_done"), sem("sp_done"), sem("spt_done"),
        sem("sptc_done"), sem("spv_done"), sem("so_hi"), sem("so_lo"))
    tri_done, ws_hi, ws_lo, vn_hi, vn_lo, ug_done = (sem("tri_done"), sem("ws_hi"), sem("ws_lo"), sem("vn_hi"),
                                                     sem("vn_lo"), sem("ug_done"))
    sp_mm, sp_ev, ya_done, ya_hi, ya_lo = sem("sp_mm"), sem("sp_ev"), sem("ya_done"), sem("ya_hi"), sem("ya_lo")
    g_ev, th_done, p_ev, mg_hi, mg_lo, wo_done, x1_ev = (sem("g_ev"), sem("th_done"), sem("p_ev"), sem("mg_hi"),
                                                         sem("mg_lo"), sem("wo_done"), sem("x1_ev"))
    f_ev, z_rdy, c0_done, conv_done, cnew_done, gelu_done, g_done, g_hi, g_lo, dn_half = (
        sem("f_ev"), sem("z_rdy"), sem("c0_done"), sem("conv_done"), sem("cnew_done"), sem("gelu_done"),
        sem("g_done"), sem("g_hi"), sem("g_lo"), sem("dn_half"))
    dg_done, bc_done, bc_copied = sem("dg_done"), sem("bc_done"), sem("bc_copied")
    sum_done_p = sem("sum_done_p")
    last_mm, y_ev, sum_done, yg_done, y_done, y_done_p = (sem("last_mm"), sem("y_ev"), sem("sum_done"), sem("yg_done"),
                                                          sem("y_done"), sem("y_done_p"))
    dve_step = sem("dve_step")

    class Link:

        def __init__(self, eng, s):
            self.eng, self.s, self.n, self.off = eng, s, 0, 0

        def __call__(self, ins):
            self.n += 1
            ins.then_inc(self.s, 1)
            self.eng.wait_ge(self.s, self.off + self.n)

    def mm3(out, ah, al, bh, bl, first, last):
        nc.tensor.matmul(out, ah, bh, start=first, stop=False)
        nc.tensor.matmul(out, ah, bl, start=False, stop=False)
        return nc.tensor.matmul(out, al, bh, start=False, stop=last)

    F = lambda ap: ap.bitcast(F32)

    def load(sp, half, j, src, n=CH, wait=True):
        if wait:
            sp.wait_ge(w_lo, 2 * half + j - 1)
        sp.dma_start(raw[:, j, 0:n], src).then_inc(raw_full[j], 16)

    def split_hi(act, half, j, dst=None, n=CH, used=None):
        act.wait_ge(raw_full[j], 16 * half + 16)
        if used is None:
            used = 2 * half + j - 1
        if used is not False:
            act.wait_ge(w_used, used)
        nc.scalar.activation(Wh[:, j, 0:n] if dst is None else dst, raw[:, j, 0:n], ACT.Copy).then_inc(w_hi, 1)

    def split_lo(pool, half, j, dst=None, n=CH):
        h, l = (Wh[:, j, 0:n], Wl[:, j, 0:n]) if dst is None else dst
        pool.wait_ge(w_hi, 2 * half + j + 1)
        nc.gpsimd.tensor_tensor(l, raw[:, j, 0:n], F(h), ALU.subtract).then_inc(w_lo, 1)

    def gmv_dst(c):
        return (Wgh[:, 2 * c:2 * c + 2, :].rearrange("p k n -> p (k n)"),
                Wgl[:, 2 * c:2 * c + 2, :].rearrange("p k n -> p (k n)"))

    UNITS = 2 * NB
    QUARTERS = [4, 4] + [3] * 16
    FILL = [[4 + sum(QUARTERS[:i]) + n for n in range(QUARTERS[i])] for i in range(UNITS + 2)]
    U_END = [[i for i in range(UNITS + 2) if 4 * NPC * (t + 1) - 1 in FILL[i]][0] for t in range(4)]

    VN_ORDER = [0, 4, 5, 6, 7, 1, 2, 3]

    def filled(i):
        return [n // 4 for n in FILL[i] if n % 4 == 3 and n < 48]

    def halves(u):
        return u + 1 if u < 2 else 2 * u

    LAST_ORDER = [list(range(KT)), list(range(KT)), [1, 2, 3, 4, 5, 6, 7, 0]]
    LAST_ROOT = {(1, 3): 0, (2, 3): 1, (2, 7): 2}
    LAST_BCAST = {(1, 6): 0, (2, 4): 1}
    LAST_BANK = (0, 0, 2)
    YP = 6

    def last_out(p, m):
        return 1 if (p, m) == (2, 0) else m

    MID = ((slice(0, 2 * PC), 2), (slice(2 * PC, T), 3))

    def lcs(p):
        return slice(LAST_PC[p], LAST_PC[p + 1])

    def lw(p):
        return LAST_PC[p + 1] - LAST_PC[p]

    def lb(p):
        return (lw(p) + P - 1) // P

    mx2, nm2, sm2, es2 = (t[:, :, :].rearrange("p a b -> p (a b)") for t in (mx, nm, sm, es))

    block_cm = nc.Block()
    block = block_cm.__enter__()

    @block.sync
    def _(sp):
        def x_load(k):
            sp.dma_start(x_raw[:, k, :], x_t[:, k, :]).then_inc(x_in[k], 16)

        sp.dma_start(raw[:, 0, 0:GMW], w_main[0, :, 0:GMW]).then_inc(w0_in, 16)
        sp.dma_start(x_raw[:, 0, 0:X0], x_t[:, 0, 0:X0]).then_inc(x0_in, 16)
        sp.dma_start(x_raw[:, 0, X0:T], x_t[:, 0, X0:T]).then_inc(x_in[0], 16)
        sp.dma_start(raw[:, 0, GMW:CH], w_main[0, :, GMW:CH]).then_inc(raw_full[0], 16)
        x_load(1)
        load(sp, 0, 1, w_main[1], wait=False)
        for k in range(2, KT):
            x_load(k)
            if k in (3, 5):
                load(sp, 1, (k - 3) // 2, w_main[(k + 1) // 2])
        for dst, src in ((ident, eye), (lnvb, lnv), (wdiag, ws_first), (snk, sink_rows), (snS, sink_cols),
                         (bmask, same_sample)):
            sp.dma_start(dst.ap(), src).then_inc(small_in, 16)
        for c in (4, 5):
            load(sp, c // 2, c % 2, w_main[c])
        sp.wait_ge(w_used, 4)
        sp.dma_start(rope_sb[:, :, :], rope).then_inc(rope_in, 16)
        load(sp, 3, 0, w_main[6])
        load(sp, 3, 1, w_main[7])
        sp.wait_ge(gv_done, NB + 1)
        sp.dma_start(band[:, :], mask).then_inc(band_in, 16)
        sp.dma_start(Kc[:, :, 0:P], k_cache).then_inc(kc_in, 16)
        sp.dma_start(Vc[:, :, :], v_cache).then_inc(vc_in, 16)
        sp.wait_ge(ln_done, NB + 1)
        sp.dma_start(gm_prompt, vnf[:, NB - 1, :]).then_inc(gm_out, 16)
        sp.dma_start(gm_sample, gv[0:NS, NB, :]).then_inc(gm_out, 16)
        sp.wait_ge(vc_in, 16)
        sp.dma_start(v_sample, Vc[:, :, :]).then_inc(s_out, 16)
        sp.wait_ge(rot_done, 1)
        sp.dma_start(kv_prompt[0], zt[:, 0, SEQ - P:SEQ]).then_inc(k_out, 16)
        load(sp, 4, 0, w_main[8])
        sp.wait_ge(kn_done, 1)
        sp.dma_start(k_sample, Kc[:, :, 1:P + 1]).then_inc(s_out, 16)
        for c in (9, 10, 11):
            load(sp, c // 2, c % 2, w_main[c])
        sp.wait_ge(z_ev, 6)
        sp.dma_start(kv_prompt[1], zt[:, 1, SEQ - P:SEQ]).then_inc(v_out, 16)
        sp.wait_ge(vs_done, 1)
        sp.dma_start(v_new, vS[:, :]).then_inc(s_out, 16)
        load(sp, 6, 0, w_main[12])
        sp.wait_ge(ss_sc, 1)
        sp.wait_ge(s_out, 48)
        sp.dma_start(ws_raw[:, :, :], ws_t).then_inc(ws_in, 16)
        for c in (13, 14):
            load(sp, c // 2, c % 2, w_main[c])
        load(sp, 7, 1, w_half[0], n=CH // 2)
        sp.wait_ge(pv_done, UNITS)
        sp.dma_start(bsb[:, :, :], bs_t).then_inc(bs_in, 16)
        load(sp, 8, 0, w_main[15])
        load(sp, 8, 1, w_half[1], n=CH // 2)
        with sp.Fori(2, 16) as q:
            load(sp, q + 7, 0, w_main[q + 14])
            load(sp, q + 7, 1, w_half[q], n=CH // 2)
        for m in range(4):
            load(sp, 23 + m // 2, m % 2, w_main[30 + m])
        sp.wait_ge(p_ev, 16)
        for w in range(NPC * KT):
            if w >= 3:
                sp.wait_ge(x1_ev, w - 2)
            sp.dma_start(xr[:, w % 3, :], x_t[:, w % KT, pcs(w // KT)]).then_inc(xr_in[w % 3], 16)
            if w + 4 < KT:
                load(sp, 25 + w // 2, w % 2, w_main[34 + w])
            if w == KT - 2:
                load(sp, 27, 0, w_ffn[0])
            if w == KT - 1:
                load(sp, 27, 1, w_ffn[1])
        sp.wait_ge(ss_done, 7 * (NPC + 1))
        for dst, src in ((cpar, conv_par), (cst, conv_state)):
            sp.dma_start(dst.ap(), src).then_inc(par_in, 16)
        for c in range(2, 8):
            load(sp, 27 + c // 2, c % 2, w_ffn[c])
        for c in range(2):
            sp.dma_start(WDr[:, c, :], w_ffn[C_LAST - C_UP0 + 2 + c]).then_inc(wd_in, 16)
        with sp.Fori(0, NG - 1) as g:
            for c in range(12):
                load(sp, 31 + 6 * g + c // 2, c % 2, w_ffn[8 + 12 * g + c])
        for c in range(2):
            load(sp, C_LAST // 2 + c // 2, c % 2, w_ffn[C_LAST - C_UP0 + c])
        sp.wait_ge(cnew_done, 2 * NPAIR)
        sp.dma_start(conv_new, cnew[:, :, :]).then_inc(y_out, 16)
        for p in (0, 1):
            for h in range(2):
                if (p, h) == (1, 1):
                    sp.wait_ge(y_done, KT - YP)
                sp.wait_ge(y_done_p, min(KT * p + 4 * (h + 1), KT + YP))
                rows = slice(4 * h, 4 * h + 4)
                sp.dma_start(y[:, rows, lcs(p)], X1[:, rows, lcs(p)]).then_inc(y_out, 16)
        for m0, m1 in ((0, 4), (4, 6), (6, KT)):
            sp.wait_ge(y_done, KT - YP + m1)
            sp.dma_start(y[:, m0:m1, lcs(2)], X1[:, m0:m1, lcs(2)]).then_inc(y_out, 16)
        sp.wait_ge(gm_out, 32)
        sp.wait_ge(k_out, 16)
        sp.wait_ge(v_out, 16)
        sp.wait_ge(s_out, 48)
        sp.wait_ge(y_out, 16 * (1 + 4 + 3))

    @block.scalar
    def _(act):
        A = nc.scalar.activation
        act.dma_start(colsb[:, :, :], cols).then_inc(cols_in, 16)
        act.wait_ge(ones_set, 1)
        A(mx[:, 0, 0:1], ones[:, 0:1], ACT.Copy)
        act.wait_ge(w0_in, 16)
        A(Wgh[:, 0, :], raw[:, 0, 0:GMW], ACT.Copy).then_inc(w0_hi, 1)
        act.wait_ge(cols_in, 16)
        act.wait_ge(x0_in, 16)
        A(Hh[:, 0, 0:X0], x_raw[:, 0, 0:X0], ACT.Copy, scale=colsb[:, 0, 0:1]).then_inc(h0_hi, 1)
        for k in range(KT):
            act.wait_ge(x_in[k], 16)
            c0 = X0 if k == 0 else 0
            A(Hh[:, k, c0:T], x_raw[:, k, c0:T], ACT.Copy, scale=colsb[:, 0, k:k + 1]).then_inc(h_hi, 1)
            if k == 0:
                act.wait_ge(raw_full[0], 16)
                A(Wgh[:, 1, :], raw[:, 0, GMW:CH], ACT.Copy).then_inc(w_hi, 1)
            elif k in (1, 3, 5):
                c = {1: 1, 3: 2, 5: 3}[k]
                split_hi(act, c // 2, c % 2, gmv_dst(c)[0], used=False)
            if k >= 3:
                act.wait_ge(ss_done, k - 2)
            A(ssq[:, :] if k == 0 else sqx[:, k % 2, :], x_raw[:, k, :], ACT.Square).then_inc(sq_done, 1)
        for c in (4, 5):
            split_hi(act, c // 2, c % 2, used=False)
        act.wait_ge(tmean_done, 1)
        A(lnr[:, 1, :], lnr[:, 0, :], ACT.Sqrt).then_inc(root_done, 1)
        for t in range(NB + 1):
            n, bank = (P, t) if t < NB else (NS, 3)
            if t == 0:
                act.wait_ge(rtok_done, 1)
            if t < NB:
                act.wait_ge(tok_done, t + 1)
            else:
                act.wait_ge(w_used, 4)
            A(gv[0:n, t, :], PS[0:n, bank, :], ACT.Gelu_apprx_tanh, scale=rtok[0:n, t:t + 1]).then_inc(gv_done, 1)
        act.wait_ge(lnv_done, 1)
        A(lnr[:, 1, :], lnr[:, 0, :], ACT.Sqrt).then_inc(lns_done, 1)
        for n in range(6):
            split_hi(act, 3 + n // 2, n % 2)
            if n < 5:
                act.wait_ge(z_ev, n + 1)
                if n >= 2:
                    act.wait_ge(rot_done, n - 1)
                for i in range(4):
                    last = A(sw[32 * i:32 * i + 32, n % 2, :], zt[32 * (i ^ 1):32 * (i ^ 1) + 32, n % 2, :], ACT.Copy)
                last.then_inc(swapped, 1)
                if n == 1:
                    act.wait_ge(mix_done, 2)
                    act.wait_ge(gm_out, 32)
                act.wait_ge(rot_done, n + 1)
                A(kh[:, :] if n == 0 else QYh[:, n - 1, :], zt[:, n % 2, :], ACT.Copy).then_inc(rot_hi, 1)
        for i in range(2):
            act.wait_ge(vt_done, i + 1)
            A(Vh[:, 4 * i:4 * i + 4, :].rearrange("p b c -> p (b c)"), PS[:, 6 + i, :], ACT.Copy).then_inc(vt_hi, 1)

        def vn_round(b):
            A(vnh[:, b, :], vnf[:, b, :], ACT.Copy).then_inc(vn_hi, 1)

        for i in range(UNITS + 2):
            for t in range(4):
                if i == U_END[t] + 1:
                    split_hi(act, (12 + t) // 2, t % 2, n=CH if t < 3 else CH // 2)
            if 2 <= i:
                u = i - 2
                act.wait_ge(pt_done, u + 1)
                if u >= 1:
                    act.wait_ge(pv_done, u)
                else:
                    act.wait_ge(v_out, 16)
                for kt in ((1,) if u < 2 else (0, 1)):
                    last = A(PTh[:, kt, :], PS[:, 4 + kt, :], ACT.Copy)
                last.then_inc(pt_hi, 1)
            if i < UNITS:
                lo = P if i < 2 else 0
                act.wait_ge(nm_done, i + 1)
                for h in range(GRP):
                    last = A(Pb[i % 3][:, h, lo:], Pb[i % 3][:, h, lo:], ACT.Exp, scale=SCALE,
                             bias=nm[:, i % 2, h:h + 1], accum_out=sm[:, i % 2, h:h + 1])
                last.then_inc(exp_done, 1)
                act.wait_ge(esin_done, i + 1)
                A(es[:, i % 2, :], es[:, i % 2, :], ACT.Exp).then_inc(es_done, 1)
            if 2 <= i:
                u, b, g = i - 2, (i - 2) // 2, (i - 2) % 2
                act.wait_ge(pv_done, u + 1)
                A(QYh[64 * g:64 * g + 64, :, blk(b)],
                  PS[64 * g:64 * g + 64, 6, :].rearrange("p (r t) -> p r t", r=GRP), ACT.Copy).then_inc(o_hi, 1)
            if i == 2:
                act.wait_ge(sn_done, 1)
                A(Ps[:, :], PS[0:64, 7, 0:P + 1], ACT.Exp, scale=SCALE, bias=st[:, 1:2], accum_out=st[:, 3:4])
                A(st[:, 4:5], st[:, 2:3], ACT.Exp).then_inc(sx_done, 1)
            if i == 4:
                act.wait_ge(spt_done, 1)
                A(PTs[:, :], PS[:, 7, 256:320], ACT.Copy)
                A(Dt[:, :], PS[0:NS, 7, 320:384], ACT.Copy).then_inc(sptc_done, 1)
            if i == 6:
                act.wait_ge(spv_done, 1)
                for g in range(KVH):
                    last = A(QYh[64 * g:64 * g + 64, :, SEQ:T],
                             PS[64 * g:64 * g + 64, 7, 384:448].rearrange("p (b h) -> p h b", h=HEADS)
                             [:, GRP * g:GRP * g + GRP, :], ACT.Copy)
                last.then_inc(so_hi, 1)
            if i == UNITS:
                act.wait_ge(masked, UNITS)
                act.wait_ge(s_out, 48)
                act.wait_ge(spv_done, 1)
                for b in VN_ORDER[:3]:
                    vn_round(b)
        act.wait_ge(tri_done, 1)
        A(wsh[:, :, :], ws_raw[:, :, :], ACT.Copy).then_inc(ws_hi, 1)
        for b in VN_ORDER[3:]:
            if b == 1:
                act.wait_ge(ws_lo, 1)
            vn_round(b)
        for t in range(4):
            act.wait_ge(u_ev, 3 * t + 3)
            A(U[:, t, :], U[:, t, :], ACT.Gelu_apprx_tanh).then_inc(ug_done, 1)
        act.wait_ge(g_ev, 1)
        A(sig[:, :], sig[:, :], ACT.Tanh, scale=0.5).then_inc(th_done, 1)
        split_hi(act, 8, 0)
        for t in range(4):
            act.wait_ge(ya_done, t + 1)
            A(YAh[:, t, :], U[:, t, :], ACT.Copy).then_inc(ya_hi, 1)
        split_hi(act, 8, 1, n=CH // 2)

        def ffn_in_hi(act, k):
            if k < 6:
                act.wait_ge(wo_done, 2 * KT + k + 2)
            else:
                act.wait_ge(w_used, C_UP0)
            A(Hh[:, k, :], X1[:, k, :], ACT.Copy, scale=colsb[:, 1, k:k + 1]).then_inc(h_hi, 1)

        def gate(q):
            act.wait_ge(g_ev, q + 1)
            A(sig[:, :], sig[:, :], ACT.Tanh, scale=0.5).then_inc(th_done, 1)

        with act.Fori(1, 15) as q:
            split_hi(act, q + 8, 0)
            gate(q)
            split_hi(act, q + 8, 1, n=CH // 2)
        def merged_hi(p, k0, k1):
            A(MSh[p % 2][:, k0:k1, :], MG[:, k0:k1, pcs(p)], ACT.Copy, scale=0.5).then_inc(mg_hi, 1)

        act.wait_ge(p_ev, 15)
        merged_hi(0, 0, KT - 1)
        split_hi(act, 23, 0, WOh[:, 0, :], used=45)
        gate(15)
        split_hi(act, 23, 1, WOh[:, 1, :], used=45)
        split_hi(act, 24, 0, WOh[:, 2, :], used=45)
        act.wait_ge(p_ev, 16)
        merged_hi(0, KT - 1, KT)
        for w in range(NPC * KT):
            m, p = w % KT, w // KT
            if w + 3 < KT:
                split_hi(act, 23 + (w + 3) // 2, (w + 3) % 2, WOh[:, w + 3, :], used=45)
            if w == 4:
                merged_hi(1, 0, KT)
            if w == 9:
                act.wait_ge(wo_done, KT)
                merged_hi(2, 0, KT)
            if w in (10, 12):
                split_hi(act, 27, (w - 10) // 2, used=46)
            act.wait_ge(x1_ev, w + 1)
            A(rstd[:, pcs(p)] if m == 0 else MG[:, m, pcs(p)], X1[:, m, pcs(p)], ACT.Square).then_inc(sq_done, 1)
            if w >= 18:
                ffn_in_hi(act, w - 18)
        for k in (6, 7):
            ffn_in_hi(act, k)
        for c, n in MID:
            act.wait_ge(v_done, n)
            A(nsm[:, c], rstd[:, c], ACT.Sqrt).then_inc(root_done, 1)
        act.wait_ge(par_in, 32)

        def after_a(pair):
            act.wait_ge(z_rdy, 2 * pair + 1)
            act.wait_ge(g_done, pair)
            A(ca[:, :], zb[0][:, 2:ZW], ACT.Identity, scale=cpar[:, bass.ds(2 * pair, 1), 2],
              bias=cpar[:, bass.ds(2 * pair, 1), 3]).then_inc(c0_done, 1)

        def after_b(pair, gated=True):
            act.wait_ge(conv_done, 2 * pair + 1)
            A(ca[:, :], ca[:, :], ACT.Gelu_apprx_tanh).then_inc(gelu_done, 1)
            act.wait_ge(z_rdy, 2 * pair + 2)
            act.wait_ge(g_lo, pair)
            A(cb[:, :], zb[1][:, 2:ZW], ACT.Identity, scale=cpar[:, bass.ds(2 * pair + 1, 1), 2],
              bias=cpar[:, bass.ds(2 * pair + 1, 1), 3]).then_inc(c0_done, 1)
            if gated:
                gate_hi(pair, None)

        def gate_hi(pair, slot):
            slot = gate_slot[0] if slot is None else slot
            act.wait_ge(g_done, pair + 1)
            A(Gh[:, slot, 0:SEQ], cb[:, 0:SEQ], ACT.Copy)
            A(Gh[:, slot, SEQ:T], cb[:, SEQ + 2:CW:3], ACT.Copy).then_inc(g_hi, 1)

        gate_slot = [0]
        for j in range(8):
            split_hi(act, 28 + j // 2, j % 2)
            gate_slot[0] = j // 2
            (after_b if j % 2 else after_a)(j // 2)
        act.wait_ge(wd_in, 32)
        for c in range(2):
            A(WDh[:, c, :], WDr[:, c, :], ACT.Copy).then_inc(wd_hi, 1)
        with act.Fori(0, NG - 1) as g:
            for j in range(12):
                split_hi(act, 32 + 6 * g + j // 2, j % 2)
                if j == 0:
                    after_a(4 * g + 4)
                elif j == 1:
                    after_b(4 * g + 4, gated=False)
                elif j == 5:
                    act.wait_ge(w_used, C_LOOP + 12 * g + 6)
                    gate_hi(4 * g + 4, 0)
                elif j >= 6:
                    gate_slot[0] = (j - 4) // 2
                    (after_b if j % 2 else after_a)(4 * g + 4 + (j - 4) // 2)
        for w in range(NPC * KT):
            p, i = w // KT, w % KT
            m = LAST_ORDER[p][i]
            X = X1[:, m, lcs(p)]
            act.wait_ge(y_ev, w + 1)
            if p and i == 1:
                act.wait_ge(*((sum_done_p, 7) if p == 1 else (sum_done, 7)))
            if i >= 3:
                act.wait_ge(*((sum_done, 7 * (p - 1) + i - 2) if p else (sum_done_p, i - 2)))
            A(rstd[:, lcs(p)] if i == 0 else sqe[:, i % 2, 0:lw(p)], X, ACT.Square).then_inc(sq_done, 1)
            act.wait_ge(sq_done, KT + NPC * KT + w + 1)
            A(X, X, ACT.Copy, scale=colsb[:, 2, m:m + 1]).then_inc(yg_done, 1)
            if (p, i) in LAST_ROOT:
                q = LAST_ROOT[p, i]
                act.wait_ge(v_done, NPC + q + 1)
                A(nm2[:, 0:lb(q)], mx2[:, 0:lb(q)], ACT.Sqrt).then_inc(root_done, 1)
            if (p, i) in LAST_BCAST:
                q = LAST_BCAST[p, i]
                act.wait_ge(bc_done, q + 1)
                A(rstd[:, lcs(q)], PS[:, LAST_BANK[q], 0:lw(q)], ACT.Copy).then_inc(bc_copied, 1)

    @block.gpsimd
    def _(pool):
        TT = nc.gpsimd.tensor_tensor

        def add_squares(p, i, own, sq, buf):
            pool.wait_ge(sq_done, sq)
            if i > 1:
                pool.wait_ge(ss_done, own)
            TT(rstd[:, pcs(p)], rstd[:, pcs(p)], buf, ALU.add).then_inc(ss_done, 1)

        for k in range(KT):
            if k == 0:
                pool.wait_ge(w0_hi, 1)
                TT(Wgl[:, 0, :], raw[:, 0, 0:GMW], F(Wgh[:, 0, :]), ALU.subtract).then_inc(w0_lo, 1)
                pool.wait_ge(w_hi, 1)
                TT(Wgl[:, 1, :], raw[:, 0, GMW:CH], F(Wgh[:, 1, :]), ALU.subtract).then_inc(w_lo, 1)
            elif k in (1, 3, 5):
                c = {1: 1, 3: 2, 5: 3}[k]
                split_lo(pool, c // 2, c % 2, gmv_dst(c))
            if k:
                pool.wait_ge(sq_done, k + 1)
                if k > 1:
                    pool.wait_ge(ss_done, k - 1)
                TT(ssq[:, :], ssq[:, :], sqx[:, k % 2, :], ALU.add).then_inc(ss_done, 1)
        for c in (4, 5):
            split_lo(pool, c // 2, c % 2)
        pool.wait_ge(small_in, 96)
        pool.wait_ge(rtok_done, 1)
        for b in range(NB + 1):
            n = P if b < NB else NS
            last = nc.gpsimd.tensor_scalar(rdiag[:, b, 0:n], ident[:, 0:n], rtok[:, b:b + 1], None, ALU.mult)
        last.then_inc(rdiag_done, 1)
        pool.wait_ge(gv_done, NB + 1)
        nc.gpsimd.memset(Qz[:, :, :], 0.0).then_inc(qz_zero, 1)
        for t in range(NB + 1):
            n = P if t < NB else NS
            pool.wait_ge(ln_sub, t + 1)
            TT(gv[0:n, t, :], gv[0:n, t, :], lnvb[0:n, 0, :], ALU.mult).then_inc(ln_mul, 1)
        for n in range(6):
            split_lo(pool, 3 + n // 2, n % 2)
            if n < 5:
                pool.wait_ge(swapped, n + 1)
                if n == 0:
                    pool.wait_ge(rope_in, 16)
                TT(sw[:, n % 2, :], sw[:, n % 2, :], rope_sb[:, 1, :], ALU.mult).then_inc(sw_sin, 1)
        for i in range(UNITS):
            for t in range(4):
                if i == U_END[t] + 1:
                    split_lo(pool, (12 + t) // 2, t % 2, n=CH if t < 3 else CH // 2)
            lo = P if i < 2 else 0
            pool.wait_ge(ri_done, i + 1)
            for h in range(GRP):
                last = nc.gpsimd.tensor_scalar(Pb[i % 3][:, h, lo:], Pb[i % 3][:, h, lo:], ri[:, i % 2, h:h + 1],
                                               None, ALU.mult)
            last.then_inc(pn_done, 1)
            if i == UNITS - 4:
                pool.wait_ge(ws_in, 16)
                nc.gpsimd.affine_select(out=ws_raw[:, :, :], in_=ws_raw[:, :, :], compare_op=ALU.is_ge, fill=0.0,
                                        base=0, pattern=[[0, HEADS], [1, P]], channel_multiplier=-1)\
                    .then_inc(tri_done, 1)
        pool.wait_ge(ws_hi, 1)
        TT(wsl[:, :, :], ws_raw[:, :, :], F(wsh[:, :, :]), ALU.subtract).then_inc(ws_lo, 1)
        split_lo(pool, 8, 0)
        split_lo(pool, 8, 1, n=CH // 2)
        with pool.Fori(1, 15) as q:
            split_lo(pool, q + 8, 0)
            split_lo(pool, q + 8, 1, n=CH // 2)
        for m in range(3):
            split_lo(pool, 23 + m // 2, m % 2, (WOh[:, m, :], WOl[:, m, :]))
        for w in range(NPC * KT):
            m, p = w % KT, w // KT
            if w + 3 < KT:
                split_lo(pool, 23 + (w + 3) // 2, (w + 3) % 2, (WOh[:, w + 3, :], WOl[:, w + 3, :]))
            if w in (10, 12):
                split_lo(pool, 27, (w - 10) // 2)
            if m:
                add_squares(p, m, 7 * (p + 1) + m - 1, KT + w + 1, MG[:, m, pcs(p)])

        def keep_conv(tile, z, count):
            zs = z[:, SEQ + 2:ZW].rearrange("p (b c) -> p b c", c=3)
            pool.wait_ge(z_rdy, count)
            nc.gpsimd.tensor_copy(cnew[:, bass.ds(tile, 1), 0:2], z[:, SEQ:SEQ + 2].rearrange("p (a c) -> p a c", a=1))
            nc.gpsimd.tensor_copy(cnew[:, bass.ds(tile, 1), 2:2 + 2 * NS].rearrange("p a (b c) -> p (a b) c", c=2),
                                  zs[:, :, 1:3]).then_inc(cnew_done, 1)

        def gate_lo(pair, slot):
            pool.wait_ge(g_hi, pair + 1)
            TT(Gl[:, slot, 0:SEQ], cb[:, 0:SEQ], F(Gh[:, slot, 0:SEQ]), ALU.subtract)
            TT(Gl[:, slot, SEQ:T], cb[:, SEQ + 2:CW:3], F(Gh[:, slot, SEQ:T]), ALU.subtract).then_inc(g_lo, 1)

        pool.wait_ge(par_in, 32)
        for j in range(8):
            split_lo(pool, 28 + j // 2, j % 2)
            keep_conv(j, zb[j % 2], j + 1)
            if j % 2:
                gate_lo(j // 2, j // 2)
        for c in range(2):
            pool.wait_ge(wd_hi, c + 1)
            TT(WDl[:, c, :], WDr[:, c, :], F(WDh[:, c, :]), ALU.subtract).then_inc(wd_lo, 1)
        with pool.Fori(0, NG - 1) as g:
            for j in range(12):
                split_lo(pool, 32 + 6 * g + j // 2, j % 2)
                if j in (0, 1):
                    keep_conv(8 * g + 8 + j, zb[j], 8 * g + 9 + j)
                elif j == 5:
                    gate_lo(4 * g + 4, 0)
                elif j >= 6:
                    keep_conv(8 * g + 8 + j - 4, zb[j % 2], 8 * g + 9 + j - 4)
                    if j % 2:
                        gate_lo(4 * g + 4 + (j - 4) // 2, (j - 4) // 2)
        for i in range(1, KT):
            pool.wait_ge(sq_done, KT + NPC * KT + i + 1)
            if i > 1:
                pool.wait_ge(sum_done_p, i - 1)
            TT(rstd[:, lcs(0)], rstd[:, lcs(0)], sqe[:, i % 2, 0:lw(0)], ALU.add).then_inc(sum_done_p, 1)
        for q in range(2):
            pool.wait_ge(bc_copied, q + 1)
            pool.wait_ge(yg_done, KT * (q + 1))
            for m in range(YP if q else KT):
                TT(X1[:, m, lcs(q)], X1[:, m, lcs(q)], rstd[:, lcs(q)], ALU.mult).then_inc(y_done_p, 1)

    @block.vector
    def _(dve):
        V = nc.vector
        TT, STT, TS = V.tensor_tensor, V.scalar_tensor_tensor, V.tensor_scalar
        link = Link(dve, dve_step)

        def newton(v, s, t, out, step, steps):
            dve.wait_ge(step, steps)
            link(V.reciprocal(s, s))
            link(TT(t, s, s, ALU.mult))
            link(TT(t, t, v, ALU.mult))
            link(TS(t, t, -0.5, 1.5, ALU.mult, ALU.add))
            return TT(out, t, s, ALU.mult)

        def mean(v, bank, n):
            dve.wait_ge(stat_done, n + 1)
            w = v.shape[-1]
            TS(v, PS[:, bank, 0:w], 1.0 / D, EPS, ALU.mult, ALU.add).then_inc(v_done, 1)

        V.memset(ones[:, :], 1.0).then_inc(ones_set, 1)
        link(V.memset(mv[:, :, :], 1.0))
        link(V.memset(lnr[:, :, :], 1.0))
        dve.wait_ge(cols_in, 16)
        dve.wait_ge(x0_in, 16)
        dve.wait_ge(h0_hi, 1)
        STT(Hl[:, 0, 0:X0], x_raw[:, 0, 0:X0], colsb[:, 0, 0:1], F(Hh[:, 0, 0:X0]), ALU.mult, ALU.subtract)\
            .then_inc(h0_lo, 1)
        for k in range(KT):
            c0 = X0 if k == 0 else 0
            dve.wait_ge(x_in[k], 16)
            dve.wait_ge(h_hi, k + 1)
            STT(Hl[:, k, c0:T], x_raw[:, k, c0:T], colsb[:, 0, k:k + 1], F(Hh[:, k, c0:T]), ALU.mult, ALU.subtract)\
                .then_inc(h_lo, 1)
        dve.wait_ge(tsum_done, 1)
        TS(lnr[:, 0, 0:NB], PS[:, 7, 0:NB], 1.0 / D, EPS, ALU.mult, ALU.add)
        TS(lnr[0:NS, 0, NB:NB + 1], PS[0:NS, 7, NB:NB + 1], 1.0 / D, EPS, ALU.mult, ALU.add).then_inc(tmean_done, 1)
        dve.wait_ge(tmean_done, 1)
        newton(lnr[:, 0, :], lnr[:, 1, :], lnr[:, 2, :], rtok[:, :], root_done, 1).then_inc(rtok_done, 1)
        dve.wait_ge(rtok_done, 1)
        for t in range(NB + 1):
            n = P if t < NB else NS
            if t == NB - 1:
                dve.wait_ge(bcast_done, 1)
                V.tensor_copy(thirds(rstd[:, :]), PS[:, 4:7, 0:PC]).then_inc(rstd_done, 1)
            dve.wait_ge(gv_done, t + 1)
            link(V.bn_stats(bst[0:n, t, :], gv[0:n, t, :]))
            link(V.bn_aggr(mv[0:n, t, :], bst[0:n, t, :]))
        TS(lnr[:, 0, :], mv[:, :, 1], EPS, None, ALU.add).then_inc(lnv_done, 1)
        dve.wait_ge(lnv_done, 1)
        link(newton(lnr[:, 0, :], lnr[:, 1, :], lnr[:, 2, :], lnr[:, 2, :], lns_done, 1))
        dve.wait_ge(small_in, 96)
        for t in range(NB + 1):
            n = P if t < NB else NS
            TS(gv[0:n, t, :], gv[0:n, t, :], mv[0:n, t, 0:1], lnr[0:n, 2, t:t + 1], ALU.subtract, ALU.mult)\
                .then_inc(ln_sub, 1)
        for t in range(NB + 1):
            n = P if t < NB else NS
            dve.wait_ge(ln_mul, t + 1)
            TT(vnf[:, t, :] if t < NB else gv[0:NS, NB, :], gv[0:n, t, :], lnvb[0:n, 1, :], ALU.add)\
                .then_inc(ln_done, 1)
        link(TS(snk[:, 0, :], snk[:, 0, :], -1.0, None, ALU.mult))
        link(TS(snS[:, 0:1], snS[:, 0:1], -1.0, None, ALU.mult))
        dve.wait_ge(rope_in, 16)
        dve.wait_ge(rstd_done, 1)
        def tile_ev(n):
            dve.wait_ge(w_used, 5 + n)
            if n == 2:
                dve.wait_ge(k_out, 16)
            if n >= 2:
                dve.wait_ge(rot_hi, n - 1)
                dve.wait_ge(rot_lo, n - 1)
            TT(thirds(zt[:, n % 2, :]), PS[:, 3 * (n % 2):3 * (n % 2) + 3, 0:PC], rstd3, ALU.mult).then_inc(z_ev, 1)

        def rotated_lo(n):
            dve.wait_ge(rot_done, n + 1)
            if n == 0:
                link(V.tensor_copy(kS[:, :], zt[:, 0, SEQ:T]))
                dve.wait_ge(kc_in, 16)
                V.tensor_copy(Kc[:, :, P:P + 1].rearrange("p b a -> p (b a)"), kS[:, :]).then_inc(kn_done, 1)
            else:
                dve.wait_ge(qz_zero, 1)
                Qf = Qz[:, :, :].rearrange("p b c -> p (b c)")
                for g in range(KVH):
                    h = GRP * g + n - 1
                    V.tensor_copy(Qf[64 * g:64 * g + 64, h:h + 72 * (NS - 1) + 1:72],
                                  zt[64 * g:64 * g + 64, n % 2, SEQ:T])
            dve.wait_ge(rot_hi, n + 1)
            hi, lo = (kh[:, :], kl[:, :]) if n == 0 else (QYh[:, n - 1, :], QYl[:, n - 1, :])
            TT(lo, zt[:, n % 2, :], F(hi), ALU.subtract).then_inc(rot_lo, 1)

        for n in range(5):
            tile_ev(n)
            if n == 1:
                dve.wait_ge(mixp_done, 1)
                for e in range(2):
                    V.tensor_copy(mixS[64 * e:64 * e + 64, :, :],
                                  PS[64 * e:64 * e + 64, 7, 0:64].rearrange("p (a e b) -> p a e b", e=2, b=NS)[:, :, e, :]
                                  ).then_inc(mix_done, 1)
            if n:
                rotated_lo(n - 1)
            dve.wait_ge(z_ev, n + 1)
            dve.wait_ge(swapped, n + 1)
            link(TT(zt[:, n % 2, :], zt[:, n % 2, :], rope_sb[:, 0, :], ALU.mult))
            dve.wait_ge(sw_sin, n + 1)
            TT(zt[:, n % 2, :], zt[:, n % 2, :], sw[:, n % 2, :], ALU.add).then_inc(rot_done, 1)
        tile_ev(5)
        rotated_lo(4)
        dve.wait_ge(vt_done, 3)
        V.tensor_copy(vS[:, :], PS[0:NS, 1, 0:P]).then_inc(vs_done, 1)
        for i in range(2):
            dve.wait_ge(vt_hi, i + 1)
            TT(Vl[:, 4 * i:4 * i + 4, :].rearrange("p b c -> p (b c)"), PS[:, 6 + i, :],
               F(Vh[:, 4 * i:4 * i + 4, :].rearrange("p b c -> p (b c)")), ALU.subtract).then_inc(vt_lo, 1)
        dve.wait_ge(band_in, 16)

        def fill_ev(f):
            t, p = f // NPC, f % NPC
            if p < 2:
                dve.wait_ge(u_done, 2 * t + p + 1)
            else:
                dve.wait_ge(w_used, C_U + t + 1)
            TT(U[:, t, pcs(p)], PS[:, f % 2, 0:PC], rstd[:, pcs(p)], ALU.mult).then_inc(u_ev, 1)

        def vn_rest(b):
            dve.wait_ge(vn_hi, VN_ORDER.index(b) + 1)
            TT(vnl[:, b, :], vnf[:, b, :], F(vnh[:, b, :]), ALU.subtract).then_inc(vn_lo, 1)

        fill_ev(0)
        for i in range(UNITS + 2):
            if i < UNITS:
                g, lo = i % 2, P if i < 2 else 0
                dve.wait_ge(s_done, i + 1)
                if i >= 3:
                    dve.wait_ge(pt_done, i - 2)
                for h in range(GRP):
                    last = V.tensor_tensor_reduce(
                        out=Pb[i % 3][:, h, lo:], in0=PS[:, 2 + h // 2, (h % 2) * 256 + lo:(h % 2) * 256 + 256],
                        in1=band[:, lo:], scale=1.0, scalar=-3.0e38, op0=ALU.add, op1=ALU.max,
                        accum_out=mx[:, i % 2, h:h + 1])
                last.then_inc(masked, 1)
                dve.wait_ge(masked, i + 1)
                STT(nm[:, i % 2, :], mx[:, i % 2, :], -SCALE, snk[:, 0, GRP * g:GRP * g + GRP], ALU.mult, ALU.min)\
                    .then_inc(nm_done, 1)
                dve.wait_ge(nm_done, i + 1)
                TT(es[:, i % 2, :], nm[:, i % 2, :], snk[:, 1, GRP * g:GRP * g + GRP], ALU.add).then_inc(esin_done, 1)
            if 2 <= i:
                u = i - 2
                dve.wait_ge(pt_hi, u + 1)
                for kt in ((1,) if u < 2 else (0, 1)):
                    TT(PTl[:, kt, :], PS[:, 4 + kt, :], F(PTh[:, kt, :]), ALU.subtract).then_inc(pt_lo, 1)
            for f in filled(i):
                fill_ev(f)
            if i < UNITS:
                dve.wait_ge(exp_done, i + 1)
                dve.wait_ge(es_done, i + 1)
                link(TT(ri[:, i % 2, :], sm[:, i % 2, :], es[:, i % 2, :], ALU.add))
                V.reciprocal(ri[:, i % 2, :], ri[:, i % 2, :]).then_inc(ri_done, 1)
            if 2 <= i:
                u, b, g = i - 2, (i - 2) // 2, (i - 2) % 2
                dve.wait_ge(o_hi, u + 1)
                TT(QYl[64 * g:64 * g + 64, :, blk(b)],
                   PS[64 * g:64 * g + 64, 6, :].rearrange("p (r t) -> p r t", r=GRP),
                   F(QYh[64 * g:64 * g + 64, :, blk(b)]), ALU.subtract).then_inc(o_ev, 1)
            if i == 1:
                dve.wait_ge(ss_sc, 1)
                link(V.tensor_reduce(st[:, 0:1], PS[0:64, 7, 0:P + 1], AX.X, ALU.max))
                link(STT(st[:, 1:2], st[:, 0:1], -SCALE, snS[:, 0:1], ALU.mult, ALU.min))
                TT(st[:, 2:3], st[:, 1:2], snS[:, 1:2], ALU.add).then_inc(sn_done, 1)
            if i == 3:
                dve.wait_ge(sx_done, 1)
                link(TT(st[:, 5:6], st[:, 3:4], st[:, 4:5], ALU.add))
                link(V.reciprocal(st[:, 5:6], st[:, 5:6]))
                link(TS(Ps[:, :], Ps[:, :], st[:, 5:6], None, ALU.mult))
                TS(Dm[:, :], bmask[:, :], Ps[:, P:P + 1], None, ALU.mult).then_inc(sp_done, 1)
            if i == 7:
                dve.wait_ge(so_hi, 1)
                for g in range(KVH):
                    last = TT(QYl[64 * g:64 * g + 64, :, SEQ:T],
                              PS[64 * g:64 * g + 64, 7, 384:448].rearrange("p (b h) -> p h b", h=HEADS)
                              [:, GRP * g:GRP * g + GRP, :], F(QYh[64 * g:64 * g + 64, :, SEQ:T]), ALU.subtract)
                last.then_inc(so_lo, 1)
            if i == UNITS:
                for b in VN_ORDER[:3]:
                    vn_rest(b)
        dve.wait_ge(w_used, C_G + 1)
        TT(thirds(sig[:, :]), PS[:, 0:3, 0:PC], rstd3, ALU.mult).then_inc(g_ev, 1)
        for b in VN_ORDER[3:]:
            vn_rest(b)
        dve.wait_ge(ws_lo, 1)
        dve.wait_ge(bs_in, 16)
        for u in range(2 * NB):
            hp, b, bank = u // NB, VN_ORDER[u % NB], (0, 1, 6, 7)[u % 4]
            dve.wait_ge(sp_mm, u + 1)
            for e in range(2):
                last = TT(YAt[64 * e:64 * e + 64, 2 * hp:2 * hp + 2, blk(b)],
                          PS[64 * e:64 * e + 64, bank, :].rearrange("p (r e t) -> p r e t", r=2, e=2)[:, :, e, :],
                          bsb[64 * e:64 * e + 64, 2 * hp:2 * hp + 2, :], ALU.add)
            last.then_inc(sp_ev, 1)
        for t in range(4):
            link(TS(YAt[:, t, SEQ:T], mixS[:, t, :], bsb[:, t, 0:1], None, ALU.add))
        dve.wait_ge(sp_ev, 2 * NB)
        for t in range(4):
            dve.wait_ge(ug_done, t + 1)
            TT(U[:, t, :], YAt[:, t, :], U[:, t, :], ALU.mult).then_inc(ya_done, 1)

        def gate_ev(q):
            dve.wait_ge(w_used, C_G + 1 + 2 * q)
            dve.wait_ge(p_ev, q)
            TT(thirds(sig[:, :]), PS[:, 0:3, 0:PC], rstd3, ALU.mult).then_inc(g_ev, 1)

        def branch_a(q):
            dve.wait_ge(th_done, q + 1)
            dve.wait_ge(w_used, C_G + 2 + 2 * q)
            STT(MGv[:, bass.ds(3 * q, 3), :], thirds(sig[:, :]), 1.0, PS[:, 3:6, 0:PC], ALU.add, ALU.mult)\
                .then_inc(p_ev, 1)

        def branch_b(q, m):
            dve.wait_ge(th_done, q + 1)
            dve.wait_ge(w_used, C_G + 2 + 2 * q)
            link(STT(thirds(sig[:, :]), thirds(sig[:, :]), 1.0, PS[:, 3:6, 0:PC], ALU.add, ALU.mult))
            TT(MGv[:, bass.ds(3 * m, 3), :], MGv[:, bass.ds(3 * m, 3), :], thirds(sig[:, :]), ALU.add)\
                .then_inc(p_ev, 1)

        branch_a(0)
        for t in range(4):
            dve.wait_ge(ya_hi, t + 1)
            TT(YAl[:, t, :], U[:, t, :], F(YAh[:, t, :]), ALU.subtract).then_inc(ya_lo, 1)
        with dve.Fori(1, KT) as q:
            gate_ev(q)
            branch_a(q)
        n0 = link.n
        with dve.Fori(0, KT - 1) as m:
            link.off = m
            gate_ev(m + 8)
            branch_b(m + 8, m)
        link.off = 0
        link.n = n0 + KT - 1

        def merged_lo(p, k0, k1, n):
            dve.wait_ge(mg_hi, n)
            STT(MSl[p % 2][:, k0:k1, :], MG[:, k0:k1, pcs(p)], 0.5, F(MSh[p % 2][:, k0:k1, :]),
                ALU.mult, ALU.subtract).then_inc(mg_lo, 1)

        def ffn_in_lo(k):
            dve.wait_ge(h_hi, KT + k + 1)
            STT(Hl[:, k, :], X1[:, k, :], colsb[:, 1, k:k + 1], F(Hh[:, k, :]), ALU.mult, ALU.subtract)\
                .then_inc(h_lo, 1)

        merged_lo(0, 0, KT - 1, 1)
        gate_ev(15)
        branch_b(15, 7)
        merged_lo(0, KT - 1, KT, 2)
        for w in range(NPC * KT):
            m, p = w % KT, w // KT
            if w == 5:
                merged_lo(1, 0, KT, 3)
            if w == 10:
                merged_lo(2, 0, KT, 4)
            dve.wait_ge(xr_in[w % 3], 16 * (w // 3 + 1))
            if w < NPC * KT - 1:
                dve.wait_ge(wo_done, w + 1)
            else:
                dve.wait_ge(w_used, C_UP0)
            TT(X1[:, m, pcs(p)], PS[:, w % 6, 0:PC], xr[:, w % 3, :], ALU.add).then_inc(x1_ev, 1)
            if w == 19:
                mean(rstd[:, pcs(0)], 6, 0)
            if w >= 19:
                ffn_in_lo(w - 19)
        mean(rstd[:, pcs(1)], 7, 1)
        for k in (5, 6, 7):
            ffn_in_lo(k)
        for i, (c, n) in enumerate(MID):
            if i:
                mean(rstd[:, pcs(2)], 6, 2)
            dve.wait_ge(v_done, n)
            newton(rstd[:, c], nsm[:, c], ntm[:, c], rstd[:, c], root_done, 2 + i).then_inc(rstd_done, 1)
        for i in range(2):
            link(V.memset(zb[i][:, 0:2], 0.0))
        dve.wait_ge(par_in, 32)

        def up_ev(s, tile, used, count):
            z = zb[s]
            zs = z[:, SEQ + 2:ZW].rearrange("p (b c) -> p b c", c=3)
            dve.wait_ge(w_used, used)
            dve.wait_ge(rstd_done, 3)
            if count is not None:
                dve.wait_ge(cnew_done, count)
            link(TT(thirds(z[:, 2:2 + T]), PS[:, 3 * s:3 * s + 3, 0:PC], rstd3, ALU.mult))
            TT(zs[:, :, 2:3].rearrange("p b c -> p (b c)"), PS[:, 3 * s + 2, PC - NS:PC], rstd[:, SEQ:T], ALU.mult)\
                .then_inc(f_ev, 1)
            V.tensor_copy(zs[:, :, 0:2], cst[:, bass.ds(tile, 1), :, :].rearrange("p a b c -> p (a b) c"))\
                .then_inc(z_rdy, 1)

        def conv(s, tile, count):
            z, c = zb[s], (ca, cb)[s]
            dve.wait_ge(z_rdy, count)
            dve.wait_ge(c0_done, count)
            link(STT(c[:, :], z[:, 1:ZW - 1], cpar[:, bass.ds(tile, 1), 1], c[:, :], ALU.mult, ALU.add))
            STT(c[:, :], z[:, 0:ZW - 2], cpar[:, bass.ds(tile, 1), 0], c[:, :], ALU.mult, ALU.add)\
                .then_inc(conv_done, 1)

        def gated(pair):
            dve.wait_ge(conv_done, 2 * pair + 2)
            dve.wait_ge(gelu_done, pair + 1)
            TT(cb[:, :], ca[:, :], cb[:, :], ALU.mult).then_inc(g_done, 1)

        def down_ev(m):
            s = m % 2
            X = X1v[:, 3 * m:3 * m + 3, :]
            TT(X, X, PS[:, 3 * s:3 * s + 3, 0:PC], ALU.add).then_inc(f_ev, 1)

        for j in range(8):
            up_ev(j % 2, j, C_UP0 + j + 1, j - 1 if j >= 2 else None)
            conv(j % 2, j, j + 1)
            if j % 2:
                gated(j // 2)
        n0 = link.n
        with dve.Fori(0, NG - 1) as g:
            link.off = 16 * g
            for j in range(12):
                used = C_LOOP + 12 * g + j + 1
                if 2 <= j < 6:
                    dve.wait_ge(dn_half, 4 * g + j - 1)
                    down_ev(2 * (j - 2))
                    dve.wait_ge(w_used, used)
                    down_ev(2 * (j - 2) + 1)
                    continue
                i = j if j < 2 else j - 4
                up_ev(j % 2, 8 * g + 8 + i, used, 8 * g + 7 + i)
                conv(j % 2, 8 * g + 8 + i, 8 * g + 9 + i)
                if j % 2:
                    gated(4 * g + 4 + i // 2)
        assert link.n - n0 == 16
        link.off = 0
        link.n = n0 + 16 * (NG - 1)

        def add_square(p, i):
            dve.wait_ge(sq_done, KT + NPC * KT + KT * p + i + 1)
            if i > 1:
                dve.wait_ge(sum_done, 7 * (p - 1) + i - 1)
            TT(rstd[:, lcs(p)], rstd[:, lcs(p)], sqe[:, i % 2, 0:lw(p)], ALU.add).then_inc(sum_done, 1)

        def token_norm(q):
            dve.wait_ge(stat_done, NPC + q + 1)
            for b in range(lb(q)):
                n = min(P, lw(q) - b * P)
                last = TS(mx2[0:n, b:b + 1], PS[0:n, LAST_BANK[q], b:b + 1], 1.0 / D, EPS, ALU.mult, ALU.add)
            last.then_inc(v_done, 1)
            dve.wait_ge(v_done, NPC + q + 1)
            newton(mx2[:, 0:lb(q)], nm2[:, 0:lb(q)], sm2[:, 0:lb(q)], es2[:, 0:lb(q)], root_done, 4 + q)\
                .then_inc(rstd_done, 1)
            dve.wait_ge(rstd_done, 4 + q)
            if q:
                dve.wait_ge(bc_done, q)
            for b in range(lb(q)):
                n = min(P, lw(q) - b * P)
                last = TS(dg[:, b * P:b * P + n], ident[:, 0:n], es2[:, b:b + 1], None, ALU.mult)
            last.then_inc(dg_done, 1)

        for w in range(NPC * KT):
            p, i = w // KT, w % KT
            m = LAST_ORDER[p][i]
            dve.wait_ge(last_mm, w + 1)
            X = X1[:, m, lcs(p)]
            TT(X, X, PS[:, last_out(p, m), 0:lw(p)], ALU.add).then_inc(y_ev, 1)
            if p and i >= 2:
                add_square(p, i - 1)
            if p and i == KT - 1:
                add_square(p, i)
            if (p, i) in LAST_ROOT:
                token_norm(LAST_ROOT[p, i])
        dve.wait_ge(bc_copied, 2)
        dve.wait_ge(yg_done, 2 * KT)
        for m in range(YP, KT):
            TT(X1[:, m, lcs(1)], X1[:, m, lcs(1)], rstd[:, lcs(1)], ALU.mult).then_inc(y_done, 1)
        dve.wait_ge(bc_done, NPC)
        dve.wait_ge(yg_done, NPC * KT)
        for m in range(KT):
            TT(X1[:, m, lcs(2)], X1[:, m, lcs(2)], PS[:, LAST_BANK[2], 0:lw(2)], ALU.mult).then_inc(y_done, 1)

    @block.tensor
    def _(pe):
        MM = nc.tensor.matmul

        def block_of(slot, i):
            return Wh[:, slot, i * P:(i + 1) * P], Wl[:, slot, i * P:(i + 1) * P]

        def tile(s, slot, rh, rl, first=0, n=KT):
            for k in range(n):
                wh, wl = block_of(slot, first + k)
                for p in range(NPC):
                    last = mm3(PS[:, 3 * s + p, 0:PC], wh, wl, rh[:, k, pcs(p)], rl[:, k, pcs(p)], k == 0, k == n - 1)
            return last

        def gmv(t, k, bank):
            rows = blk(t) if t < NB else slice(SEQ, T)
            n = P if t < NB else NS
            return mm3(PS[0:n, bank, :], Hh[:, k, rows], Hl[:, k, rows], Wgh[:, k, :], Wgl[:, k, :],
                       k == 0, k == KT - 1)

        pe.wait_ge(ones_set, 1)
        for _ in range(WARM_UP):
            MM(PS[:, 7, 0:P], ones[:, :], ones[:, :], start=True, stop=True)
        pe.wait_ge(h0_lo, 1)
        pe.wait_ge(w0_lo, 1)
        for t in range(4):
            gmv(t, 0, t)
        for k in range(KT):
            pe.wait_ge(h_lo, k + 1)
            if k % 2 or k == 2:
                pe.wait_ge(w_lo, (k + 1) // 2)
            if k == 2:
                pe.wait_ge(w_lo, 2)
            elif k and k % 2 == 0:
                pe.wait_ge(w_lo, k // 2 + 1)
            for t in range(4 if k == 0 else 0, 5):
                last = gmv(t, k, t)
                if k == KT - 1:
                    last.then_inc(tok_done, 1)
        pe.wait_ge(ones_set, 1)
        pe.wait_ge(ss_done, KT - 1)
        for b in range(NB + 1):
            n = P if b < NB else NS
            last = MM(PS[0:n, 7, b:b + 1], ssq[:, b * P:b * P + n], ones[:, 0:1], start=True, stop=True)
        last.then_inc(tsum_done, 1)
        for t in (5, 6, 7, 8):
            if t == 7:
                pe.wait_ge(tmean_done, 1)
            if t == 8:
                pe.wait_ge(rdiag_done, 1)
                pe.wait_ge(gv_done, 7)
                rd = rdiag[:, :, :].rearrange("p b t -> p (b t)")
                for p in range(NPC):
                    last = MM(PS[:, 4 + p, 0:PC], ones[:, :], rd[:, pcs(p)], start=True, stop=True)
                last.then_inc(bcast_done, 1)
            for k in range(KT):
                last = gmv(t, k, t if t < NB else 3)
            last.then_inc(*((tok_done, 1) if t < NB else (w_used, 4)))
        for n in range(6):
            pe.wait_ge(w_lo, 5 + n)
            if n == 1:
                pe.wait_ge(gv_done, NB + 1)
                pe.wait_ge(rstd_done, 1)
            if n >= 2:
                pe.wait_ge(z_ev, n - 1)
            tile(n % 2, n % 2, Hh, Hl).then_inc(w_used, 1)
            if n == 1:
                pe.wait_ge(ln_done, NB + 1)
                for a in range(4):
                    last = MM(PS[:, 7, 16 * a:16 * a + 16], gv[0:NS, NB, blk(a)],
                              wdiag[:, 2 * a:2 * a + 2, :].rearrange("p h b -> p (h b)"), start=True, stop=True)
                last.then_inc(mixp_done, 1)
        def scores(i):
            b, g = i // 2, i % 2
            rows = slice(64 * g, 64 * g + 64)
            lo = P if b == 0 else 0
            keys = slice((b - 1) * P + lo, (b + 1) * P)
            if i:
                pe.wait_ge(masked, i)
            for h in range(GRP):
                last = mm3(PS[:, 2 + h // 2, (h % 2) * 256 + lo:(h % 2) * 256 + 256],
                           QYh[rows, h, blk(b)], QYl[rows, h, blk(b)], kh[rows, keys], kl[rows, keys], True, True)
            last.then_inc(s_done, 1)

        def fill(n):
            f, h = n // 4, n % 4
            t, p = f // NPC, f % NPC
            if n == 4 * NPC * t:
                pe.wait_ge(w_lo, C_U + t + 1)
            if n == 4:
                pe.wait_ge(vs_done, 1)
            elif n == 56:
                pe.wait_ge(masked, UNITS)
            elif h == 0 and f:
                pe.wait_ge(u_ev, f - 1)
            bank = f % 2 if f < 12 else p
            for k in (2 * h, 2 * h + 1):
                wh, wl = block_of(t % 2, k)
                last = mm3(PS[:, bank, 0:PC], wh, wl, Hh[:, k, pcs(p)], Hl[:, k, pcs(p)], k == 0, k == KT - 1)
            if h == 3 and p == 2:
                last.then_inc(w_used, 1)
            elif h == 3 and f < 12:
                last.then_inc(u_done, 1)

        pe.wait_ge(z_ev, 5)
        for n in range(4):
            fill(n)
        pe.wait_ge(z_ev, 6)
        pe.wait_ge(mix_done, 2)
        pe.wait_ge(small_in, 96)
        for i in range(2):
            for b in range(4):
                last = nc.tensor.transpose(PS[:, 6 + i, blk(b)], zt[:, 1, blk(4 * i + b)], ident[:, :])
            last.then_inc(vt_done, 1)
        nc.tensor.transpose(PS[0:NS, 1, 0:P], zt[:, 1, SEQ:T], ident[:, :]).then_inc(vt_done, 1)
        pe.wait_ge(rot_lo, 5)
        for i in range(UNITS + 2):
            if i < UNITS:
                scores(i)
            if 2 <= i:
                u, b = i - 2, (i - 2) // 2
                pe.wait_ge(pn_done, u + 1)
                if u:
                    pe.wait_ge(pt_lo, halves(u - 1))
                for kt in ((1,) if b == 0 else (0, 1)):
                    for h in range(GRP):
                        last = nc.tensor.transpose(PS[:, 4 + kt, blk(h)], Pb[u % 3][:, h, blk(kt)], ident[:, :])
                last.then_inc(pt_done, 1)
            for n in FILL[i]:
                fill(n)
            if i == 1:
                pe.wait_ge(kn_done, 1)
                pe.wait_ge(vt_lo, 2)
                for b in range(NS):
                    last = MM(PS[0:64, 7, 0:P + 1], Qz[:, b, :], Kc[:, b, :], start=b == 0, stop=b == NS - 1)
                last.then_inc(ss_sc, 1)
            if i == 4:
                pe.wait_ge(sp_done, 1)
                nc.tensor.transpose(PS[:, 7, 256:320], Ps[:, 0:P], ident[0:64, 0:64])
                nc.tensor.transpose(PS[0:NS, 7, 320:384], Dm[:, :], ident[0:64, 0:64]).then_inc(spt_done, 1)
            if i == 6:
                pe.wait_ge(sptc_done, 1)
                pe.wait_ge(vc_in, 16)
                MM(PS[:, 7, 384:448], vS[:, :], Dt[:, :], start=True, stop=False)
                for b in range(NS):
                    last = MM(PS[:, 7, 384 + 8 * b:392 + 8 * b], Vc[:, b, :], PTs[:, 8 * b:8 * b + 8],
                              start=False, stop=b == NS - 1)
                last.then_inc(spv_done, 1)
            if 2 <= i:
                u, b = i - 2, (i - 2) // 2
                if u:
                    pe.wait_ge(o_ev, u)
                else:
                    pe.wait_ge(vt_lo, 2)
                kts = (1,) if b == 0 else (0, 1)
                for kt in kts:
                    pe.wait_ge(pt_lo, halves(u) - 1 + kt)
                    last = mm3(PS[:, 6, :], Vh[:, b - 1 + kt, :], Vl[:, b - 1 + kt, :], PTh[:, kt, :], PTl[:, kt, :],
                               kt == kts[0], kt == 1)
                last.then_inc(pv_done, 1)
        pe.wait_ge(w_lo, C_G + 2)
        pe.wait_ge(so_lo, 1)
        pe.wait_ge(pt_lo, halves(UNITS - 1))
        for p in range(NPC):
            pe.wait_ge(o_ev, (6, 12, UNITS)[p])
            for k in range(4):
                wh, wl = block_of(1, k)
                last = mm3(PS[:, 3 + p, 0:PC], wh, wl, QYh[:, k, pcs(p)], QYl[:, k, pcs(p)], k == 0, k == 3)
        last.then_inc(w_used, 1)
        pe.wait_ge(ws_lo, 1)
        pe.wait_ge(g_ev, 1)
        for u in range(2 * NB):
            hp, b, bank = u // NB, VN_ORDER[u % NB], (0, 1, 6, 7)[u % 4]
            pe.wait_ge(vn_lo, u % NB + 1)
            if u >= 4:
                pe.wait_ge(sp_ev, u - 3)
            for r in range(2):
                a = 2 * hp + r
                last = mm3(PS[:, bank, 256 * r:256 * r + 256], vnh[:, b, blk(a)], vnl[:, b, blk(a)],
                           wsh[:, 2 * a:2 * a + 2, :].rearrange("p h t -> p (h t)"),
                           wsl[:, 2 * a:2 * a + 2, :].rearrange("p h t -> p (h t)"), True, True)
            last.then_inc(sp_mm, 1)

        def gate_mm(q):
            pe.wait_ge(w_lo, C_G + 1 + 2 * q)
            pe.wait_ge(g_ev, q)
            tile(0, 0, Hh, Hl).then_inc(w_used, 1)

        def proj_mm(q, rh, rl):
            pe.wait_ge(w_lo, C_G + 2 + 2 * q)
            tile(1, 1, rh, rl, n=4).then_inc(w_used, 1)

        pe.wait_ge(sp_ev, 2 * NB - 2)
        with pe.Fori(1, KT) as q:
            gate_mm(q)
            pe.wait_ge(p_ev, q)
            proj_mm(q, QYh, QYl)
        pe.wait_ge(ya_lo, 4)
        with pe.Fori(KT, 2 * KT) as q:
            gate_mm(q)
            pe.wait_ge(p_ev, q)
            proj_mm(q, YAh, YAl)
        def wo_rows(w, k0, k1):
            m, p = w % KT, w // KT
            for k in range(k0, k1):
                last = mm3(PS[:, w % 6, 0:PC], WOh[:, m, blk(k)], WOl[:, m, blk(k)], MSh[p % 2][:, k, :],
                           MSl[p % 2][:, k, :], k == 0, k == KT - 1)
            return last

        for w in range(3):
            pe.wait_ge(w_lo, C_WO + w + 1)
            if w == 0:
                pe.wait_ge(mg_lo, 1)
                pe.wait_ge(g_ev, 2 * KT)
            wo_rows(w, 0, KT - 1)
        for w in range(NPC * KT):
            m, p = w % KT, w // KT
            if w >= 6:
                pe.wait_ge(x1_ev, w - 5)
            if 3 <= w < KT:
                pe.wait_ge(w_lo, C_WO + m + 1)
            if m == 0:
                pe.wait_ge(mg_lo, p + 2)
            last = wo_rows(w, KT - 1 if w < 3 else 0, KT)
            if w < NPC * KT - 1:
                last.then_inc(wo_done, 1)
            else:
                last.then_inc(w_used, KT)
            if w in (17, 23):
                q = (w - 17) // 6
                pe.wait_ge(ss_done, 7 * (q + 2))
                MM(PS[:, 6 + q, 0:PC], ones[:, :], rstd[:, pcs(q)], start=True, stop=True).then_inc(stat_done, 1)

        for j in range(8):
            pe.wait_ge(w_lo, C_UP0 + j + 1)
            if j >= 2:
                pe.wait_ge(f_ev, j - 1)
            else:
                pe.wait_ge(x1_ev, NPC * KT)
            for k in range(KT):
                if j == 0:
                    pe.wait_ge(h_lo, KT + k + 1)
                wh, wl = block_of(j % 2, k)
                for p in range(NPC):
                    last = mm3(PS[:, 3 * (j % 2) + p, 0:PC], wh, wl, Hh[:, k, pcs(p)], Hl[:, k, pcs(p)],
                               k == 0, k == KT - 1)
                if (j, k) != (0, 5):
                    continue
                pe.wait_ge(ss_done, 7 * (NPC + 1))
                pe.wait_ge(v_done, 1)
                MM(PS[:, 6, 0:PC], ones[:, :], rstd[:, pcs(2)], start=True, stop=True).then_inc(stat_done, 1)
            last.then_inc(w_used, 1)
        with pe.Fori(0, NG - 1) as g:
            n = 0
            for j in range(12):
                pe.wait_ge(w_lo, C_LOOP + 12 * g + j + 1)
                if 2 <= j < 6:
                    if j == 2:
                        pe.wait_ge(g_lo, 4 * g + 4)
                    for h in range(2):
                        pe.wait_ge(f_ev, 16 * g + 7 + n)
                        tile(h, j % 2, Gh, Gl, first=GP * h, n=GP).then_inc(w_used if h else dn_half, 1)
                        n += 1
                else:
                    pe.wait_ge(f_ev, 16 * g + 7 + n)
                    tile(j % 2, j % 2, Hh, Hl).then_inc(w_used, 1)
                    n += 1
        assert n == 16
        def last_block(m, k):
            if m < 4:
                return block_of(m // 2, (m % 2) * GP + k)
            i = ((m % 2) * GP + k) * P
            return WDh[:, m // 2 - 2, i:i + P], WDl[:, m // 2 - 2, i:i + P]

        def last_tile(m, k, p):
            wh, wl = last_block(m, k)
            return mm3(PS[:, last_out(p, m), 0:lw(p)], wh, wl, Gh[:, k, lcs(p)], Gl[:, k, lcs(p)], k == 0, k == GP - 1)

        def last_stat(q):
            pe.wait_ge(*((sum_done, 7 * q) if q else (sum_done_p, 7)))
            for b in range(lb(q)):
                n = min(P, lw(q) - b * P)
                c = LAST_PC[q] + b * P
                last = MM(PS[0:n, LAST_BANK[q], b:b + 1], rstd[:, c:c + n], ones[:, 0:1], start=True, stop=True)
            last.then_inc(stat_done, 1)

        def last_bcast(q):
            pe.wait_ge(dg_done, q + 1)
            MM(PS[:, LAST_BANK[q], 0:lw(q)], ones[:, :], dg[:, 0:lw(q)], start=True, stop=True).then_inc(bc_done, 1)

        pe.wait_ge(g_lo, NPAIR - 1)
        pe.wait_ge(wd_lo, 2)
        for c in (3, 2, 0, 1):
            if c == 2:
                pe.wait_ge(f_ev, 16 * (NG - 1) + 8)
            if c < 2:
                pe.wait_ge(w_lo, C_LAST + c + 1)
            for k in range(GP - 1):
                for m in (2 * c, 2 * c + 1):
                    last_tile(m, k, 0)
        pe.wait_ge(g_lo, NPAIR)
        for m in range(KT):
            last_tile(m, GP - 1, 0).then_inc(last_mm, 1)
        for p in (1, 2):
            for i, m in enumerate(LAST_ORDER[p]):
                pe.wait_ge(y_ev, KT * (p - 1) + LAST_ORDER[p - 1].index(m) + 1)
                if (p, m) == (2, 0):
                    pe.wait_ge(y_ev, 2 * KT + 1)
                for k in range(GP):
                    last = last_tile(m, k, p)
                last.then_inc(last_mm, 1)
                if i == 2:
                    pe.wait_ge(y_ev, KT + 1)
                    if p == 2:
                        pe.wait_ge(bc_copied, 1)
                    last_stat(p - 1)
                if i == 5:
                    last_bcast(p - 1)
        pe.wait_ge(y_ev, 2 * KT + 2)
        last_stat(2)
        last_bcast(2)

    block_cm.__exit__(None, None, None)


def tiles_of(w):
    K, N = w.shape
    return np.ascontiguousarray(w.reshape(K // P, P, N // P, P).transpose(2, 1, 0, 3).reshape(N // P, P, K))


def kernel(**inputs):
    import concourse.bacc as bacc
    from concourse.bass_utils import run_bass_kernel_spmd

    a = {k: np.asarray(v) for k, v in inputs.items()}
    f = np.float32
    x = np.concatenate([a["x_prompt"][0], a["x_sample"][:, 0]], axis=0)
    w_in = a["w_in"][0]
    o_q, o_k = 2 * GMW, 2 * GMW + HEADS * HD
    o_v = o_k + KVH * HD
    o_ga = o_v + KVH * HD
    o_gb = o_ga + D
    head_order = [h for r in range(GRP) for h in (r, GRP + r)]
    rows_b = np.concatenate([np.arange(h * HD, (h + 1) * HD) for h in head_order])
    gm = w_in[:, GMW:2 * GMW].reshape(4, 2, P, GMW).transpose(0, 2, 1, 3).reshape(4, P, CH)
    w_main = np.concatenate([gm, tiles_of(w_in[:, o_k:o_v]), tiles_of(w_in[:, o_q:o_k][:, rows_b]),
                             tiles_of(w_in[:, o_v:o_ga]), tiles_of(w_in[:, 0:GMW]),
                             tiles_of(w_in[:, o_gb:]), tiles_of(w_in[:, o_ga:o_gb]),
                             tiles_of(a["w_o"][0])], axis=0)
    w_half = np.concatenate([tiles_of(a["w_pb"][0][rows_b]), tiles_of(a["w_pa"][0])], axis=0)
    up = tiles_of(a["w_up"][0])
    up = np.stack([up[:NPAIR], up[NPAIR:]], axis=1).reshape(NG, 2 * GP, P, CH)
    dn = a["w_down"][0].reshape(NG, GP, P, KT // 2, 2, P).transpose(0, 3, 2, 4, 1, 5).reshape(NG, 4, P, CH)
    parts = [up[0]]
    for g in range(1, NG):
        parts += [up[g][0:2], dn[g - 1], up[g][2:]]
    w_ffn = np.concatenate(parts + [dn[NG - 1]], axis=0)
    cols = np.stack([a["g_mix"][0], a["g_ffn"][0], a["g_final"]]).reshape(3, KT, P).transpose(2, 0, 1)

    half = HD // 2
    inv = (10000.0 ** (-np.arange(half) / half)).astype(f)
    pos = np.concatenate([np.arange(SEQ), np.full(NS, 8192)]).astype(f)
    ang = (pos[:, None] * inv[None, :]).astype(f)
    cos = np.tile(np.cos(ang).astype(f).T, (4, 1))
    sin = np.sin(ang).astype(f).T
    rope = np.stack([cos, np.tile(np.concatenate([-sin, sin]), (2, 1))], axis=1)
    i = np.arange(P)
    mask = np.zeros((P, 2 * P), f)
    mask[:, :P][i[None, :] < i[:, None]] = MASKED
    mask[:, P:][i[None, :] > i[:, None]] = MASKED
    sinks = a["sinks"][0]
    same = np.repeat(np.eye(NS, dtype=f), HEADS, axis=0)
    by_tile = lambda v: v.reshape(v.shape[:-1] + (2, NPAIR, P))
    par = np.concatenate([a["conv_w"][0], a["conv_b"]], axis=0)
    par = by_tile(par).transpose(3, 2, 1, 0).reshape(P, 2 * NPAIR, 4)
    state = by_tile(a["state_ffn_conv"][0]).transpose(4, 3, 2, 0, 1).reshape(P, 2 * NPAIR, NS, 2)
    w_s = a["w_s"][0]

    ins = {
        "x_t": x.T.reshape(KT, P, T).transpose(1, 0, 2),
        "w_main": w_main, "w_half": w_half, "w_ffn": w_ffn,
        "cols": cols, "rope": rope, "eye": np.eye(P, dtype=f),
        "lnv": np.broadcast_to(np.stack([a["ln_v_g"][0], a["ln_v_b"][0]])[None], (P, 2, GMW)),
        "ws_t": w_s.transpose(2, 0, 1),
        "bs_t": np.repeat(a["b_s"][0], 64, axis=0).reshape(4, P, P).transpose(1, 0, 2),
        "ws_first": np.where(np.eye(NS, dtype=bool)[:, None, :], w_s[:, 0, 0][None, :, None], f(0)),
        "mask": mask,
        "sink_rows": np.broadcast_to(np.stack([sinks, sinks])[None], (P, 2, HEADS)),
        "sink_cols": np.tile(np.stack([sinks, sinks], axis=1), (NS, 1)),
        "same_sample": same,
        "k_cache": a["cache_swa_k"][0].transpose(2, 3, 0, 1).reshape(P, NS, P),
        "v_cache": a["cache_swa_v"][0].transpose(1, 0, 2, 3).reshape(P, NS, P),
        "conv_par": par, "conv_state": state,
    }
    outs = {
        "y": (P, KT, T), "kv_prompt": (2, P, P), "gm_prompt": (P, GMW), "gm_sample": (NS, GMW),
        "k_sample": (P, NS, P), "v_sample": (P, NS, P), "v_new": (NS, P), "conv_new": (P, 2 * NPAIR, 2 + 2 * NS),
    }
    nc = bacc.Bacc("TRN2", target_bir_lowering=False, num_devices=1)
    arrays, aps = {}, {}
    for name, v in ins.items():
        arrays[f"in_{name}"] = np.ascontiguousarray(v)
        aps[name] = nc.dram_tensor(f"in_{name}", v.shape, F32, kind="ExternalInput").ap()
    for name, shape in outs.items():
        aps[name] = nc.dram_tensor(f"out_{name}", shape, F32, kind="ExternalOutput").ap()
    build(nc, **aps)
    r = run_bass_kernel_spmd(nc, [arrays], core_ids=[0]).results[0]
    o = {name: np.asarray(r[f"out_{name}"]).reshape(shape) for name, shape in outs.items()}

    yt = o["y"].transpose(2, 1, 0).reshape(T, D)
    heads = lambda v: v.T.reshape(1, 1, P, KVH, HD)
    k_s = o["k_sample"].transpose(1, 2, 0).reshape(1, NS, P, KVH, HD)
    v_s = np.concatenate([o["v_sample"][1:].transpose(1, 0, 2), o["v_new"][:, None, :]], axis=1)
    conv = o["conv_new"].reshape(P, NPAIR, 2, 2 + 2 * NS).transpose(3, 2, 1, 0).reshape(2 + 2 * NS, 2 * DFF)
    return (yt[None, :SEQ], yt[SEQ:, None], heads(o["kv_prompt"][0]), heads(o["kv_prompt"][1]),
            o["gm_prompt"].reshape(1, 1, P, 8, 64), conv[None, None, 0:2],
            k_s, v_s.reshape(1, NS, P, KVH, HD), o["gm_sample"].reshape(1, NS, 1, 8, 64),
            conv[2:].reshape(1, NS, 2, 2 * DFF))
```
